# Optimizing a Trainium2 kernel written in Bass

```python
import jax, jax.numpy as jnp
from jax import lax
import numpy as np

D_MODEL = 1024
BATCH = 1
SEQ = 1024
DEPTH = 1
DEC_BATCH = 1
DEC_SEQ = 256
PAST_LEN = 128

GRID_W = 64
BLOCK = 128
WINDOW = 128
ROPE_THETA = 10000.0
EPS = 1e-6
NEG_INF = -1e30

A_HEADS = 16
A_KV = 4
A_HD = 64
A_Q = A_HEADS * A_HD
A_KVW = A_KV * A_HD
B_HEADS = 8
B_KV = 2
B_HD = 128
B_Q = B_HEADS * B_HD
B_KVW = B_KV * B_HD
IN_COLS = A_Q + 2 * A_KVW + B_Q + 2 * B_KVW
IN_SPLITS = (A_Q, A_Q + A_KVW, A_Q + 2 * A_KVW, A_Q + 2 * A_KVW + B_Q, A_Q + 2 * A_KVW + B_Q + B_KVW)
N_BRANCH = 2
PK_HEADS = 8
N_KEYS = 128
N_EXPERTS = N_KEYS * N_KEYS
PK_DIM = 256
PK_HALF = PK_DIM // 2
PK_TOPK = 16
PEER_CHUNK = 128

kernel_name = 'hybrid_window_axial_peer_encoder'

def rmsnorm(x, g):
    xf = x.astype(jnp.float32)
    y = xf * lax.rsqrt(jnp.mean(xf * xf, axis=-1, keepdims=True) + EPS) * g.astype(jnp.float32)
    return y.astype(x.dtype)

def rope_cos_sin(pos, dim):
    inv = ROPE_THETA ** (-jnp.arange(0, dim, 2, dtype=jnp.float32) / dim)
    ang = pos.astype(jnp.float32)[:, None] * inv[None, :]
    ang = jnp.concatenate([ang, ang], axis=-1)
    return jnp.cos(ang), jnp.sin(ang)

def apply_rope(x, cos, sin):
    half = x.shape[-1] // 2
    rot = jnp.concatenate([-x[..., half:], x[..., :half]], axis=-1)
    return x * cos[None, :, None, :] + rot * sin[None, :, None, :]

def window_attention(q, k, v, sink):
    B, S = q.shape[0], q.shape[1]
    nb = S // BLOCK
    G = A_HEADS // A_KV
    qb = q.reshape(B, nb, BLOCK, A_KV, G, A_HD).transpose(1, 0, 2, 3, 4, 5)
    pad = ((0, 0), (BLOCK, BLOCK), (0, 0), (0, 0))
    kp = jnp.pad(k, pad)
    vp = jnp.pad(v, pad)
    scale = A_HD ** -0.5
    sink_b = sink.astype(jnp.float32).reshape(A_KV, G)[None, :, :, None, None]

    def one_block(args):
        i, qi = args
        start = i * BLOCK
        kb = lax.dynamic_slice_in_dim(kp, start, 3 * BLOCK, axis=1)
        vb = lax.dynamic_slice_in_dim(vp, start, 3 * BLOCK, axis=1)
        s = jnp.einsum('bqkgd,bjkd->bkgqj', qi, kb).astype(jnp.float32) * scale
        qpos = start + jnp.arange(BLOCK)
        kpos = start - BLOCK + jnp.arange(3 * BLOCK)
        mask = (jnp.abs(qpos[:, None] - kpos[None, :]) <= WINDOW) & (kpos[None, :] >= 0) & (kpos[None, :] < S)
        s = jnp.where(mask[None, None, None], s, NEG_INF)
        sk = jnp.broadcast_to(sink_b, s.shape[:-1] + (1,))
        p = jax.nn.softmax(jnp.concatenate([s, sk], axis=-1), axis=-1)[..., :-1]
        return jnp.einsum('bkgqj,bjkd->bqkgd', p.astype(vb.dtype), vb)

    o = lax.map(one_block, (jnp.arange(nb), qb))
    return o.transpose(1, 0, 2, 3, 4, 5).reshape(B, S, A_Q)

def dense_attention(q, k, v):
    B, S = q.shape[0], q.shape[1]
    nb = S // BLOCK
    G = B_HEADS // B_KV
    qb = q.reshape(B, nb, BLOCK, B_KV, G, B_HD).transpose(1, 0, 2, 3, 4, 5)
    scale = B_HD ** -0.5

    def one_block(qi):
        s = jnp.einsum('bqkgd,bjkd->bkgqj', qi, k).astype(jnp.float32) * scale
        p = jax.nn.softmax(s, axis=-1)
        return jnp.einsum('bkgqj,bjkd->bqkgd', p.astype(v.dtype), v)

    o = lax.map(one_block, qb)
    return o.transpose(1, 0, 2, 3, 4, 5).reshape(B, S, B_Q)

def parallel_mixer(h, w_in, w_gate, b_gate, sink, q_norm_g, k_norm_g, w_oa, w_ob, w_out):
    B, S, _ = h.shape
    proj = jnp.einsum('bsd,dc->bsc', h, w_in)
    qa, ka, va, qb, kb, vb = jnp.split(proj, IN_SPLITS, axis=-1)
    qa = qa.reshape(B, S, A_HEADS, A_HD)
    ka = ka.reshape(B, S, A_KV, A_HD)
    va = va.reshape(B, S, A_KV, A_HD)
    cos_a, sin_a = rope_cos_sin(jnp.arange(S), A_HD)
    oa = window_attention(apply_rope(qa, cos_a, sin_a), apply_rope(ka, cos_a, sin_a), va, sink)
    qb = rmsnorm(qb.reshape(B, S, B_HEADS, B_HD), q_norm_g)
    kb = rmsnorm(kb.reshape(B, S, B_KV, B_HD), k_norm_g)
    vb = vb.reshape(B, S, B_KV, B_HD)
    rows = S // GRID_W
    row = jnp.repeat(jnp.arange(rows), GRID_W)
    col = jnp.tile(jnp.arange(GRID_W), rows)
    half = B_HD // 2
    cr, sr = rope_cos_sin(row, half)
    cc, sc = rope_cos_sin(col, half)
    qb = jnp.concatenate([apply_rope(qb[..., :half], cr, sr), apply_rope(qb[..., half:], cc, sc)], axis=-1)
    kb = jnp.concatenate([apply_rope(kb[..., :half], cr, sr), apply_rope(kb[..., half:], cc, sc)], axis=-1)
    ob = dense_attention(qb, kb, vb)
    gates = jax.nn.sigmoid((jnp.einsum('bsd,dc->bsc', h, w_gate) + b_gate).astype(jnp.float32))
    ga, gb = jnp.split(gates, N_BRANCH, axis=-1)
    ya = jnp.einsum('bsc,cd->bsd', oa, w_oa).astype(jnp.float32)
    yb = jnp.einsum('bsc,cd->bsd', ob, w_ob).astype(jnp.float32)
    merged = (ga * ya + gb * yb).astype(h.dtype)
    return jnp.einsum('bsd,de->bse', merged, w_out)

def peer(h, w_query, sub_keys, expert_u, expert_v):
    B, S, D = h.shape
    T = B * S
    hc = h.reshape(T // PEER_CHUNK, PEER_CHUNK, D)

    def one_chunk(xc):
        qry = jnp.einsum('cd,dq->cq', xc, w_query).reshape(PEER_CHUNK, PK_HEADS, 2, PK_HALF)
        sc = jnp.einsum('chpd,hpnd->chpn', qry, sub_keys).astype(jnp.float32)
        s_top, i_top = lax.top_k(sc, PK_TOPK)
        cand = (s_top[:, :, 0, :, None] + s_top[:, :, 1, None, :]).reshape(PEER_CHUNK, PK_HEADS, PK_TOPK * PK_TOPK)
        cand_idx = (i_top[:, :, 0, :, None] * N_KEYS + i_top[:, :, 1, None, :]).reshape(PEER_CHUNK, PK_HEADS, PK_TOPK * PK_TOPK)
        best_s, pos = lax.top_k(cand, PK_TOPK)
        idx = jnp.take_along_axis(cand_idx, pos, axis=-1)
        g = jax.nn.softmax(best_s, axis=-1)
        u = expert_u[idx]
        v = expert_v[idx]
        act = jax.nn.gelu(jnp.einsum('chkd,cd->chk', u, xc).astype(jnp.float32), approximate=False)
        return jnp.einsum('chk,chkd->cd', (g * act).astype(v.dtype), v)

    out = lax.map(one_chunk, hc)
    return out.reshape(B, S, D)

def trunk(x, g_mix, w_in, w_gate, b_gate, sink, q_norm_g, k_norm_g, w_oa, w_ob, w_out,
          g_ffn, w_query, sub_keys, expert_u, expert_v, g_final):
    for l in range(DEPTH):
        h = rmsnorm(x, g_mix[l])
        x = x + parallel_mixer(h, w_in[l], w_gate[l], b_gate[l], sink[l], q_norm_g[l], k_norm_g[l],
                               w_oa[l], w_ob[l], w_out[l])
        h = rmsnorm(x, g_ffn[l])
        x = x + peer(h, w_query[l], sub_keys[l], expert_u[l], expert_v[l])
    return rmsnorm(x, g_final)

def setup_inputs(seed: int = 0) -> dict:
    key = jax.random.key(seed)
    ks = jax.random.split(key, 20)
    f32 = jnp.float32
    D = D_MODEL

    def nrm(k, shape, scale):
        return jax.random.normal(k, shape, f32) * scale

    return {
        'x_prompt': nrm(ks[0], (BATCH, SEQ, D), 1.0),
        'x_sample': nrm(ks[1], (DEC_BATCH, DEC_SEQ, D), 1.0),
        'g_mix': 1.0 + nrm(ks[2], (DEPTH, D), 0.02),
        'w_in': nrm(ks[3], (DEPTH, D, IN_COLS), D ** -0.5),
        'w_gate': nrm(ks[4], (DEPTH, D, N_BRANCH * D), D ** -0.5),
        'b_gate': nrm(ks[5], (DEPTH, N_BRANCH * D), 0.02),
        'sink': nrm(ks[6], (DEPTH, A_HEADS), 0.5),
        'q_norm_g': 1.0 + nrm(ks[7], (DEPTH, B_HD), 0.02),
        'k_norm_g': 1.0 + nrm(ks[8], (DEPTH, B_HD), 0.02),
        'w_oa': nrm(ks[9], (DEPTH, A_Q, D), A_Q ** -0.5),
        'w_ob': nrm(ks[10], (DEPTH, B_Q, D), B_Q ** -0.5),
        'w_out': nrm(ks[11], (DEPTH, D, D), D ** -0.5),
        'g_ffn': 1.0 + nrm(ks[12], (DEPTH, D), 0.02),
        'w_query': nrm(ks[13], (DEPTH, D, PK_HEADS * PK_DIM), D ** -0.5),
        'sub_keys': nrm(ks[14], (DEPTH, PK_HEADS, 2, N_KEYS, PK_HALF), PK_HALF ** -0.5),
        'expert_u': nrm(ks[15], (DEPTH, N_EXPERTS, D), D ** -0.5),
        'expert_v': nrm(ks[16], (DEPTH, N_EXPERTS, D), PK_HEADS ** -0.5),
        'g_final': 1.0 + nrm(ks[17], (D,), 0.02),
    }

def reference(x_prompt, x_sample, g_mix, w_in, w_gate, b_gate, sink, q_norm_g, k_norm_g, w_oa, w_ob, w_out,
              g_ffn, w_query, sub_keys, expert_u, expert_v, g_final):
    y_prompt = trunk(x_prompt, g_mix, w_in, w_gate, b_gate, sink, q_norm_g, k_norm_g, w_oa, w_ob, w_out,
                     g_ffn, w_query, sub_keys, expert_u, expert_v, g_final)
    y_sample = trunk(x_sample, g_mix, w_in, w_gate, b_gate, sink, q_norm_g, k_norm_g, w_oa, w_ob, w_out,
                     g_ffn, w_query, sub_keys, expert_u, expert_v, g_final)
    return (y_prompt, y_sample)


_drawn_inputs = setup_inputs


def setup_inputs(seed=0):
    import zlib

    import numpy as np

    out = dict(_drawn_inputs(seed))
    spreads = {}
    factors = {'g_mix': 4.646,
     'b_gate': 8.0,
     'sink': 8.0,
     'q_norm_g': 8.0,
     'k_norm_g': 8.0,
     'g_final': 8.251,
     'g_ffn': 8.0}
    for name, (base, spread) in spreads.items():
        noise = np.random.default_rng([zlib.crc32(name.encode()), seed]).standard_normal(out[name].shape)
        drawn = base * np.exp(spread * noise) if base else spread * noise
        out[name] = __import__('jax').numpy.asarray(drawn.astype(out[name].dtype))
    for name, factor in factors.items():
        out[name] = (out[name] * factor).astype(out[name].dtype)
    return out
```

```python
import concourse.bass as bass
from concourse import mybir
from contextlib import ExitStack

F32 = mybir.dt.float32
I32 = mybir.dt.int32
U32 = mybir.dt.uint32
ALU = mybir.AluOpType
ACT = mybir.ActivationFunctionType
AXX = mybir.AxisListType.X

P = 128
D = 1024
KD = D // P
SAMPLE, PROMPT = 256, 1024
TOK = SAMPLE + PROMPT
NT = TOK // P
ST = SAMPLE // P
PT_ = PROMPT // P
AH, AKV, AD = 16, 4, 64
BH, BKV, BD = 8, 2, 128
A_SCALE = AD ** -0.5
B_SCALE = BD ** -0.5
QA, KA, VA, QB, KB, VB, GATE = 0, 1024, 1280, 1536, 2560, 2816, 3072
COLS = GATE + 2 * D
CW = 512
EPS = 1e-6
NEG = -1e30
ROPE_W = 2 * AD + 2 * BD
HEADS, KEYS, TOPK = 8, 128, 16
SLOTS = HEADS * TOPK


class Chain:

    def __init__(self, eng, sem):
        self.eng, self.sem = eng, sem
        self.base, self.i, self.per, self.n = 0, 0, 0, 0

    def __call__(self, ins):
        ins.then_inc(self.sem, 1)
        self.n += 1
        self.eng.wait_ge(self.sem, self.i * self.per + (self.base + self.n))

    def enter(self, i, per):
        self.base, self.n = self.base + self.n, 0
        self.i, self.per = i, per

    def leave(self, trips):
        assert self.n == self.per, (self.n, self.per)
        self.base += trips * self.per
        self.i, self.per, self.n = 0, 0, 0


class At:

    def __init__(self, i, per, base=0):
        self.i, self.per, self.base = i, per, base

    def __call__(self, local):
        return self.i * self.per + (self.base + local)


class Mem:

    def __init__(self, nc, ctx, sems, tag):
        self.nc, self.ctx, self.sems, self.tag = nc, ctx, sems, tag

    def sb(self, name, shape, dt=F32):
        return self.ctx.enter_context(self.nc.sbuf_tensor(f"{self.tag}_{name}", shape, dt))

    def ps(self, name, shape, dt=F32):
        return self.ctx.enter_context(self.nc.psum_tensor(f"{self.tag}_{name}", shape, dt))

    def sem(self, name):
        return self.sems.enter_context(self.nc.semaphore(f"{self.tag}_{name}"))


def phase_project(nc, sems, x, g_mix, w_all, ident_d, proj):
    with ExitStack() as ctx:
        m = Mem(nc, ctx, sems, "proj")
        ident = m.sb("ident", [P, P])
        grow = m.sb("grow", [P, D])
        xt = m.sb("xt", [P, 2, D])
        sq = m.sb("sq", [P, D])
        ht = m.sb("ht", [P, 2, D])
        ss = m.sb("ss", [P, 2])
        rs = m.sb("rs", [P, 2])
        hT = m.sb("hT", [P, KD, TOK])
        w = m.sb("w", [P, 2, KD, CW])
        stage = m.sb("stage", [P, 4, CW])
        tp = m.ps("tp", [P, 2, D])
        acc = m.ps("acc", [P, 4, CW])
        const_ld = m.sem("const_ld")
        x_ld = [m.sem(f"x_ld{b}") for b in range(2)]
        root_ready, h_ready = m.sem("root_ready"), m.sem("h_ready")
        h_transposed = m.sem("h_transposed")
        hT_copied = m.sem("hT_copied")
        w_ld = [m.sem(f"w_ld{b}") for b in range(2)]
        mm_tile = m.sem("mm_tile")
        staged = [m.sem("staged_act"), m.sem("staged_dve")]
        stored = [m.sem(f"stored{s}") for s in range(4)]
        act_chain, dve_chain, eps_set = m.sem("act_chain"), m.sem("dve_chain"), m.sem("eps_set")
        eps = m.sb("eps", [P, 1])
        rt = m.sb("rt", [P, 2])
        wv = w_all.rearrange("(k p) c -> p k c", p=P)
        CHUNKS = COLS // CW

        with nc.Block() as block:
            @block.sync
            def _(sp):
                sp.dma_start(ident[:], ident_d).then_inc(const_ld, 16)
                sp.dma_start(grow[:], g_mix.broadcast_to([P, D])).then_inc(const_ld, 16)
                for b in range(2):
                    sp.dma_start(xt[:, b, :], x[b * P:(b + 1) * P, :]).then_inc(x_ld[b], 16)
                for b in range(2):
                    sp.dma_start(w[:, b, :, :], wv[:, :, b * CW:(b + 1) * CW]).then_inc(w_ld[b], 16)
                with sp.Fori(0, NT // 2 - 1) as j:
                    for b in range(2):
                        sp.wait_ge(h_ready, j * 2 + (b + 1))
                        sp.dma_start(xt[:, b, :], x[bass.ds(j * 2 * P + (b + 2) * P, P), :]).then_inc(x_ld[b], 16)

                def chunk_pair(j, more):
                    for b in range(2):
                        for t in range(NT):
                            u = b * NT + t
                            sp.wait_ge(staged[u % 2], j * NT + (u // 2 + 1 + 2))
                            sp.dma_start(proj[t * P:(t + 1) * P, bass.ds(j * 2 * CW + b * CW, CW)],
                                         stage[:, u % 4, :]).then_inc(stored[u % 4], 16)
                        if more:
                            sp.wait_ge(mm_tile, j * 2 * NT + (b + 1) * NT)
                            sp.dma_start(w[:, b, :, :],
                                         wv[:, :, bass.ds(j * 2 * CW + (b + 2) * CW, CW)]).then_inc(w_ld[b], 16)

                with sp.Fori(0, CHUNKS // 2 - 1) as j:
                    chunk_pair(j, True)
                chunk_pair(CHUNKS // 2 - 1, False)
                for s in range(4):
                    sp.wait_ge(stored[s], 16 * (CHUNKS * NT // 4 + 1))

            @block.scalar
            def _(act):
                act.sem_inc(hT_copied, 2)
                act.sem_inc(staged[0], 2)
                link = Chain(act, act_chain)
                act.wait_ge(eps_set, 1)
                with act.Fori(0, NT // 2) as j:
                    link.enter(j, 2)
                    for b in range(2):
                        act.wait_ge(x_ld[b], j * 16 + 16)
                        link(nc.scalar.activation(sq[:], xt[:, b, :], ACT.Square, accum_out=ss[:, b:b + 1]))
                        nc.scalar.activation(rt[:, b:b + 1], ss[:, b:b + 1], ACT.Sqrt, bias=eps[:],
                                             scale=1.0 / D).then_inc(root_ready, 1)
                        act.wait_ge(h_transposed, j * 2 + (b + 1 + 2))
                        nc.scalar.copy(hT[:, :, bass.ds(j * 2 * P + b * P, P)],
                                       tp[:, b, :].rearrange("p (k c) -> p k c", c=P)).then_inc(hT_copied, 1)
                    link.leave(NT // 2)
                with act.Fori(0, CHUNKS // 2) as j:
                    for u in range(0, 2 * NT, 2):
                        act.wait_ge(mm_tile, j * 2 * NT + (u + 1))
                        act.wait_ge(stored[u % 4], j * (16 * NT // 2) + 16 * (u // 4 + 1))
                        nc.scalar.copy(stage[:, u % 4, :], acc[:, u % 4, :]).then_inc(staged[0], 1)

            @block.vector
            def _(dve):
                dve.sem_inc(staged[1], 2)
                for s in range(4):
                    dve.sem_inc(stored[s], 16)
                nc.vector.memset(eps[:], EPS).then_inc(eps_set, 1)
                dve.wait_ge(const_ld, 32)
                link = Chain(dve, dve_chain)
                with dve.Fori(0, NT // 2) as j:
                    link.enter(j, 2)
                    for b in range(2):
                        dve.wait_ge(root_ready, j * 2 + (b + 1))
                        link(nc.vector.reciprocal(rs[:, b:b + 1], rt[:, b:b + 1]))
                        dve.wait_ge(h_transposed, j * 2 + (b + 1))
                        nc.vector.scalar_tensor_tensor(ht[:, b, :], xt[:, b, :], rs[:, b:b + 1], grow[:],
                                                       ALU.mult, ALU.mult).then_inc(h_ready, 1)
                    link.leave(NT // 2)
                with dve.Fori(0, CHUNKS // 2) as j:
                    for u in range(1, 2 * NT, 2):
                        dve.wait_ge(mm_tile, j * 2 * NT + (u + 1))
                        dve.wait_ge(stored[u % 4], j * (16 * NT // 2) + 16 * (u // 4 + 1))
                        nc.vector.tensor_copy(stage[:, u % 4, :], acc[:, u % 4, :]).then_inc(staged[1], 1)

            @block.tensor
            def _(pe):
                pe.sem_inc(h_transposed, 2)
                pe.wait_ge(const_ld, 32)
                with pe.Fori(0, NT // 2) as j:
                    for b in range(2):
                        pe.wait_ge(h_ready, j * 2 + (b + 1))
                        pe.wait_ge(hT_copied, j * 2 + (b + 1))
                        for k in range(KD):
                            last = nc.tensor.transpose(tp[:, b, k * P:(k + 1) * P], ht[:, b, k * P:(k + 1) * P],
                                                       ident[:])
                        last.then_inc(h_transposed, 1)
                pe.wait_ge(hT_copied, NT + 2)
                with pe.Fori(0, CHUNKS // 2) as j:
                    for b in range(2):
                        pe.wait_ge(w_ld[b], j * 16 + 16)
                        for t in range(NT):
                            u = b * NT + t
                            pe.wait_ge(staged[u % 2], j * NT + (u // 2 + 1))
                            for k in range(KD):
                                last = nc.tensor.matmul(acc[:, u % 4, :], hT[:, k, t * P:(t + 1) * P], w[:, b, k, :],
                                                        start=(k == 0), stop=(k == KD - 1))
                            last.then_inc(mm_tile, 1)


def rope_steps(e, link, out, x, tmp, cos, sin, heads, sections):
    width = 64 * sections
    full = lambda ap: ap.rearrange("p (h c) -> p h c", c=width)
    e.tensor_tensor(full(out), full(x), cos.unsqueeze(1).to_broadcast([P, heads, width]), ALU.mult)
    for half in range(2):
        if sections == 1:
            cut = lambda ap, t: ap.rearrange("p (h t c) -> p h t c", t=2, c=32)[:, :, t, :]
            s = sin[:, half * 32:half * 32 + 32].unsqueeze(1).to_broadcast([P, heads, 32])
        else:
            cut = lambda ap, t: ap.rearrange("p (h s t c) -> p h s t c", s=sections, t=2, c=32)[:, :, :, t, :]
            s = sin.rearrange("p (s t c) -> p s t c", t=2, c=32)[:, :, half, :].unsqueeze(1).to_broadcast(
                [P, heads, sections, 32])
        last = e.tensor_tensor(cut(tmp, half), cut(x, 1 - half), s, ALU.mult)
    link(last)
    return e.tensor_tensor(out, out, tmp, ALU.add)


def phase_attend(nc, sems, proj, rope, masks, sink, q_norm_g, k_norm_g, ident_d, mixed):
    with ExitStack() as ctx:
        m = Mem(nc, ctx, sems, "att")
        BQK = 1280
        NB = BQK // BD
        ident = m.sb("ident", [P, P])
        sinks = m.sb("sinks", [P, AH])
        qg, kg = m.sb("qg", [P, BD]), m.sb("kg", [P, BD])
        eps = m.sb("eps", [P, 1])
        kTA = m.sb("kTA", [P, AKV * 2, (NT + 2) * P])
        kTB = m.sb("kTB", [P, BKV, TOK])
        vA = m.sb("vA", [P, NT + 2, AKV * AD])
        vB = m.sb("vB", [P, NT, BKV * BD])
        rB = m.sb("rB", [P, NT, NB])
        const_ld, v_ld = m.sem("const_ld"), m.sem("v_ld")
        eps_set, pads_set = m.sem("eps_set"), m.sem("pads_set")
        with ExitStack() as kctx:
            mk = Mem(nc, kctx, sems, "key")
            raw = mk.sb("raw", [P, 2, BQK + 256])
            tab = mk.sb("tab", [P, 2, ROPE_W])
            sq = mk.sb("sq", [P, 2, BQK])
            ss, rt = mk.sb("ss", [P, 2, NB]), mk.sb("rt", [P, 2, NB])
            kn = mk.sb("kn", [P, 256])
            kr = mk.sb("kr", [P, 2, AKV * 2 * P + 256])
            ka = mk.sb("ka", [P, 256])
            KRA = AKV * 2 * P
            tmp = mk.sb("tmp", [P, 256])
            tpA, tpB = mk.ps("tpA", [P, 2, AKV * 2 * P]), mk.ps("tpB", [P, 2, 512])
            ld = [mk.sem(f"ld{b}") for b in range(2)]
            sq_ready, ss_ready, rt_ready, kr_ready = (mk.sem(n) for n in ("sq_ready", "ss_ready", "rt_ready", "kr_ready"))
            k_transposed = mk.sem("k_transposed")
            k_copied = mk.sem("k_copied")
            chain = mk.sem("chain")
            with nc.Block() as block:
                @block.sync
                def _(sp):
                    for dst, src in ((ident[:], ident_d), (sinks[:], sink.broadcast_to([P, AH])),
                                     (qg[:], q_norm_g.broadcast_to([P, BD])), (kg[:], k_norm_g.broadcast_to([P, BD]))):
                        sp.dma_start(dst, src).then_inc(const_ld, 16)

                    def load(b, row):
                        sp.dma_start(raw[:, b, 0:BQK], proj[bass.ds(row, P), QB:VB]).then_inc(ld[b], 16)
                        sp.dma_start(raw[:, b, BQK:], proj[bass.ds(row, P), KA:VA]).then_inc(ld[b], 16)
                        sp.dma_start(tab[:, b, :], rope[bass.ds(row, P), :]).then_inc(ld[b], 16)

                    load(0, 0)
                    load(1, P)
                    sp.dma_start(vA[:, 1:NT + 1, :], proj[:, VA:QB].rearrange("(t p) c -> p t c", p=P)).then_inc(v_ld, 16)
                    sp.dma_start(vB[:], proj[:, VB:GATE].rearrange("(t p) c -> p t c", p=P)).then_inc(v_ld, 16)
                    with sp.Fori(0, NT // 2 - 1) as j:
                        for b in range(2):
                            sp.wait_ge(kr_ready, j * 2 + (b + 1))
                            load(b, j * 2 * P + (b + 2) * P)
                    sp.wait_ge(v_ld, 32)

                @block.gpsimd
                def _(pool):
                    nc.gpsimd.memset(kTA[:, :, 0:P], 0.0)
                    nc.gpsimd.memset(kTA[:, :, (NT + 1) * P:], 0.0)
                    nc.gpsimd.memset(vA[:, 0, :], 0.0)
                    nc.gpsimd.memset(vA[:, NT + 1, :], 0.0).then_inc(pads_set, 1)
                    with pool.Fori(0, NT // 2) as j:
                        for b in range(2):
                            pool.wait_ge(ld[b], j * 48 + 48)
                            pool.wait_ge(ss_ready, j * 2 + (b + 1))
                            nc.gpsimd.tensor_tensor(sq[:, b, :], raw[:, b, 0:BQK], raw[:, b, 0:BQK],
                                                    ALU.mult).then_inc(sq_ready, 1)

                @block.scalar
                def _(act):
                    act.sem_inc(k_copied, 4)
                    act.wait_ge(eps_set, 1)
                    with act.Fori(0, NT // 2) as j:
                        for b in range(2):
                            act.wait_ge(ss_ready, j * 2 + (b + 1 + 2))
                            nc.scalar.activation(rt[:, b, :], ss[:, b, :], ACT.Sqrt, bias=eps[:],
                                                 scale=1.0 / BD).then_inc(rt_ready, 1)
                            act.wait_ge(k_transposed, j * 2 + (b + 1 + 2))
                            nc.scalar.copy(kTA[:, :, bass.ds(j * 2 * P + (b + 1) * P, P)],
                                           tpA[:, b, :].rearrange("p (h c) -> p h c", c=P)).then_inc(k_copied, 1)
                            nc.scalar.copy(kTB[:, :, bass.ds(j * 2 * P + b * P, P)],
                                           tpB[:, b, 0:256].rearrange("p (h c) -> p h c", c=P)).then_inc(k_copied, 1)

                @block.vector
                def _(dve):
                    link = Chain(dve, chain)
                    dve.sem_inc(ss_ready, 2)
                    nc.vector.memset(eps[:], EPS).then_inc(eps_set, 1)
                    link(nc.vector.memset(kr[:], 0.0))
                    dve.wait_ge(const_ld, 64)
                    with dve.Fori(0, NT // 2) as j:
                        link.enter(j, 10)
                        for b in range(2):
                            dve.wait_ge(sq_ready, j * 2 + (b + 1))
                            nc.vector.reduce_sum(ss[:, b, :], sq[:, b, :].rearrange("p (h c) -> p h c", c=BD),
                                                 AXX).then_inc(ss_ready, 1)
                            dve.wait_ge(k_transposed, j * 2 + (b + 1))
                            link(rope_steps(nc.vector, link, ka[:], raw[:, b, BQK:], tmp[:],
                                            tab[:, b, 0:AD], tab[:, b, AD:2 * AD], AKV, 1))
                            for v in range(2):
                                nc.vector.tensor_copy(
                                    kr[:, b, 0:KRA].rearrange("p (h v c) -> p h v c", v=2, c=P)[:, :, v, v * AD:(v + 1) * AD],
                                    ka[:].rearrange("p (h c) -> p h c", c=AD))
                            dve.wait_ge(rt_ready, j * 2 + (b + 1))
                            link(nc.vector.reciprocal(rB[:, bass.ds(j * 2 + b, 1), :], rt[:, b, :].unsqueeze(1)))
                            keys = raw[:, b, BH * BD:BQK].rearrange("p (h c) -> p h c", c=BD)
                            kn3 = kn[:].rearrange("p (h c) -> p h c", c=BD)
                            for h in range(BKV):
                                last = nc.vector.scalar_tensor_tensor(
                                    kn3[:, h, :], keys[:, h, :], rB[:, bass.ds(j * 2 + b, 1), BH + h], kg[:],
                                    ALU.mult, ALU.mult)
                            link(last)
                            rope_steps(nc.vector, link, kr[:, b, KRA:], kn[:], tmp[:],
                                       tab[:, b, 128:256], tab[:, b, 256:384], BKV, 2).then_inc(kr_ready, 1)
                            dve.wait_ge(kr_ready, j * 2 + (b + 1))
                        link.leave(NT // 2)

                @block.tensor
                def _(pe):
                    pe.sem_inc(k_transposed, 2)
                    pe.wait_ge(const_ld, 64)
                    with pe.Fori(0, NT // 2) as j:
                        for b in range(2):
                            pe.wait_ge(kr_ready, j * 2 + (b + 1))
                            pe.wait_ge(k_copied, j * 4 + (2 * b + 2))
                            for h in range(2 * AKV):
                                nc.tensor.transpose(tpA[:, b, h * P:(h + 1) * P], kr[:, b, h * P:(h + 1) * P], ident[:])
                            for h in range(BKV):
                                last = nc.tensor.transpose(tpB[:, b, h * P:(h + 1) * P],
                                                           kr[:, b, KRA + h * BD:KRA + (h + 1) * BD], ident[:])
                            last.then_inc(k_transposed, 1)

        NH = AH + BH
        SW = 3 * P + 1
        q = m.sb("q", [P, 2, 2 * D])
        tab = m.sb("tab", [P, 2, ROPE_W])
        mask = m.sb("mask", [P, 2, 3 * P])
        qn, qtmp = m.sb("qn", [P, D]), m.sb("qtmp", [P, D])
        qr = m.sb("qr", [P, 2, 2 * D])
        qT = m.sb("qT", [P, 16, P])
        Sm = m.sb("Sm", [P, 2, SW])
        mx, nm, rsum, rinv = (m.sb(n, [P, NH]) for n in ("mx", "nm", "rsum", "rinv"))
        prob = m.sb("prob", [P, 2, PROMPT])
        probT = m.sb("probT", [P, 2, PROMPT])
        O = m.sb("O", [P, 2 * D])
        OT = m.sb("OT", [P, 2 * D])
        S = m.ps("S", [P, 2, PROMPT])
        tb = m.ps("tb", [P, 2, 512])
        Op = m.ps("Op", [P, 2, 512])
        q_ld = [m.sem(f"q_ld{b}") for b in range(2)]
        mask_ld = [m.sem(f"mask_ld{b}") for b in range(2)]
        q_ready = m.sem("q_ready")
        t_full = m.sem("t_full")
        t_free = [m.sem("t_free_act"), m.sem("t_free_dve")]
        s_full = m.sem("s_full")
        nm_ready = m.sem("nm_ready")
        prob_ready = m.sem("prob_ready")
        o_full = m.sem("o_full")
        o_free = m.sem("o_free")
        ot_stored = m.sem("ot_stored")
        pool_chain, chain = m.sem("pool_chain"), m.sem("chain")
        LAST = {7: 0, 15: 1, 19: 2, 23: 3}
        FIRST = {0: 0, 8: 1, 16: 2, 20: 3}

        def uses(nk):
            return 4 + AH + BH * -(-nk // 4) + 4

        def q_moves():
            for u in range(4):
                yield u, tb[:, u % 2, :].rearrange("p (h c) -> p h c", c=P), qT[:, 4 * u:4 * u + 4, :]

        def p_moves(h, nk):
            if h < AH:
                u = 4 + h
                yield u, tb[:, u % 2, 0:3 * P], probT[:, h % 2, 0:3 * P]
                return
            banks = -(-nk // 4)
            for c in range(banks):
                u, n = 4 + AH + (h - AH) * banks + c, min(4, nk - 4 * c) * P
                yield u, tb[:, u % 2, 0:n], probT[:, h % 2, 512 * c:512 * c + n]

        def o_moves(nk):
            for c in range(4):
                u = uses(nk) - 4 + c
                yield u, tb[:, u % 2, :], OT[:, 512 * c:512 * c + 512]

        def pairs(e, body, split_last=False):
            body(ST, 0, 0, 0, 0)
            full = PT_ // 2
            base = (ST, ST * uses(ST))
            with e.Fori(0, full - split_last) as j:
                body(PT_, j, *base, 1)
            if split_last:
                body(PT_, full - 1, *base, 2)

        with nc.Block() as block:
            @block.sync
            def _(sp):
                def load(b, row):
                    sp.dma_start(q[:, b, 0:D], proj[bass.ds(row, P), QA:KA]).then_inc(q_ld[b], 16)
                    sp.dma_start(q[:, b, D:], proj[bass.ds(row, P), QB:KB]).then_inc(q_ld[b], 16)
                    sp.dma_start(tab[:, b, :], rope[bass.ds(row, P), :]).then_inc(q_ld[b], 16)
                    sp.dma_start(mask[:, b, :], masks[bass.ds(row, P), :]).then_inc(mask_ld[b], 16)

                load(0, 0)
                load(1, P)

                def pair(nk, j, tiles, fills, part):
                    for b in range(2):
                        n = At(j, 2, tiles + b)
                        half = At(j, uses(nk), (fills + b * uses(nk)) // 2)
                        for par in range(2):
                            sp.wait_ge(t_free[par], half(uses(nk) // 2 + 1))
                        sp.dma_start(mixed[bass.ds(n(0) * P, P), :], OT[:]).then_inc(ot_stored, 16)
                        if part < 2:
                            load(b, n(2) * P)

                pairs(sp, pair, True)
                sp.wait_ge(ot_stored, 16 * (NT + 1))

            @block.gpsimd
            def _(pool):
                link = Chain(pool, pool_chain)
                pool.sem_inc(ot_stored, 16)

                def pair(nk, j, tiles, fills, part):
                    link.enter(j, 10)
                    for b in range(2):
                        n = At(j, 2, tiles + b)
                        pool.wait_ge(q_ld[b], j * 48 + (48 + 24 * tiles))
                        if part:
                            pool.wait_ge(s_full, (n(-2)) * NH + 1)
                        three = lambda ap: ap.rearrange("p (h c) -> p h c", c=BD)
                        link(nc.gpsimd.tensor_tensor(three(qn[:]), three(q[:, b, D:]),
                                                     rB[:, bass.ds(n(0), 1), 0:BH].rearrange("p a h -> p (a h)").unsqueeze(2).to_broadcast([P, BH, BD]), ALU.mult))
                        link(nc.gpsimd.tensor_tensor(three(qn[:]), three(qn[:]),
                                                     qg[:].unsqueeze(1).to_broadcast([P, BH, BD]), ALU.mult))
                        link(rope_steps(nc.gpsimd, link, qr[:, b, D:], qn[:], qtmp[:],
                                        tab[:, b, 128:256], tab[:, b, 256:384], BH, 2))
                        rope_steps(nc.gpsimd, link, qr[:, b, 0:D], q[:, b, 0:D], qtmp[:],
                                   tab[:, b, 0:AD], tab[:, b, AD:2 * AD], AH, 1).then_inc(q_ready, 1)
                        pool.wait_ge(q_ready, n(1))
                    link.leave(1 if not part else PT_ // 2)

                pairs(pool, pair)

            @block.scalar
            def _(act):
                act.sem_inc(prob_ready, 2)
                act.sem_inc(t_free[0], 1)

                def pair(nk, j, tiles, fills, part):
                    for b in range(2):
                        n = At(j, 2, tiles + b)
                        head = At(j, 2 * NH, (tiles + b) * NH)
                        fill = At(j, 2 * uses(nk), fills + b * uses(nk))

                        def move(moves):
                            for u, src, dst in moves:
                                if u % 2 == 0:
                                    act.wait_ge(t_full, fill(u + 1))
                                    nc.scalar.copy(dst, src).then_inc(t_free[0], 1)

                        move(q_moves())
                        for k in range(NH + 1):
                            if k < NH:
                                act.wait_ge(nm_ready, head(k + 1))
                                if k < AH:
                                    nc.scalar.activation(prob[:, k % 2, 0:SW], Sm[:, k % 2, :], ACT.Exp, bias=nm[:, k:k + 1],
                                                         accum_out=rsum[:, k:k + 1]).then_inc(prob_ready, 1)
                                else:
                                    nc.scalar.activation(prob[:, k % 2, 0:nk * P], S[:, k % 2, 0:nk * P], ACT.Exp,
                                                         bias=nm[:, k:k + 1], scale=B_SCALE,
                                                         accum_out=rsum[:, k:k + 1]).then_inc(prob_ready, 1)
                            if k >= 1:
                                move(p_moves(k - 1, nk))
                        act.wait_ge(ot_stored, n(1) * 16)
                        move(o_moves(nk))

                pairs(act, pair)

            @block.vector
            def _(dve):
                link = Chain(dve, chain)
                dve.sem_inc(o_free, 2)
                dve.sem_inc(t_free[1], 1)

                def pair(nk, j, tiles, fills, part):
                    link.enter(j, 2 * (NH + 4))
                    for b in range(2):
                        n = At(j, 2, tiles + b)
                        head = At(j, 2 * NH, (tiles + b) * NH)
                        bank = At(j, 8, (tiles + b) * 4)
                        fill = At(j, 2 * uses(nk), fills + b * uses(nk))

                        def move(moves):
                            for u, src, dst in moves:
                                if u % 2 == 1:
                                    dve.wait_ge(t_full, fill(u + 1))
                                    nc.vector.tensor_copy(dst, src).then_inc(t_free[1], 1)

                        move(q_moves())
                        dve.wait_ge(mask_ld[b], j * 16 + (16 + 8 * tiles))
                        for k in range(NH + 2):
                            if k < AH:
                                dve.wait_ge(s_full, head(k + 1))
                                dve.wait_ge(prob_ready, head(k + 1))
                                nc.vector.tensor_copy(Sm[:, k % 2, SW - 1:SW], sinks[:, k:k + 1])
                                link(nc.vector.tensor_tensor_reduce(
                                    out=Sm[:, k % 2, 0:SW - 1], in0=S[:, k % 2, 0:SW - 1], in1=mask[:, b, :], scale=A_SCALE,
                                    scalar=NEG, op0=ALU.add, op1=ALU.max, accum_out=mx[:, k:k + 1]))
                                nc.vector.tensor_scalar(nm[:, k:k + 1], mx[:, k:k + 1], sinks[:, k:k + 1], -1.0,
                                                        ALU.max, ALU.mult).then_inc(nm_ready, 1)
                            elif k < NH:
                                dve.wait_ge(s_full, head(k + 1))
                                link(nc.vector.reduce_max(mx[:, k:k + 1], S[:, k % 2, 0:nk * P], AXX))
                                nc.vector.tensor_scalar(nm[:, k:k + 1], mx[:, k:k + 1], -B_SCALE, None,
                                                        ALU.mult).then_inc(nm_ready, 1)
                            if 1 <= k <= NH:
                                move(p_moves(k - 1, nk))
                            if k - 2 in LAST:
                                w = LAST[k - 2]
                                hs = slice(8 * w, 8 * w + 8) if w < 2 else slice(4 * w + 8, 4 * w + 12)
                                nh = hs.stop - hs.start
                                dve.wait_ge(o_full, bank(w + 1))
                                link(nc.vector.reciprocal(rinv[:, hs], rsum[:, hs]))
                                nc.vector.tensor_tensor(
                                    O[:, 512 * w:512 * w + 512].rearrange("p (h c) -> p h c", h=nh),
                                    Op[:, w % 2, :].rearrange("p (h c) -> p h c", h=nh),
                                    rinv[:, hs].unsqueeze(2).to_broadcast([P, nh, 512 // nh]), ALU.mult).then_inc(o_free, 1)
                        dve.wait_ge(ot_stored, n(1) * 16)
                        move(o_moves(nk))
                    link.leave(1 if not part else PT_ // 2)

                pairs(dve, pair)

            @block.tensor
            def _(pe):
                def pair(nk, j, tiles, fills, part):
                    for b in range(2):
                        n = At(j, 2, tiles + b)
                        head = At(j, 2 * NH, (tiles + b) * NH)
                        bank = At(j, 8, (tiles + b) * 4)
                        half = At(j, uses(nk), (fills + b * uses(nk)) // 2)

                        def free(u):
                            pe.wait_ge(t_free[u % 2], half(u // 2 + 1))

                        def moved(u):
                            pe.wait_ge(t_free[u % 2], half(u // 2 + 2))

                        pe.wait_ge(q_ready, n(1))
                        for u, src, dst in q_moves():
                            free(u)
                            for c in range(4):
                                at = (4 * u + c) * P
                                last = nc.tensor.transpose(tb[:, u % 2, c * P:(c + 1) * P], qr[:, b, at:at + P], ident[:])
                            last.then_inc(t_full, 1)
                        for k in range(NH + 2):
                            if k < NH:
                                if k < AH and k % 8 == 0:
                                    moved(k // 8)
                                if k >= AH and k % 4 == 0:
                                    moved(2 + (k - AH) // 4)
                                pe.wait_ge(prob_ready, head(k + 1))
                                if k < AH:
                                    last = nc.tensor.matmul(S[:, k % 2, 0:3 * P], qT[:, k // 2, :],
                                                            kTA[:, k // 4 * 2 + k % 2, bass.ds(n(0) * P, 3 * P)], start=True, stop=True)
                                else:
                                    key0 = 0 if nk == ST else SAMPLE
                                    for c in range(0, nk * P, 512):
                                        w = min(512, nk * P - c)
                                        last = nc.tensor.matmul(S[:, k % 2, c:c + w], qT[:, 8 + k - AH, :],
                                                                kTB[:, (k - AH) // 4, key0 + c:key0 + c + w],
                                                                start=True, stop=True)
                                last.then_inc(s_full, 1)
                            if 1 <= k <= NH:
                                pe.wait_ge(prob_ready, head(k + 2))
                                for c, (u, src, dst) in enumerate(p_moves(k - 1, nk)):
                                    free(u)
                                    w = src.shape[-1] // P
                                    for t in range(w):
                                        last = nc.tensor.transpose(tb[:, u % 2, t * P:(t + 1) * P],
                                                                   prob[:, (k - 1) % 2, c * 512 + t * P:c * 512 + (t + 1) * P],
                                                                   ident[:])
                                    last.then_inc(t_full, 1)
                            if k >= 2:
                                h = k - 2
                                for u, src, dst in p_moves(h, nk):
                                    moved(u)
                                if h in FIRST:
                                    pe.wait_ge(o_free, bank(FIRST[h] + 1))
                                w = h // 8 if h < AH else 2 + (h - AH) // 4
                                if h < AH:
                                    dst = Op[:, w % 2, (h % 8) * AD:(h % 8) * AD + AD]
                                    for t in range(3):
                                        kv = h // 4
                                        last = nc.tensor.matmul(dst, probT[:, h % 2, t * P:(t + 1) * P],
                                                                vA[:, bass.ds(n(t), 1), kv * AD:(kv + 1) * AD].rearrange("p a c -> p (a c)"),
                                                                start=(t == 0), stop=(t == 2))
                                else:
                                    dst = Op[:, w % 2, (h % 4) * BD:(h % 4) * BD + BD]
                                    for t in range(nk):
                                        kv = (h - AH) // 4
                                        last = nc.tensor.matmul(dst, probT[:, h % 2, t * P:(t + 1) * P],
                                                                vB[:, (0 if nk == ST else ST) + t, kv * BD:(kv + 1) * BD],
                                                                start=(t == 0), stop=(t == nk - 1))
                                if h in LAST:
                                    last.then_inc(o_full, 1)
                        for c, (u, src, dst) in enumerate(o_moves(nk)):
                            pe.wait_ge(o_free, bank(c + 1 + 2))
                            free(u)
                            for t in range(4):
                                last = nc.tensor.transpose(tb[:, u % 2, t * P:(t + 1) * P],
                                                           O[:, 512 * c + t * P:512 * c + (t + 1) * P], ident[:])
                            last.then_inc(t_full, 1)

                pairs(pe, pair)


def phase_merge(nc, sems, x, mixed, proj, b_gate, w_oa, w_ob, w_out, ident_d, x2):
    with ExitStack() as ctx:
        m = Mem(nc, ctx, sems, "mrg")
        ident = m.sb("ident", [P, P])
        wa, wb, wo = (m.sb(n, [P, KD, D]) for n in ("wa", "wb", "wo"))
        bg = m.sb("bg", [P, 2 * D])
        mixT = m.sb("mixT", [P, 2, 2 * D])
        gate = m.sb("gate", [P, 2, 2 * D])
        xt = m.sb("xt", [P, 2, D])
        part = m.sb("part", [P, 2, D])
        merged = m.sb("merged", [P, D])
        mT = m.sb("mT", [P, D])
        res = m.sb("res", [P, D])
        Y = m.ps("Y", [P, 2, D])
        tb = m.ps("tb", [P, D])
        Z = m.ps("Z", [P, D])
        w_ld = [m.sem(f"w_ld{i}") for i in range(4)]
        ld = [m.sem(f"ld{b}") for b in range(2)]
        biased, gated = m.sem("biased"), m.sem("gated")
        y_full = m.sem("y_full")
        y_free = m.sem("y_free")
        merged_ready = m.sem("merged_ready")
        m_transposed = m.sem("m_transposed")
        mT_ready = m.sem("mT_ready")
        z_full = m.sem("z_full")
        res_ready = m.sem("res_ready")
        res_stored = m.sem("res_stored")
        chain = m.sem("chain")

        def order(e, first, second, link=None):
            first(At(0, 2, 0), 0)
            with e.Fori(0, NT // 2 - 1) as j:
                if link:
                    link.enter(j, 2)
                for b in range(2):
                    first(At(j, 2, b + 1), (b + 1) % 2)
                    second(At(j, 2, b), b)
                if link:
                    link.leave(NT // 2 - 1)
            first(At(0, 2, NT - 1), 1)
            second(At(0, 2, NT - 2), 0)
            second(At(0, 2, NT - 1), 1)

        with nc.Block() as block:
            @block.sync
            def _(sp):
                def load(b, row):
                    sp.dma_start(mixT[:, b, :], mixed[bass.ds(row, P), :]).then_inc(ld[b], 16)
                    sp.dma_start(gate[:, b, :], proj[bass.ds(row, P), GATE:]).then_inc(ld[b], 16)
                    sp.dma_start(xt[:, b, :], x[bass.ds(row, P), :]).then_inc(ld[b], 16)

                load(0, 0)
                for i, (dst, src) in enumerate(((wa, w_oa), (wb, w_ob), (wo, w_out))):
                    sp.dma_start(dst[:], src.rearrange("(k p) c -> p k c", p=P)).then_inc(w_ld[i], 16)
                    if i == 0:
                        sp.dma_start(bg[:], b_gate.broadcast_to([P, 2 * D])).then_inc(w_ld[3], 16)
                        sp.dma_start(ident[:], ident_d).then_inc(w_ld[3], 16)
                load(1, P)

                def tile(n, b, more):
                    sp.wait_ge(res_ready, n(1 + 1))
                    sp.dma_start(x2[bass.ds(n(0) * P, P), :], res[:]).then_inc(res_stored, 16)
                    if more:
                        load(b, n(2) * P)

                with sp.Fori(0, NT // 2 - 1) as j:
                    for b in range(2):
                        tile(At(j, 2, b), b, True)
                for b in range(2):
                    tile(At(0, 2, NT - 2 + b), b, False)
                sp.wait_ge(res_stored, 16 * (NT + 1))

            @block.gpsimd
            def _(pool):
                pool.sem_inc(res_stored, 16)
                pool.wait_ge(w_ld[3], 32)
                with pool.Fori(0, NT // 2) as j:
                    for b in range(2):
                        pool.wait_ge(ld[b], j * 48 + 48)
                        nc.gpsimd.tensor_tensor(gate[:, b, :], gate[:, b, :], bg[:], ALU.add).then_inc(biased, 1)

            @block.scalar
            def _(act):
                act.sem_inc(mT_ready, 1)

                def sigmoid(n, b):
                    act.wait_ge(biased, n(1))
                    nc.scalar.activation(gate[:, b, :], gate[:, b, :], ACT.Sigmoid).then_inc(gated, 1)

                def spread(n, b):
                    act.wait_ge(m_transposed, n(1 + 1))
                    nc.scalar.copy(mT[:], tb[:]).then_inc(mT_ready, 1)

                order(act, sigmoid, spread)

            @block.vector
            def _(dve):
                link = Chain(dve, chain)
                dve.sem_inc(y_free, 1)
                dve.sem_inc(res_ready, 1)

                def gates(n, b):
                    dve.wait_ge(gated, n(1))
                    for h in range(2):
                        cols = slice(h * 512, h * 512 + 512)
                        for br in range(2):
                            dve.wait_ge(y_full, n.i * 8 + (n.base * 4 + 2 * h + br + 1))
                            last = nc.vector.tensor_tensor(part[:, br, cols], Y[:, br, cols],
                                                           gate[:, b, br * D + h * 512:br * D + h * 512 + 512], ALU.mult)
                        if h == 1:
                            last.then_inc(y_free, 1)
                            dve.wait_ge(y_free, n(1 + 1))
                        else:
                            link(last)
                            dve.wait_ge(m_transposed, n(1))
                        last = nc.vector.tensor_tensor(merged[:, cols], part[:, 0, cols], part[:, 1, cols], ALU.add)
                    last.then_inc(merged_ready, 1)
                    dve.wait_ge(merged_ready, n(1))

                def residual(n, b):
                    dve.wait_ge(res_stored, n(1) * 16)
                    dve.wait_ge(z_full, n(1))
                    nc.vector.tensor_tensor(res[:], Z[:], xt[:, b, :], ALU.add).then_inc(res_ready, 1)

                order(dve, gates, residual, link)

            @block.tensor
            def _(pe):
                pe.sem_inc(m_transposed, 1)
                pe.wait_ge(w_ld[3], 32)
                for i in range(3):
                    pe.wait_ge(w_ld[i], 16)

                def branches(n, b):
                    pe.wait_ge(ld[b], n.i * 48 + 48 * (n.base // 2 + 1))
                    pe.wait_ge(y_free, n(1))
                    for h in range(2):
                        for br, w in enumerate((wa, wb)):
                            for k in range(KD):
                                last = nc.tensor.matmul(Y[:, br, h * 512:h * 512 + 512],
                                                        mixT[:, b, (br * KD + k) * P:(br * KD + k + 1) * P],
                                                        w[:, k, h * 512:h * 512 + 512], start=(k == 0), stop=(k == KD - 1))
                            last.then_inc(y_full, 1)

                def project(n, b):
                    pe.wait_ge(merged_ready, n(1))
                    pe.wait_ge(mT_ready, n(1))
                    for k in range(KD):
                        last = nc.tensor.transpose(tb[:, k * P:(k + 1) * P], merged[:, k * P:(k + 1) * P], ident[:])
                    last.then_inc(m_transposed, 1)
                    pe.wait_ge(mT_ready, n(2))
                    pe.wait_ge(res_ready, n(1))
                    for h in range(2):
                        for k in range(KD):
                            last = nc.tensor.matmul(Z[:, h * 512:h * 512 + 512], mT[:, k * P:(k + 1) * P],
                                                    wo[:, k, h * 512:h * 512 + 512], start=(k == 0), stop=(k == KD - 1))
                    last.then_inc(z_full, 1)

                order(pe, branches, project)


def phase_experts(nc, sems, x2, g_ffn, w_query, sub_keys, experts, g_final, ident_d, iota_d, out):
    with ExitStack() as ctx:
        m = Mem(nc, ctx, sems, "exp")
        RING = 8
        PAIR = 2
        STEPS = SLOTS // PAIR
        BACK = RING // PAIR
        ident = m.sb("ident", [P, P])
        iota = m.sb("iota", [P, TOPK])
        gffn, gfin = m.sb("gffn", [P, D]), m.sb("gfin", [P, D])
        wq = m.sb("wq", [P, KD, HEADS * 2 * P])
        keys = m.sb("keys", [P, 2 * HEADS, KEYS])
        eps = m.sb("eps", [P, 1])
        ring = m.sb("ring", [P, RING, 2 * D])
        xn, xr = m.sb("xn", [P, D]), m.sb("xr", [P, D])
        h_next, h_now = m.sb("h_next", [P, D]), m.sb("h_now", [P, D])
        hT = m.sb("hT", [P, D])
        junk = m.sb("junk", [P, 2, D])
        sqj = m.sb("sqj", [P, D])
        stat = m.sb("stat", [P, 6])
        qT = m.sb("qT", [P, 2 * P])
        top = m.sb("top", [P, HEADS, 2, TOPK])
        topi = m.sb("topi", [P, HEADS, 2, TOPK], U32)
        topf = m.sb("topf", [P, HEADS, 2, TOPK])
        rest = m.sb("rest", [P, 2, KEYS])
        cand, crest = m.sb("cand", [P, TOPK * TOPK]), m.sb("crest", [P, TOPK * TOPK])
        best = m.sb("best", [P, HEADS, TOPK])
        pos = m.sb("pos", [P, TOPK], U32)
        posd = m.sb("posd", [P, 2, TOPK], U32)
        posf = m.sb("posf", [P, 2, TOPK])
        hit = m.sb("hit", [P, 2, TOPK, TOPK])
        sel = m.sb("sel", [P, 2, TOPK])
        idx_all = m.sb("idx_all", [P, NT, SLOTS], I32)
        idx = m.sb("idx", [P, 2, SLOTS], I32)
        soft, ssum = m.sb("soft", [P, HEADS, TOPK]), m.sb("ssum", [P, HEADS])
        g_next, g_now = m.sb("g_next", [P, SLOTS]), m.sb("g_now", [P, SLOTS])
        dot, ge, wgt = (m.sb(n, [P, SLOTS]) for n in ("dot", "ge", "wgt"))
        diag = m.sb("diag", [P, 2, PAIR, P])
        y, yo = m.sb("y", [P, D]), m.sb("yo", [P, D])
        tb = m.ps("tb", [P, D])
        qp, sp_ = m.ps("qp", [P, 512]), m.ps("sc", [P, 512])
        acc = m.ps("acc", [P, D])
        const_ld, w_ld, eps_set = m.sem("const_ld"), m.sem("w_ld"), m.sem("eps_set")
        xn_ld, xr_ld = m.sem("xn_ld"), m.sem("xr_ld")
        root, h_ready, h_transposed, hT_ready = (m.sem(n) for n in ("root", "h_ready", "h_transposed", "hT_ready"))
        q_full, q_ready, s_full = m.sem("q_full"), m.sem("q_ready"), m.sem("s_full")
        s_free = m.sem("s_free")
        best_ready, exp_ready, chosen = m.sem("best_ready"), m.sem("exp_ready"), m.sem("chosen")
        row_ld = [m.sem(f"row_ld{r}") for r in range(RING)]
        dotted, gelued, weighted, diag_ready = (m.sem(n) for n in ("dotted", "gelued", "weighted", "diag_ready"))
        used = m.sem("used")
        y_ready = m.sem("y_ready")
        root2, yo_ready = m.sem("root2"), m.sem("yo_ready")
        out_stored = m.sem("out_stored")
        idx_ready = m.sem("idx_ready")
        pool_passed, dve_passed = m.sem("pool_passed"), m.sem("dve_passed")
        act_chain, chain = m.sem("act_chain"), m.sem("chain")
        Q0, QS = 6, 6

        def head_at(step, lag):
            h, off = divmod(step - Q0 - lag, QS)
            return h if off == 0 and 0 <= h < HEADS else None

        def tiles(e, prologue, tile, link=None, per=0):
            prologue(At(0, 1, 0))
            with e.Fori(0, NT - 1) as i:
                if link:
                    link.enter(i, per)
                tile(At(i, 1, 0), True)
                if link:
                    link.leave(NT - 1)
            tile(At(0, 1, NT - 1), False)

        def mul(n, k, c):
            return n.i * k + (n.base * k + c)

        with nc.Block() as block:
            @block.sync
            def _(sp):
                sp.dma_start(xn[:], x2[0:P, :]).then_inc(xn_ld, 16)
                for dst, src in ((ident[:], ident_d), (iota[:], iota_d.broadcast_to([P, TOPK])),
                                 (gffn[:], g_ffn.broadcast_to([P, D])), (gfin[:], g_final.broadcast_to([P, D])),
                                 (keys[:], sub_keys)):
                    sp.dma_start(dst, src).then_inc(const_ld, 16)
                sp.dma_start(wq[:], w_query.rearrange("(k p) c -> p k c", p=P)).then_inc(w_ld, 16)

                def tile(n, more):
                    if more:
                        sp.wait_ge(h_ready, n(1))
                        sp.dma_start(xn[:], x2[bass.ds(n(1) * P, P), :]).then_inc(xn_ld, 16)
                    sp.wait_ge(y_ready, n(1))
                    sp.dma_start(xr[:], x2[bass.ds(n(0) * P, P), :]).then_inc(xr_ld, 16)
                    sp.wait_ge(yo_ready, n(1))
                    sp.dma_start(out[bass.ds(n(0) * P, P), :], yo[:]).then_inc(out_stored, 16)

                tiles(sp, lambda n: None, tile)
                sp.wait_ge(out_stored, 16 * (NT + 1))

            @block.gpsimd
            def _(pool):
                pool.sem_inc(out_stored, 16)
                with pool.Fori(0, NT // 2) as j:
                    for b in range(2):
                        n = At(j, 2, b)
                        pool.wait_ge(chosen, n(1))
                        nc.gpsimd.tensor_copy(idx[:, b, :], idx_all[:, bass.ds(n(0), 1), :].rearrange("p a s -> p (a s)")).then_inc(idx_ready, 1)
                        pool.wait_ge(idx_ready, n(1))
                        for s in range(SLOTS):
                            if s % PAIR == 0:
                                pool.wait_ge(used, j * (2 * STEPS) + (b * STEPS + s // PAIR + 1))
                                pool.sem_inc(pool_passed, 1)
                            nc.gpsimd.indirect_dma_start(
                                out=ring[:, s % RING, :], out_offset=None, in_=experts,
                                in_offset=bass.IndirectOffsetOnAxis(ap=idx[:, b, s:s + 1], axis=0)).then_inc(row_ld[s % RING], 16)

            @block.scalar
            def _(act):
                link = Chain(act, act_chain)

                def norm(n):
                    act.wait_ge(xn_ld, mul(n, 16, 16))
                    link(nc.scalar.activation(sqj[:], xn[:], ACT.Square, accum_out=stat[:, 0:1]))
                    nc.scalar.activation(stat[:, 1:2], stat[:, 0:1], ACT.Sqrt, bias=eps[:], scale=1.0 / D).then_inc(root, 1)

                def spread_h(n):
                    act.wait_ge(h_transposed, n(1))
                    nc.scalar.copy(hT[:], tb[:]).then_inc(hT_ready, 1)

                def spread_q(n, h):
                    act.wait_ge(q_full, mul(n, HEADS, h + 1))
                    nc.scalar.copy(qT[:], qp[:, 0:2 * P]).then_inc(q_ready, 1)

                def expo(n):
                    act.wait_ge(best_ready, n(1))
                    nc.scalar.activation(soft[:], soft[:], ACT.Exp).then_inc(exp_ready, 1)

                def first(n):
                    act.wait_ge(eps_set, 1)
                    norm(n)
                    spread_h(n)
                    for h in range(HEADS):
                        spread_q(n, h)
                    expo(n)

                def tile(n, more):
                    nxt = At(n.i, 1, n.base + 1)
                    for g in range(STEPS + 1):
                        if g < STEPS:
                            act.wait_ge(dotted, mul(n, SLOTS, PAIR * (g + 1)))
                            c = slice(PAIR * g, PAIR * (g + 1))
                            nc.scalar.activation(ge[:, c], dot[:, c], ACT.Gelu).then_inc(gelued, 1)
                        if g >= 1:
                            act.wait_ge(weighted, mul(n, STEPS, g))
                            act.wait_ge(used, mul(n, STEPS, g - 2 + BACK))
                            for c in range(PAIR):
                                s = PAIR * (g - 1) + c
                                last = nc.scalar.activation(diag[:, (g - 1) % 2, c, :], ident[:], ACT.Copy, scale=wgt[:, s:s + 1])
                            last.then_inc(diag_ready, 1)
                        if more:
                            if g == 0:
                                norm(nxt)
                            if g == 5:
                                spread_h(nxt)
                            if (h := head_at(g, 1)) is not None:
                                spread_q(nxt, h)
                            if g == 58:
                                expo(nxt)
                    act.wait_ge(y_ready, n(2))
                    link(nc.scalar.activation(sqj[:], y[:], ACT.Square, accum_out=stat[:, 3:4]))
                    nc.scalar.activation(stat[:, 4:5], stat[:, 3:4], ACT.Sqrt, bias=eps[:], scale=1.0 / D).then_inc(root2, 1)

                tiles(act, first, tile, link, 2)

            @block.vector
            def _(dve):
                link = Chain(dve, chain)

                def norm(n):
                    dve.wait_ge(root, n(1))
                    link(nc.vector.reciprocal(stat[:, 2:3], stat[:, 1:2]))
                    nc.vector.scalar_tensor_tensor(h_next[:], xn[:], stat[:, 2:3], gffn[:], ALU.mult, ALU.mult).then_inc(h_ready, 1)

                def top16(vals, index, scores, left, signal=None):
                    dve.sem_inc(dve_passed, 1)
                    link(nc.vector.max(vals[:, 0:8], scores))
                    dve.sem_inc(dve_passed, 1)
                    nc.vector.max_index(index[:, 0:8], vals[:, 0:8], scores)
                    last = nc.vector.match_replace(left, vals[:, 0:8], scores, -3e38)
                    link(last)
                    if signal:
                        signal()
                    dve.sem_inc(dve_passed, 1)
                    link(nc.vector.max(vals[:, 8:16], left))
                    dve.sem_inc(dve_passed, 1)
                    return nc.vector.max_index(index[:, 8:16], vals[:, 8:16], left)

                def choose(n, h):
                    dve.wait_ge(s_full, mul(n, HEADS, h + 1))
                    for p in range(2):
                        last = top16(top[:, h, p, :], topi[:, h, p, :], sp_[:, p * P:(p + 1) * P], rest[:, p, :],
                                     (lambda: dve.sem_inc(s_free, 1)) if p else None)
                    link(last)
                    nc.vector.tensor_copy(topf[:, h, :, :], topi[:, h, :, :])
                    sums = cand[:].rearrange("p (a b) -> p a b", a=TOPK)
                    link(nc.vector.tensor_tensor(sums, top[:, h, 0, :].unsqueeze(2).to_broadcast([P, TOPK, TOPK]),
                                                 top[:, h, 1, :].unsqueeze(1).to_broadcast([P, TOPK, TOPK]), ALU.add))
                    link(top16(best[:, h, :], pos[:], cand[:], crest[:]))
                    nc.vector.tensor_scalar(posd[:, 0, :], pos[:], 4, None, ALU.logical_shift_right)
                    link(nc.vector.tensor_scalar(posd[:, 1, :], pos[:], TOPK - 1, None, ALU.bitwise_and))
                    link(nc.vector.tensor_copy(posf[:], posd[:]))
                    for p in range(2):
                        last = nc.vector.tensor_tensor(hit[:, p, :, :], posf[:, p, :].unsqueeze(2).to_broadcast([P, TOPK, TOPK]),
                                                       iota[:].unsqueeze(1).to_broadcast([P, TOPK, TOPK]), ALU.is_equal)
                    link(last)
                    for p in range(2):
                        last = nc.vector.tensor_tensor(hit[:, p, :, :], hit[:, p, :, :],
                                                       topf[:, h, p, :].unsqueeze(1).to_broadcast([P, TOPK, TOPK]), ALU.mult)
                    link(last)
                    link(nc.vector.reduce_sum(sel[:], hit[:], AXX))
                    link(nc.vector.scalar_tensor_tensor(
                        idx_all[:, bass.ds(n(0), 1), h * TOPK:(h + 1) * TOPK].rearrange("p a s -> p (a s)"), sel[:, 0, :], float(KEYS),
                        sel[:, 1, :], ALU.mult, ALU.add))

                def soften(n):
                    dve.sem_inc(chosen, 1)
                    nc.vector.tensor_tensor(soft[:], best[:], best[:, :, 0:1].to_broadcast([P, HEADS, TOPK]),
                                            ALU.subtract).then_inc(best_ready, 1)

                def gates(n):
                    dve.wait_ge(exp_ready, n(1))
                    link(nc.vector.reduce_sum(ssum[:], soft[:], AXX))
                    link(nc.vector.reciprocal(ssum[:], ssum[:]))
                    link(nc.vector.tensor_tensor(g_next[:].rearrange("p (h c) -> p h c", c=TOPK), soft[:],
                                                 ssum[:].unsqueeze(2).to_broadcast([P, HEADS, TOPK]), ALU.mult))

                def first(n):
                    dve.sem_inc(used, BACK)
                    dve.sem_inc(s_free, 1)
                    dve.sem_inc(y_ready, 1)
                    nc.vector.memset(eps[:], EPS).then_inc(eps_set, 1)
                    dve.wait_ge(const_ld, 5 * 16)
                    norm(n)
                    for h in range(HEADS):
                        choose(n, h)
                    soften(n)
                    gates(n)

                def tile(n, more):
                    nxt = At(n.i, 1, n.base + 1)
                    nc.vector.tensor_copy(h_now[:], h_next[:])
                    link(nc.vector.tensor_copy(g_now[:], g_next[:]))
                    for g in range(STEPS + 1):
                        if g < STEPS:
                            for s in range(PAIR * g, PAIR * (g + 1)):
                                dve.wait_ge(row_ld[s % RING], mul(n, 16 * SLOTS // RING, 16 * (s // RING + 1)))
                                if s >= 2:
                                    dve.wait_ge(dotted, mul(n, SLOTS, s - 1))
                                nc.vector.tensor_tensor_reduce(
                                    out=junk[:, s % 2, :], in0=ring[:, s % RING, 0:D], in1=h_now[:], scale=1.0, scalar=0.0,
                                    op0=ALU.mult, op1=ALU.add, accum_out=dot[:, s:s + 1]).then_inc(dotted, 1)
                        if g >= 1:
                            dve.wait_ge(gelued, mul(n, STEPS, g))
                            c = slice(PAIR * (g - 1), PAIR * g)
                            nc.vector.tensor_tensor(wgt[:, c], ge[:, c], g_now[:, c], ALU.mult).then_inc(weighted, 1)
                        if more:
                            if g == 1:
                                norm(nxt)
                            if (h := head_at(g, 5)) is not None:
                                choose(nxt, h)
                            if g == 56:
                                soften(nxt)
                            if g == 60:
                                gates(nxt)
                    dve.wait_ge(xr_ld, mul(n, 16, 16))
                    dve.wait_ge(used, mul(n, STEPS, STEPS + BACK))
                    nc.vector.tensor_tensor(y[:], acc[:], xr[:], ALU.add).then_inc(y_ready, 1)
                    dve.wait_ge(root2, n(1))
                    link(nc.vector.reciprocal(stat[:, 5:6], stat[:, 4:5]))
                    dve.wait_ge(out_stored, mul(n, 16, 16))
                    nc.vector.scalar_tensor_tensor(yo[:], y[:], stat[:, 5:6], gfin[:], ALU.mult, ALU.mult).then_inc(yo_ready, 1)
                    dve.wait_ge(yo_ready, n(1))

                tiles(dve, first, tile, link, 150)

            @block.tensor
            def _(pe):
                def transpose_h(n):
                    pe.wait_ge(h_ready, n(1))
                    for k in range(KD):
                        last = nc.tensor.transpose(tb[:, k * P:(k + 1) * P], h_next[:, k * P:(k + 1) * P], ident[:])
                    last.then_inc(h_transposed, 1)

                def query(n, h):
                    if h == 0:
                        pe.wait_ge(hT_ready, n(1))
                    for p in range(2):
                        for k in range(KD):
                            last = nc.tensor.matmul(qp[:, p * P:(p + 1) * P], wq[:, k, (2 * h + p) * P:(2 * h + p + 1) * P],
                                                    hT[:, k * P:(k + 1) * P], start=(k == 0), stop=(k == KD - 1))
                    last.then_inc(q_full, 1)

                def scores(n, h):
                    pe.wait_ge(q_ready, mul(n, HEADS, h + 1))
                    pe.wait_ge(s_free, mul(n, HEADS, h + 1))
                    for p in range(2):
                        last = nc.tensor.matmul(sp_[:, p * P:(p + 1) * P], qT[:, p * P:(p + 1) * P], keys[:, 2 * h + p, :],
                                                start=True, stop=True)
                    last.then_inc(s_full, 1)

                def first(n):
                    pe.wait_ge(const_ld, 5 * 16)
                    transpose_h(n)
                    pe.wait_ge(w_ld, 16)
                    for h in range(HEADS):
                        query(n, h)
                        scores(n, h)

                def tile(n, more):
                    nxt = At(n.i, 1, n.base + 1)
                    pe.wait_ge(y_ready, n(1))
                    for g in range(STEPS + 1):
                        if g >= 1:
                            pe.wait_ge(diag_ready, mul(n, STEPS, g))
                            for c in range(PAIR):
                                s = PAIR * (g - 1) + c
                                for half in range(2):
                                    last = nc.tensor.matmul(acc[:, half * 512:half * 512 + 512], diag[:, (g - 1) % 2, c, :],
                                                            ring[:, s % RING, D + half * 512:D + half * 512 + 512],
                                                            start=(s == 0), stop=(s == SLOTS - 1))
                            last.then_inc(used, 1)
                        if more:
                            if g == 4:
                                transpose_h(nxt)
                            if (h := head_at(g, 0)) is not None:
                                query(nxt, h)
                            if (h := head_at(g, 3)) is not None:
                                scores(nxt, h)

                tiles(pe, first, tile)


def build(nc, x, g_mix, w_all, b_gate, sink, q_norm_g, k_norm_g, w_oa, w_ob, w_out, g_ffn, w_query,
          sub_keys, experts, g_final, rope, masks, ident, iota, out):
    def scratch(name, shape):
        return nc.dram_tensor(name, shape, F32, kind="Internal").ap()

    proj = scratch("proj_dram", (TOK, COLS))
    mixed = scratch("mixed_dram", (TOK, 2 * D))
    x2 = scratch("x2_dram", (TOK, D))
    with ExitStack() as sems:
        phase_project(nc, sems, x, g_mix, w_all, ident, proj)
        phase_attend(nc, sems, proj, rope, masks, sink, q_norm_g, k_norm_g, ident, mixed)
        phase_merge(nc, sems, x, mixed, proj, b_gate, w_oa, w_ob, w_out, ident, x2)
        phase_experts(nc, sems, x2, g_ffn, w_query, sub_keys, experts, g_final, ident, iota, out)


def kernel(x_prompt, x_sample, g_mix, w_in, w_gate, b_gate, sink, q_norm_g, k_norm_g, w_oa, w_ob, w_out,
           g_ffn, w_query, sub_keys, expert_u, expert_v, g_final):
    import numpy as np
    import concourse.bacc as bacc
    from concourse.bass_utils import run_bass_kernel_spmd

    def rope_tables(pos, dim):
        inv = (np.float64(10000.0) ** (-np.arange(0, dim, 2) / dim)).astype(np.float32)
        ang = pos.astype(np.float32)[:, None] * inv[None, :]
        return np.concatenate([np.cos(ang)] * 2, -1), np.concatenate([-np.sin(ang), np.sin(ang)], -1)

    pos = np.concatenate([np.arange(SAMPLE), np.arange(PROMPT)])
    cos_a, sin_a = rope_tables(pos, AD)
    cos_r, sin_r = rope_tables(pos // 64, BD // 2)
    cos_c, sin_c = rope_tables(pos % 64, BD // 2)
    rope = np.concatenate([cos_a, sin_a, cos_r, cos_c, sin_r, sin_c], -1).astype(np.float32)
    masks = np.zeros((NT, P, 3 * P), np.float32)
    q, k = np.arange(P)[:, None], np.arange(3 * P)[None, :] - P
    for t in range(NT):
        first, last = t in (0, ST), t in (ST - 1, NT - 1)
        ok = (np.abs(q - k) <= P) & ((k >= 0) | (not first)) & ((k < P) | (not last))
        masks[t] = np.where(ok, 0.0, NEG / A_SCALE)
    masks = masks.reshape(TOK, 3 * P)
    arrays = {
        "x": np.concatenate([x_sample[0], x_prompt[0]], 0),
        "g_mix": g_mix, "w_all": np.concatenate([w_in[0], w_gate[0]], 1), "b_gate": b_gate, "sink": sink,
        "q_norm_g": q_norm_g, "k_norm_g": k_norm_g, "w_oa": w_oa[0], "w_ob": w_ob[0], "w_out": w_out[0],
        "g_ffn": g_ffn, "w_query": w_query[0],
        "sub_keys": np.asarray(sub_keys)[0].reshape(2 * HEADS, KEYS, P).transpose(2, 0, 1),
        "experts": np.concatenate([expert_u[0], expert_v[0]], 1),
        "g_final": np.asarray(g_final)[None], "rope": rope, "masks": masks, "ident": np.eye(P, dtype=np.float32),
        "iota": np.arange(TOPK, dtype=np.float32)[None],
    }
    nc = bacc.Bacc("TRN2", target_bir_lowering=False, num_devices=1)
    ins, args = {}, []
    for name, a in arrays.items():
        a = np.ascontiguousarray(a)
        ins[f"in_{name}_dram"] = a
        args.append(nc.dram_tensor(f"in_{name}_dram", a.shape, F32, kind="ExternalInput").ap())
    args.append(nc.dram_tensor("out_0_dram", (TOK, D), F32, kind="ExternalOutput").ap())
    build(nc, *args)
    got = run_bass_kernel_spmd(nc, [ins], core_ids=[0]).results[0]["out_0_dram"]
    return got[SAMPLE:].reshape(1, PROMPT, D), got[:SAMPLE].reshape(1, SAMPLE, D)
```

```python
import concourse.bass as bass
from concourse import mybir
from contextlib import ExitStack

F32 = mybir.dt.float32
F32R = mybir.dt.float32r
I32 = mybir.dt.int32
U32 = mybir.dt.uint32
ALU = mybir.AluOpType
ACT = mybir.ActivationFunctionType
AXX = mybir.AxisListType.X

P = 128
D = 1024
KD = D // P
SAMPLE, PROMPT = 256, 1024
TOK = SAMPLE + PROMPT
NT = TOK // P
ST = SAMPLE // P
PT_ = PROMPT // P
AH, AKV, AD = 16, 4, 64
BH, BKV, BD = 8, 2, 128
A_SCALE = AD ** -0.5
B_SCALE = BD ** -0.5
QA, KA, VA, QB, KB, VB, GATE = 0, 1024, 1280, 1536, 2560, 2816, 3072
COLS = GATE + 2 * D
CW = 512
EPS = 1e-6
NEG = -1e30
ROPE_W = 2 * AD + 2 * BD
HEADS, KEYS, TOPK = 8, 128, 16
SLOTS = HEADS * TOPK


class Chain:

    def __init__(self, eng, sem):
        self.eng, self.sem = eng, sem
        self.base, self.i, self.per, self.n = 0, 0, 0, 0

    def __call__(self, ins):
        ins.then_inc(self.sem, 1)
        self.n += 1
        self.eng.wait_ge(self.sem, self.i * self.per + (self.base + self.n))

    def enter(self, i, per):
        self.base, self.n = self.base + self.n, 0
        self.i, self.per = i, per

    def leave(self, trips):
        assert self.n == self.per, (self.n, self.per)
        self.base += trips * self.per
        self.i, self.per, self.n = 0, 0, 0


class At:

    def __init__(self, i, per, base=0):
        self.i, self.per, self.base = i, per, base

    def __call__(self, local):
        return self.i * self.per + (self.base + local)


class Mem:

    def __init__(self, nc, ctx, sems, tag):
        self.nc, self.ctx, self.sems, self.tag = nc, ctx, sems, tag

    def sb(self, name, shape, dt=F32):
        return self.ctx.enter_context(self.nc.sbuf_tensor(f"{self.tag}_{name}", shape, dt))

    def ps(self, name, shape, dt=F32):
        return self.ctx.enter_context(self.nc.psum_tensor(f"{self.tag}_{name}", shape, dt))

    def sem(self, name):
        return self.sems.enter_context(self.nc.semaphore(f"{self.tag}_{name}"))


def phase_project(nc, sems, x, g_mix, w_all, ident_d, proj):
    with ExitStack() as ctx:
        m = Mem(nc, ctx, sems, "proj")
        ident = m.sb("ident", [P, P])
        grow = m.sb("grow", [P, D])
        xt = m.sb("xt", [P, 2, D])
        sq = m.sb("sq", [P, D])
        ht = m.sb("ht", [P, 2, D])
        ss, rt, rs = (m.sb(n, [P, 2]) for n in ("ss", "rt", "rs"))
        eps = m.sb("eps", [P, 1])
        hT_hi, hT_lo = m.sb("hT_hi", [P, KD, TOK], F32R), m.sb("hT_lo", [P, KD, TOK], F32R)
        w = m.sb("w", [P, KD, CW])
        w_hi, w_lo = m.sb("w_hi", [P, 2, KD, CW], F32R), m.sb("w_lo", [P, 2, KD, CW], F32R)
        stage = m.sb("stage", [P, 4, CW])
        tp = m.ps("tp", [P, 2, D])
        acc = m.ps("acc", [P, 4, CW])
        const_ld, eps_set = m.sem("const_ld"), m.sem("eps_set")
        x_ld = [m.sem(f"x_ld{b}") for b in range(2)]
        sum_ready, root_ready, h_ready = m.sem("sum_ready"), m.sem("root_ready"), m.sem("h_ready")
        h_transposed = m.sem("h_transposed")
        hi_ready = m.sem("hi_ready")
        lo_ready = m.sem("lo_ready")
        w_ld = m.sem("w_ld")
        w_hi_ready, w_lo_ready = m.sem("w_hi_ready"), m.sem("w_lo_ready")
        mm_tile = m.sem("mm_tile")
        staged = [m.sem("staged_act"), m.sem("staged_dve")]
        stored = [m.sem(f"stored{s}") for s in range(4)]
        dve_chain = m.sem("dve_chain")
        wv = w_all.rearrange("(k p) c -> p k c", p=P)
        CHUNKS = COLS // CW

        with nc.Block() as block:
            @block.sync
            def _(sp):
                for b in range(2):
                    sp.dma_start(xt[:, b, :], x[b * P:(b + 1) * P, :]).then_inc(x_ld[b], 16)
                sp.dma_start(grow[:], g_mix.broadcast_to([P, D])).then_inc(const_ld, 16)
                sp.dma_start(ident[:], ident_d).then_inc(const_ld, 16)
                sp.dma_start(w[:], wv[:, :, 0:CW]).then_inc(w_ld, 16)
                with sp.Fori(0, NT // 2 - 1) as j:
                    for b in range(2):
                        sp.wait_ge(h_ready, j * 2 + (b + 1))
                        sp.dma_start(xt[:, b, :], x[bass.ds(j * 2 * P + (b + 2) * P, P), :]).then_inc(x_ld[b], 16)

                def chunk(c, b, more):
                    if more:
                        sp.wait_ge(w_lo_ready, c(1))
                        sp.dma_start(w[:], wv[:, :, bass.ds(c(1) * CW, CW)]).then_inc(w_ld, 16)
                    for t in range(NT):
                        u = b * NT + t
                        sp.wait_ge(staged[u % 2], c.i * NT + (c.base * NT // 2 + t // 2 + 1 + 2))
                        sp.dma_start(proj[t * P:(t + 1) * P, bass.ds(c(0) * CW, CW)],
                                     stage[:, u % 4, :]).then_inc(stored[u % 4], 16)

                with sp.Fori(0, CHUNKS // 2 - 1) as j:
                    for b in range(2):
                        chunk(At(j, 2, b), b, True)
                chunk(At(0, 2, CHUNKS - 2), 0, True)
                chunk(At(0, 2, CHUNKS - 1), 1, False)
                for s in range(4):
                    sp.wait_ge(stored[s], 16 * (CHUNKS * NT // 4 + 1))

            @block.scalar
            def _(act):
                act.sem_inc(staged[0], 2)
                act.wait_ge(eps_set, 1)
                with act.Fori(0, NT // 2) as j:
                    for b in range(2):
                        act.wait_ge(sum_ready, j * 2 + (b + 1))
                        nc.scalar.activation(rt[:, b:b + 1], ss[:, b:b + 1], ACT.Sqrt, bias=eps[:],
                                             scale=1.0 / D).then_inc(root_ready, 1)
                        act.wait_ge(h_transposed, j * 2 + (b + 1 + 2))
                        nc.scalar.copy(hT_hi[:, :, bass.ds(j * 2 * P + b * P, P)],
                                       tp[:, b, :].rearrange("p (k c) -> p k c", c=P)).then_inc(hi_ready, 1)

                def split(b, c):
                    act.wait_ge(w_ld, c(1) * 16)
                    nc.scalar.copy(w_hi[:, b, :, :], w[:]).then_inc(w_hi_ready, 1)

                def chunk(c, b, more):
                    for t in range(NT):
                        u = b * NT + t
                        if u % 2 == 0:
                            act.wait_ge(mm_tile, c.i * 2 * NT + (c.base * NT + t + 1))
                            act.wait_ge(stored[u % 4], c.i * (16 * NT // 2) + (c.base // 2 * (16 * NT // 2) + 16 * (u // 4 + 1)))
                            nc.scalar.copy(stage[:, u % 4, :], acc[:, u % 4, :]).then_inc(staged[0], 1)
                        if t == 1 and more:
                            split(1 - b, At(c.i, 2, c.base + 1))

                split(0, At(0, 2, 0))
                with act.Fori(0, CHUNKS // 2 - 1) as j:
                    for b in range(2):
                        chunk(At(j, 2, b), b, True)
                chunk(At(0, 2, CHUNKS - 2), 0, True)
                chunk(At(0, 2, CHUNKS - 1), 1, False)

            @block.vector
            def _(dve):
                dve.sem_inc(staged[1], 2)
                dve.sem_inc(lo_ready, 2)
                for s in range(4):
                    dve.sem_inc(stored[s], 16)
                nc.vector.memset(eps[:], EPS).then_inc(eps_set, 1)
                link = Chain(dve, dve_chain)

                def rest(b, j):
                    dve.wait_ge(hi_ready, j * 2 + (b + 1))
                    cols = bass.ds(j * 2 * P + b * P, P)
                    nc.vector.tensor_tensor(hT_lo[:, :, cols], tp[:, b, :].rearrange("p (k c) -> p k c", c=P),
                                            hT_hi[:, :, cols].bitcast(F32), ALU.subtract).then_inc(lo_ready, 1)

                def norm(b, j):
                    dve.wait_ge(x_ld[b], j * 16 + 16)
                    nc.vector.tensor_tensor_reduce(out=sq[:], in0=xt[:, b, :], in1=xt[:, b, :], scale=1.0, scalar=0.0,
                                                   op0=ALU.mult, op1=ALU.add, accum_out=ss[:, b:b + 1]).then_inc(sum_ready, 1)
                    dve.wait_ge(root_ready, j * 2 + (b + 1))
                    link(nc.vector.reciprocal(rs[:, b:b + 1], rt[:, b:b + 1]))
                    dve.wait_ge(h_transposed, j * 2 + (b + 1))
                    nc.vector.scalar_tensor_tensor(ht[:, b, :], xt[:, b, :], rs[:, b:b + 1], grow[:],
                                                   ALU.mult, ALU.mult).then_inc(h_ready, 1)

                dve.wait_ge(const_ld, 32)
                with dve.Fori(0, NT // 2) as j:
                    link.enter(j, 2)
                    norm(0, j)
                    norm(1, j)
                    rest(0, j)
                    rest(1, j)
                    link.leave(NT // 2)

                def split(b, c):
                    dve.wait_ge(w_hi_ready, c(1))
                    nc.vector.tensor_tensor(w_lo[:, b, :, :], w[:], w_hi[:, b, :, :].bitcast(F32),
                                            ALU.subtract).then_inc(w_lo_ready, 1)

                def chunk(c, b, more):
                    for t in range(NT):
                        u = b * NT + t
                        if u % 2 == 1:
                            dve.wait_ge(mm_tile, c.i * 2 * NT + (c.base * NT + t + 1))
                            dve.wait_ge(stored[u % 4], c.i * (16 * NT // 2) + (c.base // 2 * (16 * NT // 2) + 16 * (u // 4 + 1)))
                            nc.vector.tensor_copy(stage[:, u % 4, :], acc[:, u % 4, :]).then_inc(staged[1], 1)
                        if t == 1 and more:
                            split(1 - b, At(c.i, 2, c.base + 1))

                split(0, At(0, 2, 0))
                with dve.Fori(0, CHUNKS // 2 - 1) as j:
                    for b in range(2):
                        chunk(At(j, 2, b), b, True)
                chunk(At(0, 2, CHUNKS - 2), 0, True)
                chunk(At(0, 2, CHUNKS - 1), 1, False)

            @block.tensor
            def _(pe):
                pe.sem_inc(h_transposed, 2)
                pe.wait_ge(const_ld, 32)
                with pe.Fori(0, NT // 2) as j:
                    for b in range(2):
                        pe.wait_ge(h_ready, j * 2 + (b + 1))
                        pe.wait_ge(lo_ready, j * 2 + (b + 1))
                        for k in range(KD):
                            last = nc.tensor.transpose(tp[:, b, k * P:(k + 1) * P], ht[:, b, k * P:(k + 1) * P],
                                                       ident[:])
                        last.then_inc(h_transposed, 1)
                pe.wait_ge(lo_ready, NT + 2)
                with pe.Fori(0, CHUNKS // 2) as j:
                    for b in range(2):
                        pe.wait_ge(w_lo_ready, j * 2 + (b + 1))
                        for t in range(NT):
                            u = b * NT + t
                            pe.wait_ge(staged[u % 2], j * NT + (u // 2 + 1))
                            for k in range(KD):
                                cols = slice(t * P, (t + 1) * P)
                                for n, (h, v) in enumerate(((hT_hi, w_hi), (hT_hi, w_lo), (hT_lo, w_hi))):
                                    last = nc.tensor.matmul(acc[:, u % 4, :], h[:, k, cols], v[:, b, k, :],
                                                            start=(k == 0 and n == 0), stop=(k == KD - 1 and n == 2))
                            last.then_inc(mm_tile, 1)


def rope_steps(e, link, out, x, tmp, cos, sin, heads, sections):
    width = 64 * sections
    full = lambda ap: ap.rearrange("p (h c) -> p h c", c=width)
    e.tensor_tensor(full(out), full(x), cos.unsqueeze(1).to_broadcast([P, heads, width]), ALU.mult)
    for half in range(2):
        if sections == 1:
            cut = lambda ap, t: ap.rearrange("p (h t c) -> p h t c", t=2, c=32)[:, :, t, :]
            s = sin[:, half * 32:half * 32 + 32].unsqueeze(1).to_broadcast([P, heads, 32])
        else:
            cut = lambda ap, t: ap.rearrange("p (h s t c) -> p h s t c", s=sections, t=2, c=32)[:, :, :, t, :]
            s = sin.rearrange("p (s t c) -> p s t c", t=2, c=32)[:, :, half, :].unsqueeze(1).to_broadcast(
                [P, heads, sections, 32])
        last = e.tensor_tensor(cut(tmp, half), cut(x, 1 - half), s, ALU.mult)
    link(last)
    return e.tensor_tensor(out, out, tmp, ALU.add)


def phase_attend(nc, sems, proj, rope, masks, sink, q_norm_g, k_norm_g, ident_d, mixed):
    with ExitStack() as ctx:
        m = Mem(nc, ctx, sems, "att")
        BQK = 1280
        NB = BQK // BD
        ident = m.sb("ident", [P, P])
        sinks = m.sb("sinks", [P, AH])
        qg, kg = m.sb("qg", [P, BD]), m.sb("kg", [P, BD])
        eps = m.sb("eps", [P, 1])
        kTA = m.sb("kTA", [P, AKV * 2, (NT + 2) * P])
        kTB = m.sb("kTB", [P, BKV, TOK])
        vA = m.sb("vA", [P, NT + 2, AKV * AD])
        vB = m.sb("vB", [P, NT, BKV * BD])
        rB = m.sb("rB", [P, NT, NB])
        const_ld, v_ld = m.sem("const_ld"), m.sem("v_ld")
        eps_set, pads_set = m.sem("eps_set"), m.sem("pads_set")
        with ExitStack() as kctx:
            mk = Mem(nc, kctx, sems, "key")
            raw = mk.sb("raw", [P, 2, BQK + 256])
            tab = mk.sb("tab", [P, 2, ROPE_W])
            sq = mk.sb("sq", [P, 2, BQK])
            ss, rt = mk.sb("ss", [P, 2, NB]), mk.sb("rt", [P, 2, NB])
            kn = mk.sb("kn", [P, 256])
            kr = mk.sb("kr", [P, 2, AKV * 2 * P + 256])
            ka = mk.sb("ka", [P, 256])
            KRA = AKV * 2 * P
            tmp = mk.sb("tmp", [P, 256])
            tpA, tpB = mk.ps("tpA", [P, 2, AKV * 2 * P]), mk.ps("tpB", [P, 2, 512])
            ld = [mk.sem(f"ld{b}") for b in range(2)]
            sq_ready, ss_ready, rt_ready, kr_ready = (mk.sem(n) for n in ("sq_ready", "ss_ready", "rt_ready", "kr_ready"))
            k_transposed = mk.sem("k_transposed")
            k_copied = mk.sem("k_copied")
            chain = mk.sem("chain")
            with nc.Block() as block:
                @block.sync
                def _(sp):
                    for dst, src in ((ident[:], ident_d), (sinks[:], sink.broadcast_to([P, AH])),
                                     (qg[:], q_norm_g.broadcast_to([P, BD])), (kg[:], k_norm_g.broadcast_to([P, BD]))):
                        sp.dma_start(dst, src).then_inc(const_ld, 16)

                    def load(b, row):
                        sp.dma_start(raw[:, b, 0:BQK], proj[bass.ds(row, P), QB:VB]).then_inc(ld[b], 16)
                        sp.dma_start(raw[:, b, BQK:], proj[bass.ds(row, P), KA:VA]).then_inc(ld[b], 16)
                        sp.dma_start(tab[:, b, :], rope[bass.ds(row, P), :]).then_inc(ld[b], 16)

                    load(0, 0)
                    load(1, P)
                    sp.dma_start(vA[:, 1:NT + 1, :], proj[:, VA:QB].rearrange("(t p) c -> p t c", p=P)).then_inc(v_ld, 16)
                    sp.dma_start(vB[:], proj[:, VB:GATE].rearrange("(t p) c -> p t c", p=P)).then_inc(v_ld, 16)
                    with sp.Fori(0, NT // 2 - 1) as j:
                        for b in range(2):
                            sp.wait_ge(kr_ready, j * 2 + (b + 1))
                            load(b, j * 2 * P + (b + 2) * P)
                    sp.wait_ge(v_ld, 32)

                @block.gpsimd
                def _(pool):
                    nc.gpsimd.memset(kTA[:, :, 0:P], 0.0)
                    nc.gpsimd.memset(kTA[:, :, (NT + 1) * P:], 0.0)
                    nc.gpsimd.memset(vA[:, 0, :], 0.0)
                    nc.gpsimd.memset(vA[:, NT + 1, :], 0.0).then_inc(pads_set, 1)
                    with pool.Fori(0, NT // 2) as j:
                        for b in range(2):
                            pool.wait_ge(ld[b], j * 48 + 48)
                            pool.wait_ge(ss_ready, j * 2 + (b + 1))
                            nc.gpsimd.tensor_tensor(sq[:, b, :], raw[:, b, 0:BQK], raw[:, b, 0:BQK],
                                                    ALU.mult).then_inc(sq_ready, 1)

                @block.scalar
                def _(act):
                    act.sem_inc(k_copied, 4)
                    act.wait_ge(eps_set, 1)
                    with act.Fori(0, NT // 2) as j:
                        for b in range(2):
                            act.wait_ge(ss_ready, j * 2 + (b + 1 + 2))
                            nc.scalar.activation(rt[:, b, :], ss[:, b, :], ACT.Sqrt, bias=eps[:],
                                                 scale=1.0 / BD).then_inc(rt_ready, 1)
                            act.wait_ge(k_transposed, j * 2 + (b + 1 + 2))
                            nc.scalar.copy(kTA[:, :, bass.ds(j * 2 * P + (b + 1) * P, P)],
                                           tpA[:, b, :].rearrange("p (h c) -> p h c", c=P)).then_inc(k_copied, 1)
                            nc.scalar.copy(kTB[:, :, bass.ds(j * 2 * P + b * P, P)],
                                           tpB[:, b, 0:256].rearrange("p (h c) -> p h c", c=P)).then_inc(k_copied, 1)

                @block.vector
                def _(dve):
                    link = Chain(dve, chain)
                    dve.sem_inc(ss_ready, 2)
                    nc.vector.memset(eps[:], EPS).then_inc(eps_set, 1)
                    link(nc.vector.memset(kr[:], 0.0))
                    dve.wait_ge(const_ld, 64)
                    with dve.Fori(0, NT // 2) as j:
                        link.enter(j, 10)
                        for b in range(2):
                            dve.wait_ge(sq_ready, j * 2 + (b + 1))
                            nc.vector.reduce_sum(ss[:, b, :], sq[:, b, :].rearrange("p (h c) -> p h c", c=BD),
                                                 AXX).then_inc(ss_ready, 1)
                            dve.wait_ge(k_transposed, j * 2 + (b + 1))
                            link(rope_steps(nc.vector, link, ka[:], raw[:, b, BQK:], tmp[:],
                                            tab[:, b, 0:AD], tab[:, b, AD:2 * AD], AKV, 1))
                            for v in range(2):
                                nc.vector.tensor_copy(
                                    kr[:, b, 0:KRA].rearrange("p (h v c) -> p h v c", v=2, c=P)[:, :, v, v * AD:(v + 1) * AD],
                                    ka[:].rearrange("p (h c) -> p h c", c=AD))
                            dve.wait_ge(rt_ready, j * 2 + (b + 1))
                            link(nc.vector.reciprocal(rB[:, bass.ds(j * 2 + b, 1), :], rt[:, b, :].unsqueeze(1)))
                            keys = raw[:, b, BH * BD:BQK].rearrange("p (h c) -> p h c", c=BD)
                            kn3 = kn[:].rearrange("p (h c) -> p h c", c=BD)
                            for h in range(BKV):
                                last = nc.vector.scalar_tensor_tensor(
                                    kn3[:, h, :], keys[:, h, :], rB[:, bass.ds(j * 2 + b, 1), BH + h], kg[:],
                                    ALU.mult, ALU.mult)
                            link(last)
                            rope_steps(nc.vector, link, kr[:, b, KRA:], kn[:], tmp[:],
                                       tab[:, b, 128:256], tab[:, b, 256:384], BKV, 2).then_inc(kr_ready, 1)
                            dve.wait_ge(kr_ready, j * 2 + (b + 1))
                        link.leave(NT // 2)

                @block.tensor
                def _(pe):
                    pe.sem_inc(k_transposed, 2)
                    pe.wait_ge(const_ld, 64)
                    with pe.Fori(0, NT // 2) as j:
                        for b in range(2):
                            pe.wait_ge(kr_ready, j * 2 + (b + 1))
                            pe.wait_ge(k_copied, j * 4 + (2 * b + 2))
                            for h in range(2 * AKV):
                                nc.tensor.transpose(tpA[:, b, h * P:(h + 1) * P], kr[:, b, h * P:(h + 1) * P], ident[:])
                            for h in range(BKV):
                                last = nc.tensor.transpose(tpB[:, b, h * P:(h + 1) * P],
                                                           kr[:, b, KRA + h * BD:KRA + (h + 1) * BD], ident[:])
                            last.then_inc(k_transposed, 1)

        NH = AH + BH
        SW = 3 * P + 1
        q = m.sb("q", [P, 2, 2 * D])
        tab = m.sb("tab", [P, 2, ROPE_W])
        mask = m.sb("mask", [P, 2, 3 * P])
        qn, qtmp = m.sb("qn", [P, D]), m.sb("qtmp", [P, D])
        qr = m.sb("qr", [P, 2, 2 * D])
        qT = m.sb("qT", [P, 16, P])
        Sm = m.sb("Sm", [P, 4, SW])
        mx, nm, rsum, rinv = (m.sb(n, [P, NH]) for n in ("mx", "nm", "rsum", "rinv"))
        prob = m.sb("prob", [P, 4 * 512])
        probT = m.sb("probT", [P, 2, PROMPT])
        O = m.sb("O", [P, 2 * D])
        OT = m.sb("OT", [P, 2 * D])
        S = m.ps("S", [P, 4 * 512])
        tb = m.ps("tb", [P, 2, 512])
        Op = m.ps("Op", [P, 2, 512])
        q_ld = [m.sem(f"q_ld{b}") for b in range(2)]
        mask_ld = [m.sem(f"mask_ld{b}") for b in range(2)]
        q_ready = m.sem("q_ready")
        t_full = m.sem("t_full")
        t_free = [m.sem("t_free_act"), m.sem("t_free_dve")]
        s_full = m.sem("s_full")
        nm_ready = m.sem("nm_ready")
        prob_ready = m.sem("prob_ready")
        o_full = m.sem("o_full")
        o_free = m.sem("o_free")
        ot_stored = m.sem("ot_stored")
        pool_chain, chain = m.sem("pool_chain"), m.sem("chain")
        AHEAD = 3

        def steps():
            done = 0
            for k in range(NH + 1):
                upto = min(k + AHEAD, AH - 1) if k + 1 < AH else k + 1
                while k < NH and done <= min(upto, NH - 1):
                    yield "scores", done
                    done += 1
                if k < NH:
                    yield "spread", k
                if k >= 1:
                    yield "values", k - 1

        def slot(h, width):
            at = h % 4 * 512 if h < AH else h % 2 * 1024
            return slice(at, at + width)

        def freed(k):
            return k - 3 if k < AH else {AH: AH - 2, AH + 1: AH}.get(k, k - 1)

        LAST = {7: 0, 15: 1, 19: 2, 23: 3}
        FIRST = {0: 0, 8: 1, 16: 2, 20: 3}

        def uses(nk):
            return 4 + AH + BH * -(-nk // 4) + 4

        def q_moves():
            for u in range(4):
                yield u, tb[:, u % 2, :].rearrange("p (h c) -> p h c", c=P), qT[:, 4 * u:4 * u + 4, :]

        def p_moves(h, nk):
            if h < AH:
                u = 4 + h
                yield u, tb[:, u % 2, 0:3 * P], probT[:, h % 2, 0:3 * P]
                return
            banks = -(-nk // 4)
            for c in range(banks):
                u, n = 4 + AH + (h - AH) * banks + c, min(4, nk - 4 * c) * P
                yield u, tb[:, u % 2, 0:n], probT[:, h % 2, 512 * c:512 * c + n]

        def o_moves(nk):
            for c in range(4):
                u = uses(nk) - 4 + c
                yield u, tb[:, u % 2, :], OT[:, 512 * c:512 * c + 512]

        def pairs(e, body, split_last=False):
            body(ST, 0, 0, 0, 0)
            full = PT_ // 2
            base = (ST, ST * uses(ST))
            with e.Fori(0, full - split_last) as j:
                body(PT_, j, *base, 1)
            if split_last:
                body(PT_, full - 1, *base, 2)

        with nc.Block() as block:
            @block.sync
            def _(sp):
                def load(b, row):
                    sp.dma_start(q[:, b, 0:D], proj[bass.ds(row, P), QA:KA]).then_inc(q_ld[b], 16)
                    sp.dma_start(q[:, b, D:], proj[bass.ds(row, P), QB:KB]).then_inc(q_ld[b], 16)
                    sp.dma_start(tab[:, b, :], rope[bass.ds(row, P), :]).then_inc(q_ld[b], 16)
                    sp.dma_start(mask[:, b, :], masks[bass.ds(row, P), :]).then_inc(mask_ld[b], 16)

                load(0, 0)
                load(1, P)

                def pair(nk, j, tiles, fills, part):
                    for b in range(2):
                        n = At(j, 2, tiles + b)
                        half = At(j, uses(nk), (fills + b * uses(nk)) // 2)
                        for par in range(2):
                            sp.wait_ge(t_free[par], half(uses(nk) // 2 + 1))
                        sp.dma_start(mixed[bass.ds(n(0) * P, P), :], OT[:]).then_inc(ot_stored, 16)
                        if part < 2:
                            load(b, n(2) * P)

                pairs(sp, pair, True)
                sp.wait_ge(ot_stored, 16 * (NT + 1))

            @block.gpsimd
            def _(pool):
                link = Chain(pool, pool_chain)
                pool.sem_inc(ot_stored, 16)

                def pair(nk, j, tiles, fills, part):
                    link.enter(j, 10)
                    for b in range(2):
                        n = At(j, 2, tiles + b)
                        pool.wait_ge(q_ld[b], j * 48 + (48 + 24 * tiles))
                        if part:
                            pool.wait_ge(s_full, (n(-2)) * NH + 1)
                        three = lambda ap: ap.rearrange("p (h c) -> p h c", c=BD)
                        link(nc.gpsimd.tensor_tensor(three(qn[:]), three(q[:, b, D:]),
                                                     rB[:, bass.ds(n(0), 1), 0:BH].rearrange("p a h -> p (a h)").unsqueeze(2).to_broadcast([P, BH, BD]), ALU.mult))
                        link(nc.gpsimd.tensor_tensor(three(qn[:]), three(qn[:]),
                                                     qg[:].unsqueeze(1).to_broadcast([P, BH, BD]), ALU.mult))
                        link(rope_steps(nc.gpsimd, link, qr[:, b, D:], qn[:], qtmp[:],
                                        tab[:, b, 128:256], tab[:, b, 256:384], BH, 2))
                        rope_steps(nc.gpsimd, link, qr[:, b, 0:D], q[:, b, 0:D], qtmp[:],
                                   tab[:, b, 0:AD], tab[:, b, AD:2 * AD], AH, 1).then_inc(q_ready, 1)
                        pool.wait_ge(q_ready, n(1))
                    link.leave(1 if not part else PT_ // 2)

                pairs(pool, pair)

            @block.scalar
            def _(act):
                act.sem_inc(t_free[0], 1)

                def pair(nk, j, tiles, fills, part):
                    for b in range(2):
                        n = At(j, 2, tiles + b)
                        head = At(j, 2 * NH, (tiles + b) * NH)
                        fill = At(j, 2 * uses(nk), fills + b * uses(nk))

                        def move(moves):
                            for u, src, dst in moves:
                                if u % 2 == 0:
                                    act.wait_ge(t_full, fill(u + 1))
                                    nc.scalar.copy(dst, src).then_inc(t_free[0], 1)

                        move(q_moves())
                        for stage, k in steps():
                            if stage == "scores":
                                act.wait_ge(nm_ready, head(k + 1))
                                if k < AH:
                                    nc.scalar.activation(prob[:, slot(k, SW)], Sm[:, k % 4, :], ACT.Exp, bias=nm[:, k:k + 1],
                                                         accum_out=rsum[:, k:k + 1]).then_inc(prob_ready, 1)
                                else:
                                    nc.scalar.activation(prob[:, slot(k, nk * P)], S[:, slot(k, nk * P)], ACT.Exp,
                                                         bias=nm[:, k:k + 1], scale=B_SCALE,
                                                         accum_out=rsum[:, k:k + 1]).then_inc(prob_ready, 1)
                            elif stage == "spread":
                                move(p_moves(k, nk))
                        act.wait_ge(ot_stored, n(1) * 16)
                        move(o_moves(nk))

                pairs(act, pair)

            @block.vector
            def _(dve):
                link = Chain(dve, chain)
                dve.sem_inc(o_free, 2)
                dve.sem_inc(t_free[1], 1)

                def pair(nk, j, tiles, fills, part):
                    link.enter(j, 2 * (NH + 4))
                    for b in range(2):
                        n = At(j, 2, tiles + b)
                        head = At(j, 2 * NH, (tiles + b) * NH)
                        bank = At(j, 8, (tiles + b) * 4)
                        fill = At(j, 2 * uses(nk), fills + b * uses(nk))

                        def move(moves):
                            for u, src, dst in moves:
                                if u % 2 == 1:
                                    dve.wait_ge(t_full, fill(u + 1))
                                    nc.vector.tensor_copy(dst, src).then_inc(t_free[1], 1)

                        move(q_moves())
                        dve.wait_ge(mask_ld[b], j * 16 + (16 + 8 * tiles))
                        for stage, k in steps():
                            if stage == "scores" and k < AH:
                                dve.wait_ge(s_full, head(k + 1))
                                if k >= 4:
                                    dve.wait_ge(prob_ready, head(freed(k)))
                                nc.vector.tensor_copy(Sm[:, k % 4, SW - 1:SW], sinks[:, k:k + 1])
                                link(nc.vector.tensor_tensor_reduce(
                                    out=Sm[:, k % 4, 0:SW - 1], in0=S[:, slot(k, SW - 1)], in1=mask[:, b, :], scale=A_SCALE,
                                    scalar=NEG, op0=ALU.add, op1=ALU.max, accum_out=mx[:, k:k + 1]))
                                nc.vector.tensor_scalar(nm[:, k:k + 1], mx[:, k:k + 1], sinks[:, k:k + 1], -1.0,
                                                        ALU.max, ALU.mult).then_inc(nm_ready, 1)
                            elif stage == "scores":
                                dve.wait_ge(s_full, head(k + 1))
                                link(nc.vector.reduce_max(mx[:, k:k + 1], S[:, slot(k, nk * P)], AXX))
                                nc.vector.tensor_scalar(nm[:, k:k + 1], mx[:, k:k + 1], -B_SCALE, None,
                                                        ALU.mult).then_inc(nm_ready, 1)
                            elif stage == "spread":
                                move(p_moves(k, nk))
                            elif k in LAST:
                                w = LAST[k]
                                hs = slice(8 * w, 8 * w + 8) if w < 2 else slice(4 * w + 8, 4 * w + 12)
                                nh = hs.stop - hs.start
                                dve.wait_ge(o_full, bank(w + 1))
                                link(nc.vector.reciprocal(rinv[:, hs], rsum[:, hs]))
                                nc.vector.tensor_tensor(
                                    O[:, 512 * w:512 * w + 512].rearrange("p (h c) -> p h c", h=nh),
                                    Op[:, w % 2, :].rearrange("p (h c) -> p h c", h=nh),
                                    rinv[:, hs].unsqueeze(2).to_broadcast([P, nh, 512 // nh]), ALU.mult).then_inc(o_free, 1)
                        dve.wait_ge(ot_stored, n(1) * 16)
                        move(o_moves(nk))
                    link.leave(1 if not part else PT_ // 2)

                pairs(dve, pair)

            @block.tensor
            def _(pe):
                def pair(nk, j, tiles, fills, part):
                    for b in range(2):
                        n = At(j, 2, tiles + b)
                        head = At(j, 2 * NH, (tiles + b) * NH)
                        bank = At(j, 8, (tiles + b) * 4)
                        half = At(j, uses(nk), (fills + b * uses(nk)) // 2)

                        def free(u):
                            pe.wait_ge(t_free[u % 2], half(u // 2 + 1))

                        def moved(u):
                            pe.wait_ge(t_free[u % 2], half(u // 2 + 2))

                        pe.wait_ge(q_ready, n(1))
                        for u, src, dst in q_moves():
                            free(u)
                            for c in range(4):
                                at = (4 * u + c) * P
                                last = nc.tensor.transpose(tb[:, u % 2, c * P:(c + 1) * P], qr[:, b, at:at + P], ident[:])
                            last.then_inc(t_full, 1)
                        for stage, k in steps():
                            if stage == "scores":
                                if k < AH and k % 8 == 0:
                                    moved(k // 8)
                                if k >= AH and k % 4 == 0:
                                    moved(2 + (k - AH) // 4)
                                if k >= 4:
                                    pe.wait_ge(prob_ready, head(freed(k)))
                                if k < AH:
                                    last = nc.tensor.matmul(S[:, slot(k, 3 * P)], qT[:, k // 2, :],
                                                            kTA[:, k // 4 * 2 + k % 2, bass.ds(n(0) * P, 3 * P)],
                                                            start=True, stop=True)
                                else:
                                    key0 = 0 if nk == ST else SAMPLE
                                    for c in range(0, nk * P, 512):
                                        w = min(512, nk * P - c)
                                        at = slot(k, w).start + c
                                        last = nc.tensor.matmul(S[:, at:at + w], qT[:, 8 + k - AH, :],
                                                                kTB[:, (k - AH) // 4, key0 + c:key0 + c + w],
                                                                start=True, stop=True)
                                last.then_inc(s_full, 1)
                            elif stage == "spread":
                                pe.wait_ge(prob_ready, head(k + 1))
                                for c, (u, src, dst) in enumerate(p_moves(k, nk)):
                                    free(u)
                                    for t in range(src.shape[-1] // P):
                                        at = slot(k, P).start + c * 512 + t * P
                                        last = nc.tensor.transpose(tb[:, u % 2, t * P:(t + 1) * P], prob[:, at:at + P], ident[:])
                                    last.then_inc(t_full, 1)
                            else:
                                h = k
                                for u, src, dst in p_moves(h, nk):
                                    moved(u)
                                if h in FIRST:
                                    pe.wait_ge(o_free, bank(FIRST[h] + 1))
                                w = h // 8 if h < AH else 2 + (h - AH) // 4
                                if h < AH:
                                    dst = Op[:, w % 2, (h % 8) * AD:(h % 8) * AD + AD]
                                    for t in range(3):
                                        kv = h // 4
                                        last = nc.tensor.matmul(dst, probT[:, h % 2, t * P:(t + 1) * P],
                                                                vA[:, bass.ds(n(t), 1), kv * AD:(kv + 1) * AD].rearrange("p a c -> p (a c)"),
                                                                start=(t == 0), stop=(t == 2))
                                else:
                                    dst = Op[:, w % 2, (h % 4) * BD:(h % 4) * BD + BD]
                                    for t in range(nk):
                                        kv = (h - AH) // 4
                                        last = nc.tensor.matmul(dst, probT[:, h % 2, t * P:(t + 1) * P],
                                                                vB[:, (0 if nk == ST else ST) + t, kv * BD:(kv + 1) * BD],
                                                                start=(t == 0), stop=(t == nk - 1))
                                if h in LAST:
                                    last.then_inc(o_full, 1)
                        for c, (u, src, dst) in enumerate(o_moves(nk)):
                            pe.wait_ge(o_free, bank(c + 1 + 2))
                            free(u)
                            for t in range(4):
                                last = nc.tensor.transpose(tb[:, u % 2, t * P:(t + 1) * P],
                                                           O[:, 512 * c + t * P:512 * c + (t + 1) * P], ident[:])
                            last.then_inc(t_full, 1)

                pairs(pe, pair)


def phase_merge(nc, sems, x, mixed, proj, b_gate, w_oa, w_ob, w_out, ident_d, x2):
    with ExitStack() as ctx:
        m = Mem(nc, ctx, sems, "mrg")
        ident = m.sb("ident", [P, P])
        wa, wb, wo = (m.sb(n, [P, KD, D]) for n in ("wa", "wb", "wo"))
        bg = m.sb("bg", [P, 2 * D])
        mixT = m.sb("mixT", [P, 2, 2 * D])
        gate = m.sb("gate", [P, 2, 2 * D])
        xt = m.sb("xt", [P, 2, D])
        part = m.sb("part", [P, 2, D])
        merged = m.sb("merged", [P, D])
        mT = m.sb("mT", [P, D])
        res = m.sb("res", [P, D])
        Y = m.ps("Y", [P, 2, D])
        tb = m.ps("tb", [P, D])
        Z = m.ps("Z", [P, D])
        w_ld = [m.sem(f"w_ld{i}") for i in range(4)]
        ld = [m.sem(f"ld{b}") for b in range(2)]
        x_ld = [m.sem(f"x_ld{b}") for b in range(2)]
        biased, gated = m.sem("biased"), m.sem("gated")
        y_full = m.sem("y_full")
        y_free = m.sem("y_free")
        merged_ready = m.sem("merged_ready")
        m_transposed = m.sem("m_transposed")
        mT_ready = m.sem("mT_ready")
        z_full = m.sem("z_full")
        res_ready = m.sem("res_ready")
        res_stored = m.sem("res_stored")
        chain = m.sem("chain")

        def order(e, first, second, link=None):
            first(At(0, 2, 0), 0)
            with e.Fori(0, NT // 2 - 1) as j:
                if link:
                    link.enter(j, 2)
                for b in range(2):
                    first(At(j, 2, b + 1), (b + 1) % 2)
                    second(At(j, 2, b), b)
                if link:
                    link.leave(NT // 2 - 1)
            first(At(0, 2, NT - 1), 1)
            second(At(0, 2, NT - 2), 0)
            second(At(0, 2, NT - 1), 1)

        with nc.Block() as block:
            @block.sync
            def _(sp):
                def load(b, row):
                    sp.dma_start(mixT[:, b, :], mixed[bass.ds(row, P), :]).then_inc(ld[b], 16)
                    sp.dma_start(gate[:, b, :], proj[bass.ds(row, P), GATE:]).then_inc(ld[b], 16)

                def load_x(b, row):
                    sp.dma_start(xt[:, b, :], x[bass.ds(row, P), :]).then_inc(x_ld[b], 16)

                load(0, 0)
                sp.dma_start(bg[:], b_gate.broadcast_to([P, 2 * D])).then_inc(w_ld[3], 16)
                for i, (dst, src) in enumerate(((wa, w_oa), (wb, w_ob), (wo, w_out))):
                    sp.dma_start(dst[:], src.rearrange("(k p) c -> p k c", p=P)).then_inc(w_ld[i], 16)
                    if i == 1:
                        sp.dma_start(ident[:], ident_d).then_inc(w_ld[3], 16)
                        load(1, P)
                load_x(0, 0)
                load_x(1, P)

                def tile(n, b, more):
                    if more:
                        sp.wait_ge(merged_ready, n(1))
                        load(b, n(2) * P)
                    sp.wait_ge(res_ready, n(1 + 1))
                    sp.dma_start(x2[bass.ds(n(0) * P, P), :], res[:]).then_inc(res_stored, 16)
                    if more:
                        load_x(b, n(2) * P)

                with sp.Fori(0, NT // 2 - 1) as j:
                    for b in range(2):
                        tile(At(j, 2, b), b, True)
                for b in range(2):
                    tile(At(0, 2, NT - 2 + b), b, False)
                sp.wait_ge(res_stored, 16 * (NT + 1))

            @block.gpsimd
            def _(pool):
                pool.sem_inc(res_stored, 16)
                pool.wait_ge(w_ld[3], 32)
                with pool.Fori(0, NT // 2) as j:
                    for b in range(2):
                        pool.wait_ge(ld[b], j * 32 + 32)
                        nc.gpsimd.tensor_tensor(gate[:, b, :], gate[:, b, :], bg[:], ALU.add).then_inc(biased, 1)

            @block.scalar
            def _(act):
                act.sem_inc(mT_ready, 1)

                def sigmoid(n, b):
                    act.wait_ge(biased, n(1))
                    nc.scalar.activation(gate[:, b, :], gate[:, b, :], ACT.Sigmoid).then_inc(gated, 1)

                def spread(n, b):
                    act.wait_ge(m_transposed, n(1 + 1))
                    nc.scalar.copy(mT[:], tb[:]).then_inc(mT_ready, 1)

                order(act, sigmoid, spread)

            @block.vector
            def _(dve):
                link = Chain(dve, chain)
                dve.sem_inc(y_free, 1)
                dve.sem_inc(res_ready, 1)

                def gates(n, b):
                    dve.wait_ge(gated, n(1))
                    for h in range(2):
                        cols = slice(h * 512, h * 512 + 512)
                        for br in range(2):
                            dve.wait_ge(y_full, n.i * 8 + (n.base * 4 + 2 * h + br + 1))
                            last = nc.vector.tensor_tensor(part[:, br, cols], Y[:, br, cols],
                                                           gate[:, b, br * D + h * 512:br * D + h * 512 + 512], ALU.mult)
                        if h == 1:
                            last.then_inc(y_free, 1)
                            dve.wait_ge(y_free, n(1 + 1))
                        else:
                            link(last)
                            dve.wait_ge(m_transposed, n(1))
                        last = nc.vector.tensor_tensor(merged[:, cols], part[:, 0, cols], part[:, 1, cols], ALU.add)
                    last.then_inc(merged_ready, 1)
                    dve.wait_ge(merged_ready, n(1))

                def residual(n, b):
                    dve.wait_ge(res_stored, n(1) * 16)
                    dve.wait_ge(x_ld[b], n.i * 16 + 16 * (n.base // 2 + 1))
                    dve.wait_ge(z_full, n(1))
                    nc.vector.tensor_tensor(res[:], Z[:], xt[:, b, :], ALU.add).then_inc(res_ready, 1)

                order(dve, gates, residual, link)

            @block.tensor
            def _(pe):
                pe.sem_inc(m_transposed, 1)

                def branches(n, b):
                    pe.wait_ge(ld[b], n.i * 32 + 32 * (n.base // 2 + 1))
                    pe.wait_ge(y_free, n(1))
                    for h in range(2):
                        for br, w in enumerate((wa, wb)):
                            pe.wait_ge(w_ld[br], 16)
                            for k in range(KD):
                                last = nc.tensor.matmul(Y[:, br, h * 512:h * 512 + 512],
                                                        mixT[:, b, (br * KD + k) * P:(br * KD + k + 1) * P],
                                                        w[:, k, h * 512:h * 512 + 512], start=(k == 0), stop=(k == KD - 1))
                            last.then_inc(y_full, 1)

                def project(n, b):
                    pe.wait_ge(w_ld[2], 16)
                    pe.wait_ge(w_ld[3], 32)
                    pe.wait_ge(merged_ready, n(1))
                    pe.wait_ge(mT_ready, n(1))
                    for k in range(KD):
                        last = nc.tensor.transpose(tb[:, k * P:(k + 1) * P], merged[:, k * P:(k + 1) * P], ident[:])
                    last.then_inc(m_transposed, 1)
                    pe.wait_ge(mT_ready, n(2))
                    pe.wait_ge(res_ready, n(1))
                    for h in range(2):
                        for k in range(KD):
                            last = nc.tensor.matmul(Z[:, h * 512:h * 512 + 512], mT[:, k * P:(k + 1) * P],
                                                    wo[:, k, h * 512:h * 512 + 512], start=(k == 0), stop=(k == KD - 1))
                    last.then_inc(z_full, 1)

                order(pe, branches, project)


def phase_experts(nc, sems, x2, g_ffn, w_query, sub_keys, experts, g_final, ident_d, iota_d, out):
    with ExitStack() as ctx:
        m = Mem(nc, ctx, sems, "exp")
        RING = 8
        PAIR = 2
        STEPS = SLOTS // PAIR
        BACK = RING // PAIR
        ident = m.sb("ident", [P, P])
        iota = m.sb("iota", [P, TOPK])
        gffn, gfin = m.sb("gffn", [P, D]), m.sb("gfin", [P, D])
        wq = m.sb("wq", [P, KD, HEADS * 2 * P])
        keys = m.sb("keys", [P, 2 * HEADS, KEYS])
        eps = m.sb("eps", [P, 1])
        ring = m.sb("ring", [P, RING, 2 * D])
        xn, xr = m.sb("xn", [P, D]), m.sb("xr", [P, D])
        h_next, h_now = m.sb("h_next", [P, D]), m.sb("h_now", [P, D])
        hT = m.sb("hT", [P, D])
        junk = m.sb("junk", [P, 2, D])
        sqj = m.sb("sqj", [P, D])
        stat = m.sb("stat", [P, 6])
        qT = m.sb("qT", [P, 2, 2 * P])
        top = m.sb("top", [P, HEADS, 2, TOPK])
        topi = m.sb("topi", [P, HEADS, 2, TOPK], U32)
        topf = m.sb("topf", [P, HEADS, 2, TOPK])
        rest = m.sb("rest", [P, 2, KEYS])
        cand, crest = m.sb("cand", [P, TOPK * TOPK]), m.sb("crest", [P, TOPK * TOPK])
        best = m.sb("best", [P, HEADS, TOPK])
        pos = m.sb("pos", [P, TOPK], U32)
        posd = m.sb("posd", [P, 2, TOPK], U32)
        posf = m.sb("posf", [P, 2, TOPK])
        hit = m.sb("hit", [P, 2, TOPK, TOPK])
        sel = m.sb("sel", [P, 2, TOPK])
        idx_all = m.sb("idx_all", [P, NT, SLOTS], I32)
        idx = m.sb("idx", [P, 2, SLOTS], I32)
        soft, ssum = m.sb("soft", [P, HEADS, TOPK]), m.sb("ssum", [P, HEADS])
        g_next, g_now = m.sb("g_next", [P, SLOTS]), m.sb("g_now", [P, SLOTS])
        dot, ge, wgt = (m.sb(n, [P, SLOTS]) for n in ("dot", "ge", "wgt"))
        diag = m.sb("diag", [P, 2, PAIR, P])
        y, yo = m.sb("y", [P, D]), m.sb("yo", [P, D])
        tb = m.ps("tb", [P, D])
        qp, sc = m.ps("qp", [P, 2, 512]), m.ps("sc", [P, 2, 512])
        acc = m.ps("acc", [P, D])
        const_ld, eps_set = m.sem("const_ld"), m.sem("eps_set")
        w_ld = [m.sem(f"w_ld{i}") for i in range(4)]
        xn_ld, xr_ld = m.sem("xn_ld"), m.sem("xr_ld")
        root, h_ready, h_transposed, hT_ready = (m.sem(n) for n in ("root", "h_ready", "h_transposed", "hT_ready"))
        q_full, s_full = m.sem("q_full"), m.sem("s_full")
        q_ready = m.sem("q_ready")
        s_free = m.sem("s_free")
        best_ready, exp_ready, chosen = m.sem("best_ready"), m.sem("exp_ready"), m.sem("chosen")
        row_ld = [m.sem(f"row_ld{r}") for r in range(RING)]
        dotted, gelued, weighted, diag_ready = (m.sem(n) for n in ("dotted", "gelued", "weighted", "diag_ready"))
        used = m.sem("used")
        y_ready = m.sem("y_ready")
        root2, yo_ready = m.sem("root2"), m.sem("yo_ready")
        out_stored = m.sem("out_stored")
        idx_ready = m.sem("idx_ready")
        pool_passed, dve_passed = m.sem("pool_passed"), m.sem("dve_passed")
        act_chain, chain = m.sem("act_chain"), m.sem("chain")
        Q0, QS = 6, 6

        def head_at(step, lag):
            h, off = divmod(step - Q0 - lag, QS)
            return h if off == 0 and 0 <= h < HEADS else None

        def tiles(e, prologue, tile, link=None, per=0):
            prologue(At(0, 1, 0))
            tile(At(0, 1, 0), True, False)
            with e.Fori(0, NT - 2) as i:
                if link:
                    link.enter(i, per)
                tile(At(i, 1, 1), True, True)
                if link:
                    link.leave(NT - 2)
            tile(At(0, 1, NT - 1), False, True)

        def mul(n, k, c):
            return n.i * k + (n.base * k + c)

        with nc.Block() as block:
            @block.sync
            def _(sp):
                sp.dma_start(xn[:], x2[0:P, :]).then_inc(xn_ld, 16)
                for dst, src in ((ident[:], ident_d), (iota[:], iota_d.broadcast_to([P, TOPK])),
                                 (gffn[:], g_ffn.broadcast_to([P, D])), (gfin[:], g_final.broadcast_to([P, D])),
                                 (keys[:], sub_keys)):
                    sp.dma_start(dst, src).then_inc(const_ld, 16)
                wv = w_query.rearrange("(k p) c -> p k c", p=P)
                for i in range(4):
                    sp.dma_start(wq[:, :, i * 512:(i + 1) * 512], wv[:, :, i * 512:(i + 1) * 512]).then_inc(w_ld[i], 16)

                def tile(n, more, before):
                    if more:
                        sp.wait_ge(h_ready, n(1))
                        sp.dma_start(xn[:], x2[bass.ds(n(1) * P, P), :]).then_inc(xn_ld, 16)
                    sp.wait_ge(y_ready, n(1))
                    sp.dma_start(xr[:], x2[bass.ds(n(0) * P, P), :]).then_inc(xr_ld, 16)
                    if before:
                        store(n(-1), n(0))

                def store(t, count):
                    sp.wait_ge(yo_ready, count)
                    sp.dma_start(out[bass.ds(t * P, P), :], yo[:]).then_inc(out_stored, 16)

                tiles(sp, lambda n: None, tile)
                store(NT - 1, NT)
                sp.wait_ge(out_stored, 16 * (NT + 1))

            @block.gpsimd
            def _(pool):
                pool.sem_inc(out_stored, 16)
                with pool.Fori(0, NT // 2) as j:
                    for b in range(2):
                        n = At(j, 2, b)
                        pool.wait_ge(chosen, n(1))
                        nc.gpsimd.tensor_copy(idx[:, b, :], idx_all[:, bass.ds(n(0), 1), :].rearrange("p a s -> p (a s)")).then_inc(idx_ready, 1)
                        pool.wait_ge(idx_ready, n(1))
                        for s in range(SLOTS):
                            if s % PAIR == 0:
                                pool.wait_ge(used, j * (2 * STEPS) + (b * STEPS + s // PAIR + 1))
                                pool.sem_inc(pool_passed, 1)
                            nc.gpsimd.indirect_dma_start(
                                out=ring[:, s % RING, :], out_offset=None, in_=experts,
                                in_offset=bass.IndirectOffsetOnAxis(ap=idx[:, b, s:s + 1], axis=0)).then_inc(row_ld[s % RING], 16)

            @block.scalar
            def _(act):
                link = Chain(act, act_chain)

                def norm(n):
                    act.wait_ge(xn_ld, mul(n, 16, 16))
                    link(nc.scalar.activation(sqj[:], xn[:], ACT.Square, accum_out=stat[:, 0:1]))
                    nc.scalar.activation(stat[:, 1:2], stat[:, 0:1], ACT.Sqrt, bias=eps[:], scale=1.0 / D).then_inc(root, 1)

                def spread_h(n):
                    act.wait_ge(h_transposed, n(1))
                    nc.scalar.copy(hT[:], tb[:]).then_inc(hT_ready, 1)

                def spread_q(n, h):
                    act.wait_ge(q_full, mul(n, HEADS, h + 1))
                    nc.scalar.copy(qT[:, h % 2, :], qp[:, h % 2, 0:2 * P]).then_inc(q_ready, 1)

                def expo(n):
                    act.wait_ge(best_ready, n(1))
                    nc.scalar.activation(soft[:], soft[:], ACT.Exp).then_inc(exp_ready, 1)

                def first(n):
                    act.sem_inc(q_ready, 2)
                    act.wait_ge(eps_set, 1)
                    norm(n)
                    spread_h(n)
                    for h in range(HEADS):
                        spread_q(n, h)
                    expo(n)

                def tile(n, more, before):
                    nxt = At(n.i, 1, n.base + 1)
                    for g in range(STEPS + 1):
                        if g < STEPS:
                            act.wait_ge(dotted, mul(n, SLOTS, PAIR * (g + 1)))
                            c = slice(PAIR * g, PAIR * (g + 1))
                            nc.scalar.activation(ge[:, c], dot[:, c], ACT.Gelu).then_inc(gelued, 1)
                        if g >= 1:
                            act.wait_ge(weighted, mul(n, STEPS, g))
                            act.wait_ge(used, mul(n, STEPS, g - 2 + BACK))
                            for c in range(PAIR):
                                s = PAIR * (g - 1) + c
                                last = nc.scalar.activation(diag[:, (g - 1) % 2, c, :], ident[:], ACT.Copy, scale=wgt[:, s:s + 1])
                            last.then_inc(diag_ready, 1)
                        if more:
                            if g == 0:
                                norm(nxt)
                            if g == 5:
                                spread_h(nxt)
                            if (h := head_at(g, 2)) is not None:
                                spread_q(nxt, h)
                            if g == 59:
                                expo(nxt)
                        if before and g == 2:
                            norm_y(n(1))

                def norm_y(count):
                    act.wait_ge(y_ready, count)
                    link(nc.scalar.activation(sqj[:], y[:], ACT.Square, accum_out=stat[:, 3:4]))
                    nc.scalar.activation(stat[:, 4:5], stat[:, 3:4], ACT.Sqrt, bias=eps[:], scale=1.0 / D).then_inc(root2, 1)

                tiles(act, first, tile, link, 2)
                norm_y(NT + 1)

            @block.vector
            def _(dve):
                link = Chain(dve, chain)

                def norm(n):
                    dve.wait_ge(root, n(1))
                    link(nc.vector.reciprocal(stat[:, 2:3], stat[:, 1:2]))
                    nc.vector.scalar_tensor_tensor(h_next[:], xn[:], stat[:, 2:3], gffn[:], ALU.mult, ALU.mult).then_inc(h_ready, 1)

                def top8(vals, index, scores):
                    link(nc.vector.max(vals, scores))
                    dve.sem_inc(dve_passed, 1)
                    return nc.vector.max_index(index, vals, scores)

                def top16(vals, index, scores, left):
                    top8(vals[:, 0:8], index[:, 0:8], scores)
                    link(nc.vector.match_replace(left, vals[:, 0:8], scores, -3e38))
                    dve.sem_inc(dve_passed, 1)
                    link(top8(vals[:, 8:16], index[:, 8:16], left))

                def choose(n, h, part):
                    if part < 2:
                        if part == 0:
                            dve.wait_ge(s_full, mul(n, HEADS, h + 1))
                            dve.sem_inc(dve_passed, 1)
                        top16(top[:, h, part, :], topi[:, h, part, :], sc[:, h % 2, part * P:(part + 1) * P], rest[:, part, :])
                    elif part == 2:
                        dve.sem_inc(s_free, 1)
                        nc.vector.tensor_copy(topf[:, h, :, :], topi[:, h, :, :])
                        link(nc.vector.tensor_tensor(cand[:].rearrange("p (a b) -> p a b", a=TOPK),
                                                     top[:, h, 0, :].unsqueeze(2).to_broadcast([P, TOPK, TOPK]),
                                                     top[:, h, 1, :].unsqueeze(1).to_broadcast([P, TOPK, TOPK]), ALU.add))
                        dve.sem_inc(dve_passed, 1)
                        top16(best[:, h, :], pos[:], cand[:], crest[:])
                    else:
                        nc.vector.tensor_scalar(posd[:, 0, :], pos[:], 4, None, ALU.logical_shift_right)
                        link(nc.vector.tensor_scalar(posd[:, 1, :], pos[:], TOPK - 1, None, ALU.bitwise_and))
                        link(nc.vector.tensor_copy(posf[:], posd[:]))
                        for p in range(2):
                            last = nc.vector.tensor_tensor(hit[:, p, :, :], posf[:, p, :].unsqueeze(2).to_broadcast([P, TOPK, TOPK]),
                                                           iota[:].unsqueeze(1).to_broadcast([P, TOPK, TOPK]), ALU.is_equal)
                        link(last)
                        for p in range(2):
                            last = nc.vector.tensor_tensor(hit[:, p, :, :], hit[:, p, :, :],
                                                           topf[:, h, p, :].unsqueeze(1).to_broadcast([P, TOPK, TOPK]), ALU.mult)
                        link(last)
                        link(nc.vector.reduce_sum(sel[:], hit[:], AXX))
                        link(nc.vector.scalar_tensor_tensor(
                            idx_all[:, bass.ds(n(0), 1), h * TOPK:(h + 1) * TOPK].rearrange("p a s -> p (a s)"),
                            sel[:, 0, :], float(KEYS), sel[:, 1, :], ALU.mult, ALU.add))

                def soften(n):
                    dve.sem_inc(chosen, 1)
                    nc.vector.tensor_tensor(soft[:], best[:], best[:, :, 0:1].to_broadcast([P, HEADS, TOPK]),
                                            ALU.subtract).then_inc(best_ready, 1)

                def gates(n):
                    dve.wait_ge(exp_ready, n(1))
                    link(nc.vector.reduce_sum(ssum[:], soft[:], AXX))
                    link(nc.vector.reciprocal(ssum[:], ssum[:]))
                    link(nc.vector.tensor_tensor(g_next[:].rearrange("p (h c) -> p h c", c=TOPK), soft[:],
                                                 ssum[:].unsqueeze(2).to_broadcast([P, HEADS, TOPK]), ALU.mult))

                def first(n):
                    dve.sem_inc(used, BACK)
                    dve.sem_inc(s_free, 2)
                    dve.sem_inc(y_ready, 1)
                    nc.vector.memset(eps[:], EPS).then_inc(eps_set, 1)
                    dve.wait_ge(const_ld, 5 * 16)
                    norm(n)
                    for h in range(HEADS):
                        for part in range(4):
                            choose(n, h, part)
                    soften(n)
                    gates(n)

                def tile(n, more, before):
                    nxt = At(n.i, 1, n.base + 1)
                    nc.vector.tensor_copy(h_now[:], h_next[:])
                    link(nc.vector.tensor_copy(g_now[:], g_next[:]))
                    for g in range(STEPS + 1):
                        if g < STEPS:
                            for s in range(PAIR * g, PAIR * (g + 1)):
                                dve.wait_ge(row_ld[s % RING], mul(n, 16 * SLOTS // RING, 16 * (s // RING + 1)))
                                if s >= 2:
                                    dve.wait_ge(dotted, mul(n, SLOTS, s - 1))
                                nc.vector.tensor_tensor_reduce(
                                    out=junk[:, s % 2, :], in0=ring[:, s % RING, 0:D], in1=h_now[:], scale=1.0, scalar=0.0,
                                    op0=ALU.mult, op1=ALU.add, accum_out=dot[:, s:s + 1]).then_inc(dotted, 1)
                        if g >= 1:
                            dve.wait_ge(gelued, mul(n, STEPS, g))
                            c = slice(PAIR * (g - 1), PAIR * g)
                            nc.vector.tensor_tensor(wgt[:, c], ge[:, c], g_now[:, c], ALU.mult).then_inc(weighted, 1)
                        if more:
                            if g == 1:
                                norm(nxt)
                            for part in range(4):
                                if (h := head_at(g, 6 + part)) is not None:
                                    choose(nxt, h, part)
                            if g == 58:
                                soften(nxt)
                            if g == 61:
                                gates(nxt)
                        if before and g == 4:
                            norm_y(n(0), mul(n, 16, 0))
                    dve.wait_ge(xr_ld, mul(n, 16, 16))
                    dve.wait_ge(used, mul(n, STEPS, STEPS + BACK))
                    nc.vector.tensor_tensor(y[:], acc[:], xr[:], ALU.add).then_inc(y_ready, 1)

                def norm_y(count, stored):
                    dve.wait_ge(root2, count)
                    link(nc.vector.reciprocal(stat[:, 5:6], stat[:, 4:5]))
                    dve.wait_ge(out_stored, stored)
                    nc.vector.scalar_tensor_tensor(yo[:], y[:], stat[:, 5:6], gfin[:], ALU.mult, ALU.mult).then_inc(yo_ready, 1)
                    dve.wait_ge(yo_ready, count)

                tiles(dve, first, tile, link, 158)
                norm_y(NT, 16 * NT)

            @block.tensor
            def _(pe):
                def transpose_h(n):
                    pe.wait_ge(h_ready, n(1))
                    for k in range(KD):
                        last = nc.tensor.transpose(tb[:, k * P:(k + 1) * P], h_next[:, k * P:(k + 1) * P], ident[:])
                    last.then_inc(h_transposed, 1)

                def query(n, h, p):
                    if p == 0:
                        if h == 0:
                            pe.wait_ge(hT_ready, n(1))
                        pe.wait_ge(q_ready, mul(n, HEADS, h + 1))
                    for k in range(KD):
                        last = nc.tensor.matmul(qp[:, h % 2, p * P:(p + 1) * P], wq[:, k, (2 * h + p) * P:(2 * h + p + 1) * P],
                                                hT[:, k * P:(k + 1) * P], start=(k == 0), stop=(k == KD - 1))
                    if p == 1:
                        last.then_inc(q_full, 1)

                def scores(n, h):
                    pe.wait_ge(q_ready, mul(n, HEADS, h + 1 + 2))
                    pe.wait_ge(s_free, mul(n, HEADS, h + 1))
                    for p in range(2):
                        last = nc.tensor.matmul(sc[:, h % 2, p * P:(p + 1) * P], qT[:, h % 2, p * P:(p + 1) * P],
                                                keys[:, 2 * h + p, :], start=True, stop=True)
                    last.then_inc(s_full, 1)

                def first(n):
                    pe.wait_ge(const_ld, 5 * 16)
                    transpose_h(n)
                    for h in range(HEADS + 1):
                        if h < HEADS:
                            if h % 2 == 0:
                                pe.wait_ge(w_ld[h // 2], 16)
                            query(n, h, 0)
                            query(n, h, 1)
                        if h >= 1:
                            scores(n, h - 1)

                def tile(n, more, before):
                    nxt = At(n.i, 1, n.base + 1)
                    pe.wait_ge(y_ready, n(1))
                    for g in range(STEPS + 1):
                        if g >= 1:
                            pe.wait_ge(diag_ready, mul(n, STEPS, g))
                            for c in range(PAIR):
                                s = PAIR * (g - 1) + c
                                for half in range(2):
                                    last = nc.tensor.matmul(acc[:, half * 512:half * 512 + 512], diag[:, (g - 1) % 2, c, :],
                                                            ring[:, s % RING, D + half * 512:D + half * 512 + 512],
                                                            start=(s == 0), stop=(s == SLOTS - 1))
                            last.then_inc(used, 1)
                        if more:
                            if g == 4:
                                transpose_h(nxt)
                            for p in range(2):
                                if (h := head_at(g, p)) is not None:
                                    query(nxt, h, p)
                            if (h := head_at(g, 4)) is not None:
                                scores(nxt, h)

                tiles(pe, first, tile)


def build(nc, x, g_mix, w_all, b_gate, sink, q_norm_g, k_norm_g, w_oa, w_ob, w_out, g_ffn, w_query,
          sub_keys, experts, g_final, rope, masks, ident, iota, out):
    def scratch(name, shape):
        return nc.dram_tensor(name, shape, F32, kind="Internal").ap()

    proj = scratch("proj_dram", (TOK, COLS))
    mixed = scratch("mixed_dram", (TOK, 2 * D))
    x2 = scratch("x2_dram", (TOK, D))
    with ExitStack() as sems:
        phase_project(nc, sems, x, g_mix, w_all, ident, proj)
        phase_attend(nc, sems, proj, rope, masks, sink, q_norm_g, k_norm_g, ident, mixed)
        phase_merge(nc, sems, x, mixed, proj, b_gate, w_oa, w_ob, w_out, ident, x2)
        phase_experts(nc, sems, x2, g_ffn, w_query, sub_keys, experts, g_final, ident, iota, out)


def kernel(x_prompt, x_sample, g_mix, w_in, w_gate, b_gate, sink, q_norm_g, k_norm_g, w_oa, w_ob, w_out,
           g_ffn, w_query, sub_keys, expert_u, expert_v, g_final):
    import numpy as np
    import concourse.bacc as bacc
    from concourse.bass_utils import run_bass_kernel_spmd

    def rope_tables(pos, dim):
        inv = (np.float64(10000.0) ** (-np.arange(0, dim, 2) / dim)).astype(np.float32)
        ang = pos.astype(np.float32)[:, None] * inv[None, :]
        return np.concatenate([np.cos(ang)] * 2, -1), np.concatenate([-np.sin(ang), np.sin(ang)], -1)

    pos = np.concatenate([np.arange(SAMPLE), np.arange(PROMPT)])
    cos_a, sin_a = rope_tables(pos, AD)
    cos_r, sin_r = rope_tables(pos // 64, BD // 2)
    cos_c, sin_c = rope_tables(pos % 64, BD // 2)
    rope = np.concatenate([cos_a, sin_a, cos_r, cos_c, sin_r, sin_c], -1).astype(np.float32)
    masks = np.zeros((NT, P, 3 * P), np.float32)
    q, k = np.arange(P)[:, None], np.arange(3 * P)[None, :] - P
    for t in range(NT):
        first, last = t in (0, ST), t in (ST - 1, NT - 1)
        ok = (np.abs(q - k) <= P) & ((k >= 0) | (not first)) & ((k < P) | (not last))
        masks[t] = np.where(ok, 0.0, NEG / A_SCALE)
    masks = masks.reshape(TOK, 3 * P)
    arrays = {
        "x": np.concatenate([x_sample[0], x_prompt[0]], 0),
        "g_mix": g_mix, "w_all": np.concatenate([w_in[0], w_gate[0]], 1), "b_gate": b_gate, "sink": sink,
        "q_norm_g": q_norm_g, "k_norm_g": k_norm_g, "w_oa": w_oa[0], "w_ob": w_ob[0], "w_out": w_out[0],
        "g_ffn": g_ffn, "w_query": w_query[0],
        "sub_keys": np.asarray(sub_keys)[0].reshape(2 * HEADS, KEYS, P).transpose(2, 0, 1),
        "experts": np.concatenate([expert_u[0], expert_v[0]], 1),
        "g_final": np.asarray(g_final)[None], "rope": rope, "masks": masks, "ident": np.eye(P, dtype=np.float32),
        "iota": np.arange(TOPK, dtype=np.float32)[None],
    }
    nc = bacc.Bacc("TRN2", target_bir_lowering=False, num_devices=1)
    ins, args = {}, []
    for name, a in arrays.items():
        a = np.ascontiguousarray(a)
        ins[f"in_{name}_dram"] = a
        args.append(nc.dram_tensor(f"in_{name}_dram", a.shape, F32, kind="ExternalInput").ap())
    args.append(nc.dram_tensor("out_0_dram", (TOK, D), F32, kind="ExternalOutput").ap())
    build(nc, *args)
    got = run_bass_kernel_spmd(nc, [ins], core_ids=[0]).results[0]["out_0_dram"]
    return got[SAMPLE:].reshape(1, PROMPT, D), got[:SAMPLE].reshape(1, SAMPLE, D)
```

```python
import concourse.bass as bass
from concourse import mybir
from contextlib import ExitStack

F32 = mybir.dt.float32
F32R = mybir.dt.float32r
I32 = mybir.dt.int32
U32 = mybir.dt.uint32
ALU = mybir.AluOpType
ACT = mybir.ActivationFunctionType
AXX = mybir.AxisListType.X

P = 128
D = 1024
KD = D // P
SAMPLE, PROMPT = 256, 1024
TOK = SAMPLE + PROMPT
NT = TOK // P
ST = SAMPLE // P
PT_ = PROMPT // P
AH, AKV, AD = 16, 4, 64
BH, BKV, BD = 8, 2, 128
A_SCALE = AD ** -0.5
B_SCALE = BD ** -0.5
QA, KA, VA, QB, KB, VB, GATE = 0, 1024, 1280, 1536, 2560, 2816, 3072
COLS = GATE + 2 * D
CW = 512
EPS = 1e-6
NEG = -1e30
ROPE_W = 2 * AD + 2 * BD
HEADS, KEYS, TOPK = 8, 128, 16
SLOTS = HEADS * TOPK


class Chain:

    def __init__(self, eng, sem):
        self.eng, self.sem = eng, sem
        self.base, self.i, self.per, self.n = 0, 0, 0, 0

    def __call__(self, ins):
        ins.then_inc(self.sem, 1)
        self.n += 1
        self.eng.wait_ge(self.sem, self.i * self.per + (self.base + self.n))

    def enter(self, i, per):
        self.base, self.n = self.base + self.n, 0
        self.i, self.per = i, per

    def leave(self, trips):
        assert self.n == self.per, (self.n, self.per)
        self.base += trips * self.per
        self.i, self.per, self.n = 0, 0, 0


class At:

    def __init__(self, i, per, base=0):
        self.i, self.per, self.base = i, per, base

    def __call__(self, local):
        return self.i * self.per + (self.base + local)


class Mem:

    def __init__(self, nc, ctx, sems, tag):
        self.nc, self.ctx, self.sems, self.tag = nc, ctx, sems, tag

    def sb(self, name, shape, dt=F32):
        return self.ctx.enter_context(self.nc.sbuf_tensor(f"{self.tag}_{name}", shape, dt))

    def ps(self, name, shape, dt=F32):
        return self.ctx.enter_context(self.nc.psum_tensor(f"{self.tag}_{name}", shape, dt))

    def sem(self, name):
        handle = self.nc.alloc_semaphore(name=f"{self.tag}_{name}")
        self.sems.append(handle)
        return handle


def release(nc, sems):
    nc.all_engine_barrier()
    nc.clear_and_free_semaphores(sems)
    nc.all_engine_barrier()
    sems.clear()


class Background:

    RING = 4

    def __init__(self, nc, m, kept, experts, g_final):
        self.nc, self.kept, self.experts, self.g_final = nc, kept, experts, g_final
        self.ring = m.sb("ring", [P, self.RING, 2 * D])
        self.h, self.acc = m.sb("h", [P, D]), m.sb("acc", [P, D])
        self.junk = m.sb("junk", [P, 2, D], mybir.dt.bfloat16)
        self.idx, self.g = m.sb("idx", [P, SLOTS], I32), m.sb("g", [P, SLOTS])
        self.window = m.sb("window", [P, 2, 8], I32)
        self.dot, self.ge = m.sb("dot", [P, 2, 2]), m.sb("ge", [P, 2, 2])
        self.w = m.sb("w", [P, 2])
        self.stat = m.sb("stat", [P, 3])
        self.eps = m.sb("eps", [P, 1])
        self.ld, self.eps_set = m.sem("ld"), m.sem("eps_set")
        self.row_ld = [m.sem(f"row_ld{r}") for r in range(self.RING)]
        self.window_set, self.passed = m.sem("window_set"), m.sem("passed")
        self.dotted, self.gelued = m.sem("dotted"), m.sem("gelued")
        self.used = m.sem("used")
        self.fin_ld, self.summed, self.root = m.sem("fin_ld"), m.sem("summed"), m.sem("root")
        self.y_ready, self.stored = m.sem("y_ready"), m.sem("stored")

    def load(self, sp, tile):
        h, idx, g = self.kept
        for dst, src in ((self.h[:], h), (self.idx[:], idx), (self.g[:], g)):
            sp.dma_start(dst, src[tile * P:(tile + 1) * P, :]).then_inc(self.ld, 16)

    def load_last(self, sp, tile, x2, place):
        self.place = place
        sp.dma_start(place[:, 0, :], x2[tile * P:(tile + 1) * P, :]).then_inc(self.fin_ld, 16)
        sp.dma_start(place[:, 1, :], self.g_final.broadcast_to([P, D])).then_inc(self.fin_ld, 16)

    def store(self, sp, tile, out):
        sp.wait_ge(self.y_ready, tile + 1)
        sp.dma_start(out[tile * P:(tile + 1) * P, :], self.place[:, 3, :]).then_inc(self.stored, 16)
        sp.wait_ge(self.stored, 16 * (tile + 1))

    def gather(self, pool, tile, at, count, column):
        for k in range(count):
            if k % 2 == 0:
                pool.wait_ge(self.used, at.i * (at.per // 2) + ((at.base + k) // 2 + 1))
                pool.sem_inc(self.passed, 1)
            self.nc.gpsimd.indirect_dma_start(
                out=self.ring[:, k % self.RING, :], out_offset=None, in_=self.experts,
                in_offset=bass.IndirectOffsetOnAxis(ap=column(k), axis=0)).then_inc(self.row_ld[k % self.RING], 16)

    def gather_window(self, pool, tile, b, at, windows, count=8):
        cols = bass.ds(at(0) - tile * SLOTS, count)
        self.nc.gpsimd.tensor_copy(self.window[:, b, 0:count], self.idx[:, cols]).then_inc(self.window_set, 1)
        pool.wait_ge(self.window_set, windows(1))
        self.gather(pool, tile, at, count, lambda k: self.window[:, b, k:k + 1])

    def start(self, dve, link, tile):
        if tile == 0:
            dve.sem_inc(self.used, 2)
            self.nc.vector.memset(self.eps[:], EPS).then_inc(self.eps_set, 1)
        link(self.nc.vector.memset(self.acc[:], 0.0))
        dve.wait_ge(self.ld, 48 * (tile + 1))

    def dot_of(self, dve, at, k, c):
        if c == 0 and at.base + k:
            dve.wait_ge(self.dotted, at(k))
        place = (k + c) % self.RING
        dve.wait_ge(self.row_ld[place], at.i * (at.per * 4) + 16 * ((at.base + k + c) // self.RING + 1))
        self.nc.vector.tensor_tensor_reduce(out=self.junk[:, c, :], in0=self.ring[:, place, 0:D], in1=self.h[:],
                                            scale=1.0, scalar=0.0, op0=ALU.mult, op1=ALU.add,
                                            accum_out=self.dot[:, (k // 2) % 2, c:c + 1]).then_inc(self.dotted, 1)

    def add_of(self, dve, link, tile, at, k, c):
        nc, pair = self.nc, (k // 2) % 2
        hook = at.i * (at.per // 2) + ((at.base + k) // 2 + 1)
        if c == 0:
            dve.wait_ge(self.gelued, hook)
            link(nc.vector.tensor_tensor(self.w[:], self.ge[:, pair, :], self.g[:, bass.ds(at(k - tile * SLOTS), 2)], ALU.mult))
        last = nc.vector.scalar_tensor_tensor(self.acc[:], self.ring[:, (k + c) % self.RING, D:], self.w[:, c:c + 1],
                                              self.acc[:], ALU.mult, ALU.add)
        if c == 0:
            link(last)
        else:
            last.then_inc(self.used, 1)
            dve.wait_ge(self.used, hook + 2)

    def dots(self, dve, at, k):
        for c in range(2):
            self.dot_of(dve, at, k, c)

    def add(self, dve, link, tile, at, k):
        for c in range(2):
            self.add_of(dve, link, tile, at, k, c)

    def finish(self, dve, link, tile):
        nc, place, stat = self.nc, self.place, self.stat
        dve.wait_ge(self.fin_ld, 32 * (tile + 1))
        link(nc.vector.tensor_tensor(place[:, 2, :], self.acc[:], place[:, 0, :], ALU.add))
        nc.vector.tensor_tensor_reduce(out=place[:, 3, :], in0=place[:, 2, :], in1=place[:, 2, :], scale=1.0,
                                       scalar=0.0, op0=ALU.mult, op1=ALU.add, accum_out=stat[:, 0:1]).then_inc(self.summed, 1)
        dve.wait_ge(self.root, tile + 1)
        link(nc.vector.reciprocal(stat[:, 2:3], stat[:, 1:2]))
        nc.vector.scalar_tensor_tensor(place[:, 3, :], place[:, 2, :], stat[:, 2:3], place[:, 1, :],
                                       ALU.mult, ALU.mult).then_inc(self.y_ready, 1)

    def gelu(self, act, at, k):
        act.wait_ge(self.dotted, at(k + 2))
        pair = (k // 2) % 2
        self.nc.scalar.activation(self.ge[:, pair, :], self.dot[:, pair, :], ACT.Gelu).then_inc(self.gelued, 1)

    def gelu4(self, act, at, k):
        act.wait_ge(self.dotted, at(k + 4))
        self.nc.scalar.activation(self.ge[:], self.dot[:], ACT.Gelu).then_inc(self.gelued, 2)

    def square_root(self, act, tile):
        act.wait_ge(self.eps_set, 1)
        act.wait_ge(self.summed, tile + 1)
        self.nc.scalar.activation(self.stat[:, 1:2], self.stat[:, 0:1], ACT.Sqrt, bias=self.eps[:],
                                  scale=1.0 / D).then_inc(self.root, 1)


def phase_project(nc, sems, tag, nt, x, g_mix, w_all, ident_d, proj, bg=None, x2=None, out=None):
    with ExitStack() as ctx:
        m = Mem(nc, ctx, sems, tag)
        hT_hi, hT_lo = m.sb("hT_hi", [P, KD, nt * P], F32R), m.sb("hT_lo", [P, KD, nt * P], F32R)
        norm_ctx = ExitStack()
        mn = Mem(nc, norm_ctx, sems, tag)
        WB = 2 if nt == 2 else 1
        w = m.sb("w", [P, WB, KD, CW])
        ident = mn.sb("ident", [P, P])
        grow = mn.sb("grow", [P, D])
        xt = mn.sb("xt", [P, 2, D])
        sq = mn.sb("sq", [P, 2, D], mybir.dt.bfloat16)
        ht = mn.sb("ht", [P, 2, D])
        ss, rt, rs = (mn.sb(n, [P, 2]) for n in ("ss", "rt", "rs"))
        eps = mn.sb("eps", [P, 1])
        tp = m.ps("tp", [P, 2, D])
        acc = m.ps("acc", [P, 4, CW])
        const_ld, eps_set = m.sem("const_ld"), m.sem("eps_set")
        x_ld = [m.sem(f"x_ld{b}") for b in range(2)]
        sum_ready, root_ready, h_ready = m.sem("sum_ready"), m.sem("root_ready"), m.sem("h_ready")
        h_transposed = m.sem("h_transposed")
        hi_ready = m.sem("hi_ready")
        lo_ready = m.sem("lo_ready")
        w_ld = [m.sem(f"w_ld{b}") for b in range(WB)]
        w_hi_ready, w_lo_ready = m.sem("w_hi_ready"), m.sem("w_lo_ready")
        mm_tile = m.sem("mm_tile")
        staged = [m.sem("staged_act"), m.sem("staged_dve")]
        stored = [m.sem(f"stored{s}") for s in range(4)]
        dve_chain = m.sem("dve_chain")
        wv = w_all.rearrange("(k p) c -> p k c", p=P)
        CHUNKS = COLS // CW

        BODY, TAIL = 24, 16
        assert (CHUNKS // 2 - 1) * BODY + 2 * TAIL == SLOTS

        def hooks(t, slots):
            if slots == BODY:
                return {0: [0], 1: [1], 2: [2], 4: [3], 5: [4], 6: [5]}.get(t, [])
            return [t] if slots == TAIL else []

        with nc.Block() as block:
            @block.sync
            def _(sp):
                for b in range(2):
                    sp.dma_start(xt[:, b, :], x[b * P:(b + 1) * P, :]).then_inc(x_ld[b], 16)
                sp.dma_start(grow[:], g_mix.broadcast_to([P, D])).then_inc(const_ld, 16)
                sp.dma_start(ident[:], ident_d).then_inc(const_ld, 16)
                for c in range(WB):
                    sp.dma_start(w[:, c, :, :], wv[:, :, c * CW:(c + 1) * CW]).then_inc(w_ld[c], 16)
                if nt > 2:
                    with sp.Fori(0, nt // 2 - 1) as j:
                        for b in range(2):
                            sp.wait_ge(h_ready, j * 2 + (b + 1))
                            sp.dma_start(xt[:, b, :], x[bass.ds(j * 2 * P + (b + 2) * P, P), :]).then_inc(x_ld[b], 16)

            @block.scalar
            def _(act):
                act.wait_ge(eps_set, 1)
                with act.Fori(0, nt // 2) as j:
                    for b in range(2):
                        act.wait_ge(sum_ready, j * 2 + (b + 1))
                        nc.scalar.activation(rt[:, b:b + 1], ss[:, b:b + 1], ACT.Sqrt, bias=eps[:],
                                             scale=1.0 / D).then_inc(root_ready, 1)
                    for b in range(2):
                        act.wait_ge(h_transposed, j * 2 + (b + 1 + 2))
                        nc.scalar.copy(hT_hi[:, :, bass.ds(j * 2 * P + b * P, P)],
                                       tp[:, b, :].rearrange("p (k c) -> p k c", c=P)).then_inc(hi_ready, 1)

            @block.vector
            def _(dve):
                dve.sem_inc(lo_ready, 2)
                nc.vector.memset(eps[:], EPS).then_inc(eps_set, 1)
                link = Chain(dve, dve_chain)

                def rest(b, j):
                    dve.wait_ge(hi_ready, j * 2 + (b + 1))
                    cols = bass.ds(j * 2 * P + b * P, P)
                    nc.vector.tensor_tensor(hT_lo[:, :, cols], tp[:, b, :].rearrange("p (k c) -> p k c", c=P),
                                            hT_hi[:, :, cols].bitcast(F32), ALU.subtract).then_inc(lo_ready, 1)

                def square(b, j):
                    dve.wait_ge(x_ld[b], j * 16 + 16)
                    nc.vector.tensor_tensor_reduce(out=sq[:, b, :], in0=xt[:, b, :], in1=xt[:, b, :], scale=1.0, scalar=0.0,
                                                   op0=ALU.mult, op1=ALU.add, accum_out=ss[:, b:b + 1]).then_inc(sum_ready, 1)

                def norm(b, j):
                    dve.wait_ge(root_ready, j * 2 + (b + 1))
                    link(nc.vector.reciprocal(rs[:, b:b + 1], rt[:, b:b + 1]))
                    dve.wait_ge(h_transposed, j * 2 + (b + 1))
                    nc.vector.scalar_tensor_tensor(ht[:, b, :], xt[:, b, :], rs[:, b:b + 1], grow[:],
                                                   ALU.mult, ALU.mult).then_inc(h_ready, 1)

                dve.wait_ge(const_ld, 32)
                with dve.Fori(0, nt // 2) as j:
                    link.enter(j, 2)
                    square(0, j)
                    square(1, j)
                    norm(0, j)
                    norm(1, j)
                    rest(0, j)
                    rest(1, j)
                    link.leave(nt // 2)

            @block.tensor
            def _(pe):
                pe.sem_inc(h_transposed, 2)
                pe.wait_ge(const_ld, 32)
                with pe.Fori(0, nt // 2) as j:
                    for b in range(2):
                        pe.wait_ge(h_ready, j * 2 + (b + 1))
                        pe.wait_ge(lo_ready, j * 2 + (b + 1))
                        for k in range(KD):
                            last = nc.tensor.transpose(tp[:, b, k * P:(k + 1) * P], ht[:, b, k * P:(k + 1) * P],
                                                       ident[:])
                        last.then_inc(h_transposed, 1)

        norm_ctx.close()
        w_hi, w_lo = m.sb("w_hi", [P, 2, KD, CW], F32R), m.sb("w_lo", [P, 2, KD, CW], F32R)
        stage = m.sb("stage", [P, 4, CW])
        with nc.Block() as block:
            @block.sync
            def _(sp):
                if bg:
                    bg.load(sp, 0)

                def chunk(c, b, more):
                    if more:
                        sp.wait_ge(w_lo_ready, c(1))
                        sp.dma_start(w[:, b % WB, :, :], wv[:, :, bass.ds(c(WB) * CW, CW)]).then_inc(w_ld[b % WB], 16)
                    for t in range(nt):
                        u = b * nt + t
                        sp.wait_ge(staged[u % 2], c.i * nt + (c.base * nt // 2 + t // 2 + 1 + 2))
                        sp.dma_start(proj[t * P:(t + 1) * P, bass.ds(c(0) * CW, CW)],
                                     stage[:, u % 4, :]).then_inc(stored[u % 4], 16)

                with sp.Fori(0, CHUNKS // 2 - 1) as j:
                    for b in range(2):
                        chunk(At(j, 2, b), b, True)
                chunk(At(0, 2, CHUNKS - 2), 0, WB == 1)
                chunk(At(0, 2, CHUNKS - 1), 1, False)
                if bg:
                    sp.wait_ge(w_lo_ready, CHUNKS)
                    bg.load_last(sp, 0, x2, w[:, 0, :, :].rearrange("p (a k) c -> p a (k c)", k=KD // 4))
                    bg.store(sp, 0, out)
                for s in range(4):
                    sp.wait_ge(stored[s], 16 * (CHUNKS * nt // 4 + 1))

            @block.scalar
            def _(act):
                act.sem_inc(staged[0], 2)

                def split(b, c):
                    act.wait_ge(w_ld[b % WB], c(1) * 16 if WB == 1 else c.i * 16 + (c.base // 2 + 1) * 16)
                    nc.scalar.copy(w_hi[:, b, :, :], w[:, b % WB, :, :]).then_inc(w_hi_ready, 1)

                def chunk(c, b, more, slots):
                    for t in range(nt):
                        u = b * nt + t
                        if u % 2 == 0:
                            act.wait_ge(mm_tile, c.i * 2 * nt + (c.base * nt + t + 1))
                            act.wait_ge(stored[u % 4], c.i * (16 * nt // 2) + (c.base // 2 * (16 * nt // 2) + 16 * (u // 4 + 1)))
                            nc.scalar.copy(stage[:, u % 4, :], acc[:, u % 4, :]).then_inc(staged[0], 1)
                        for i in hooks(t, slots.per if slots else 0):
                            bg.gelu(act, slots, 2 * i)
                        if WB == 1 and t == 1 and more:
                            split(1 - b, At(c.i, 2, c.base + 1))
                    if WB == 2 and c.base < CHUNKS - 2:
                        act.wait_ge(mm_tile, c.i * 2 * nt + (c.base + 1) * nt)
                        split(b, At(c.i, 2, c.base + 2))

                for c in range(WB):
                    split(c, At(0, 2, c))
                with act.Fori(0, CHUNKS // 2 - 1) as j:
                    for b in range(2):
                        chunk(At(j, 2, b), b, True, At(j, BODY, b * BODY // 2) if bg else None)
                for b in range(2):
                    chunk(At(0, 2, CHUNKS - 2 + b), b, not b, At(0, TAIL, (CHUNKS // 2 - 1) * BODY + b * TAIL) if bg else None)
                if bg:
                    bg.square_root(act, 0)

            @block.vector
            def _(dve):
                link = Chain(dve, m.sem("links"))
                dve.sem_inc(staged[1], 2)
                for s in range(4):
                    dve.sem_inc(stored[s], 16)

                def split(b, c):
                    dve.wait_ge(w_hi_ready, c(1))
                    nc.vector.tensor_tensor(w_lo[:, b, :, :], w[:, b % WB, :, :], w_hi[:, b, :, :].bitcast(F32),
                                            ALU.subtract).then_inc(w_lo_ready, 1)

                def chunk(c, b, more, slots):
                    for t in range(nt):
                        u = b * nt + t
                        if u % 2 == 1:
                            dve.wait_ge(mm_tile, c.i * 2 * nt + (c.base * nt + t + 1))
                            dve.wait_ge(stored[u % 4], c.i * (16 * nt // 2) + (c.base // 2 * (16 * nt // 2) + 16 * (u // 4 + 1)))
                            nc.vector.tensor_copy(stage[:, u % 4, :], acc[:, u % 4, :]).then_inc(staged[1], 1)
                        for i in hooks(t, slots.per if slots else 0):
                            bg.dots(dve, slots, 2 * i)
                            bg.add(dve, link, 0, slots, 2 * i)
                        if WB == 1 and t == 1 and more:
                            split(1 - b, At(c.i, 2, c.base + 1))
                    if WB == 2 and c.base < CHUNKS - 2:
                        split(b, At(c.i, 2, c.base + 2))

                for c in range(WB):
                    split(c, At(0, 2, c))
                if bg:
                    bg.start(dve, link, 0)
                with dve.Fori(0, CHUNKS // 2 - 1) as j:
                    link.enter(j, BODY if bg else 0)
                    for b in range(2):
                        chunk(At(j, 2, b), b, True, At(j, BODY, b * BODY // 2) if bg else None)
                    link.leave(CHUNKS // 2 - 1)
                for b in range(2):
                    chunk(At(0, 2, CHUNKS - 2 + b), b, not b, At(0, TAIL, (CHUNKS // 2 - 1) * BODY + b * TAIL) if bg else None)
                if bg:
                    bg.finish(dve, link, 0)

            if bg:
                @block.gpsimd
                def _(pool):
                    pool.wait_ge(bg.ld, 48)
                    bg.gather(pool, 0, At(0, SLOTS, 0), SLOTS, lambda k: bg.idx[:, k:k + 1])

            @block.tensor
            def _(pe):
                with pe.Fori(0, CHUNKS // 2) as j:
                    for b in range(2):
                        pe.wait_ge(w_lo_ready, j * 2 + (b + 1))
                        for t in range(nt):
                            u = b * nt + t
                            pe.wait_ge(staged[u % 2], j * nt + (u // 2 + 1))
                            for k in range(KD):
                                cols = slice(t * P, (t + 1) * P)
                                for n, (h, v) in enumerate(((hT_hi, w_hi), (hT_hi, w_lo), (hT_lo, w_hi))):
                                    last = nc.tensor.matmul(acc[:, u % 4, :], h[:, k, cols], v[:, b, k, :],
                                                            start=(k == 0 and n == 0), stop=(k == KD - 1 and n == 2))
                            last.then_inc(mm_tile, 1)


def rope_steps(e, link, out, x, tmp, cos, sin, heads, sections):
    width = 64 * sections
    full = lambda ap: ap.rearrange("p (h c) -> p h c", c=width)
    e.tensor_tensor(full(out), full(x), cos.unsqueeze(1).to_broadcast([P, heads, width]), ALU.mult)
    for half in range(2):
        if sections == 1:
            cut = lambda ap, t: ap.rearrange("p (h t c) -> p h t c", t=2, c=32)[:, :, t, :]
            s = sin[:, half * 32:half * 32 + 32].unsqueeze(1).to_broadcast([P, heads, 32])
        else:
            cut = lambda ap, t: ap.rearrange("p (h s t c) -> p h s t c", s=sections, t=2, c=32)[:, :, :, t, :]
            s = sin.rearrange("p (s t c) -> p s t c", t=2, c=32)[:, :, half, :].unsqueeze(1).to_broadcast(
                [P, heads, sections, 32])
        last = e.tensor_tensor(cut(tmp, half), cut(x, 1 - half), s, ALU.mult)
    link(last)
    return e.tensor_tensor(out, out, tmp, ALU.add)


def phase_attend(nc, sems, tag, nt, proj, rope, masks, sink, q_norm_g, k_norm_g, ident_d, mixed, bg=None):
    with ExitStack() as ctx:
        m = Mem(nc, ctx, sems, tag)
        BQK = 1280
        NB = BQK // BD
        ident = m.sb("ident", [P, P])
        sinks = m.sb("sinks", [P, AH])
        qg, kg = m.sb("qg", [P, BD]), m.sb("kg", [P, BD])
        eps = m.sb("eps", [P, 1])
        kTA = m.sb("kTA", [P, AKV * 2, (nt + 2) * P])
        kTB = m.sb("kTB", [P, BKV, nt * P])
        vA = m.sb("vA", [P, nt + 2, AKV * AD])
        vB = m.sb("vB", [P, nt, BKV * BD])
        rB = m.sb("rB", [P, nt, NB])
        const_ld, v_ld = m.sem("const_ld"), m.sem("v_ld")
        eps_set, pads_set = m.sem("eps_set"), m.sem("pads_set")
        with ExitStack() as kctx:
            mk = Mem(nc, kctx, sems, tag + "_key")
            raw = mk.sb("raw", [P, 2, BQK + 256])
            tab = mk.sb("tab", [P, 2, ROPE_W])
            sq = mk.sb("sq", [P, 2, BQK])
            ss, rt = mk.sb("ss", [P, 2, NB]), mk.sb("rt", [P, 2, NB])
            kn = mk.sb("kn", [P, 256])
            kr = mk.sb("kr", [P, 2, AKV * 2 * P + 256])
            ka = mk.sb("ka", [P, 256])
            KRA = AKV * 2 * P
            tmp = mk.sb("tmp", [P, 256])
            tpA, tpB = mk.ps("tpA", [P, 2, AKV * 2 * P]), mk.ps("tpB", [P, 2, 512])
            ld = [mk.sem(f"ld{b}") for b in range(2)]
            sq_ready, ss_ready, rt_ready, kr_ready = (mk.sem(n) for n in ("sq_ready", "ss_ready", "rt_ready", "kr_ready"))
            k_transposed = mk.sem("k_transposed")
            k_copied = mk.sem("k_copied")
            chain = mk.sem("chain")
            with nc.Block() as block:
                @block.sync
                def _(sp):
                    for dst, src in ((ident[:], ident_d), (sinks[:], sink.broadcast_to([P, AH])),
                                     (qg[:], q_norm_g.broadcast_to([P, BD])), (kg[:], k_norm_g.broadcast_to([P, BD]))):
                        sp.dma_start(dst, src).then_inc(const_ld, 16)

                    def load(b, row):
                        sp.dma_start(raw[:, b, 0:BQK], proj[bass.ds(row, P), QB:VB]).then_inc(ld[b], 16)
                        sp.dma_start(raw[:, b, BQK:], proj[bass.ds(row, P), KA:VA]).then_inc(ld[b], 16)
                        sp.dma_start(tab[:, b, :], rope[bass.ds(row, P), :]).then_inc(ld[b], 16)

                    load(0, 0)
                    load(1, P)
                    sp.dma_start(vA[:, 1:nt + 1, :], proj[:, VA:QB].rearrange("(t p) c -> p t c", p=P)).then_inc(v_ld, 16)
                    sp.dma_start(vB[:], proj[:, VB:GATE].rearrange("(t p) c -> p t c", p=P)).then_inc(v_ld, 16)
                    if nt > 2:
                        with sp.Fori(0, nt // 2 - 1) as j:
                            for b in range(2):
                                sp.wait_ge(kr_ready, j * 2 + (b + 1))
                                load(b, j * 2 * P + (b + 2) * P)
                    sp.wait_ge(v_ld, 32)

                @block.gpsimd
                def _(pool):
                    nc.gpsimd.memset(kTA[:, :, 0:P], 0.0)
                    nc.gpsimd.memset(kTA[:, :, (nt + 1) * P:], 0.0)
                    nc.gpsimd.memset(vA[:, 0, :], 0.0)
                    nc.gpsimd.memset(vA[:, nt + 1, :], 0.0).then_inc(pads_set, 1)
                    with pool.Fori(0, nt // 2) as j:
                        for b in range(2):
                            pool.wait_ge(ld[b], j * 48 + 48)
                            pool.wait_ge(ss_ready, j * 2 + (b + 1))
                            nc.gpsimd.tensor_tensor(sq[:, b, :], raw[:, b, 0:BQK], raw[:, b, 0:BQK],
                                                    ALU.mult).then_inc(sq_ready, 1)

                @block.scalar
                def _(act):
                    act.sem_inc(k_copied, 4)
                    act.wait_ge(eps_set, 1)
                    with act.Fori(0, nt // 2) as j:
                        for b in range(2):
                            act.wait_ge(ss_ready, j * 2 + (b + 1 + 2))
                            nc.scalar.activation(rt[:, b, :], ss[:, b, :], ACT.Sqrt, bias=eps[:],
                                                 scale=1.0 / BD).then_inc(rt_ready, 1)
                            act.wait_ge(k_transposed, j * 2 + (b + 1 + 2))
                            nc.scalar.copy(kTA[:, :, bass.ds(j * 2 * P + (b + 1) * P, P)],
                                           tpA[:, b, :].rearrange("p (h c) -> p h c", c=P)).then_inc(k_copied, 1)
                            nc.scalar.copy(kTB[:, :, bass.ds(j * 2 * P + b * P, P)],
                                           tpB[:, b, 0:256].rearrange("p (h c) -> p h c", c=P)).then_inc(k_copied, 1)

                @block.vector
                def _(dve):
                    link = Chain(dve, chain)
                    dve.sem_inc(ss_ready, 2)
                    nc.vector.memset(eps[:], EPS).then_inc(eps_set, 1)
                    link(nc.vector.memset(kr[:], 0.0))
                    dve.wait_ge(const_ld, 64)
                    with dve.Fori(0, nt // 2) as j:
                        link.enter(j, 10)
                        for b in range(2):
                            dve.wait_ge(sq_ready, j * 2 + (b + 1))
                            nc.vector.reduce_sum(ss[:, b, :], sq[:, b, :].rearrange("p (h c) -> p h c", c=BD),
                                                 AXX).then_inc(ss_ready, 1)
                            dve.wait_ge(k_transposed, j * 2 + (b + 1))
                            link(rope_steps(nc.vector, link, ka[:], raw[:, b, BQK:], tmp[:],
                                            tab[:, b, 0:AD], tab[:, b, AD:2 * AD], AKV, 1))
                            for v in range(2):
                                nc.vector.tensor_copy(
                                    kr[:, b, 0:KRA].rearrange("p (h v c) -> p h v c", v=2, c=P)[:, :, v, v * AD:(v + 1) * AD],
                                    ka[:].rearrange("p (h c) -> p h c", c=AD))
                            dve.wait_ge(rt_ready, j * 2 + (b + 1))
                            link(nc.vector.reciprocal(rB[:, bass.ds(j * 2 + b, 1), :], rt[:, b, :].unsqueeze(1)))
                            keys = raw[:, b, BH * BD:BQK].rearrange("p (h c) -> p h c", c=BD)
                            kn3 = kn[:].rearrange("p (h c) -> p h c", c=BD)
                            for h in range(BKV):
                                last = nc.vector.scalar_tensor_tensor(
                                    kn3[:, h, :], keys[:, h, :], rB[:, bass.ds(j * 2 + b, 1), BH + h], kg[:],
                                    ALU.mult, ALU.mult)
                            link(last)
                            rope_steps(nc.vector, link, kr[:, b, KRA:], kn[:], tmp[:],
                                       tab[:, b, 128:256], tab[:, b, 256:384], BKV, 2).then_inc(kr_ready, 1)
                            dve.wait_ge(kr_ready, j * 2 + (b + 1))
                        link.leave(nt // 2)

                @block.tensor
                def _(pe):
                    pe.sem_inc(k_transposed, 2)
                    pe.wait_ge(const_ld, 64)
                    with pe.Fori(0, nt // 2) as j:
                        for b in range(2):
                            pe.wait_ge(kr_ready, j * 2 + (b + 1))
                            pe.wait_ge(k_copied, j * 4 + (2 * b + 2))
                            for h in range(2 * AKV):
                                nc.tensor.transpose(tpA[:, b, h * P:(h + 1) * P], kr[:, b, h * P:(h + 1) * P], ident[:])
                            for h in range(BKV):
                                last = nc.tensor.transpose(tpB[:, b, h * P:(h + 1) * P],
                                                           kr[:, b, KRA + h * BD:KRA + (h + 1) * BD], ident[:])
                            last.then_inc(k_transposed, 1)

        NH = AH + BH
        nk = nt
        FILLS = 4 + AH + BH * -(-nk // 4) + 4
        SW = 3 * P + 1
        q = m.sb("q", [P, 2, 2 * D])
        tab = m.sb("tab", [P, 2, ROPE_W])
        mask = m.sb("mask", [P, 2, 3 * P])
        qn, qtmp = m.sb("qn", [P, D]), m.sb("qtmp", [P, D])
        qr = m.sb("qr", [P, 2, 2 * D])
        qT = m.sb("qT", [P, 16, P])
        Sm = m.sb("Sm", [P, 4, SW])
        mx, nm, rsum, rinv = (m.sb(n, [P, NH]) for n in ("mx", "nm", "rsum", "rinv"))
        prob = m.sb("prob", [P, 4 * 512])
        probT = m.sb("probT", [P, 2, PROMPT])
        O = m.sb("O", [P, 2 * D])
        OT = m.sb("OT", [P, 2 * D])
        S = m.ps("S", [P, 4 * 512])
        tb = m.ps("tb", [P, 2, 512])
        Op = m.ps("Op", [P, 2, 512])
        q_ld = [m.sem(f"q_ld{b}") for b in range(2)]
        mask_ld = [m.sem(f"mask_ld{b}") for b in range(2)]
        q_ready = m.sem("q_ready")
        first_b_ready = m.sem("first_b_ready")
        t_full = m.sem("t_full")
        t_free = [m.sem("t_free_act"), m.sem("t_free_dve")]
        s_full = m.sem("s_full")
        nm_ready = m.sem("nm_ready")
        prob_ready = m.sem("prob_ready")
        o_full = m.sem("o_full")
        o_free = m.sem("o_free")
        ot_stored = m.sem("ot_stored")
        pool_chain, chain = m.sem("pool_chain"), m.sem("chain")
        AHEAD = 3

        DOTS = [8, 10, 12, 14, 18, 18, 19, 19]
        GELUS = [15, 20]
        ADDS = [16, 16, 17, 17, 21, 21, 22, 22]

        def steps():
            done = 0
            for k in range(NH + 1):
                upto = min(k + AHEAD, AH - 1) if k + 1 < AH else k + 1
                while k < NH and done <= min(upto, NH - 1):
                    yield "scores", done
                    done += 1
                if k < NH:
                    yield "spread", k
                if k >= 1:
                    yield "values", k - 1

        def slot(h, width):
            at = h % 4 * 512 if h < AH else h % 2 * 1024
            return slice(at, at + width)

        def freed(k):
            return k - 3 if k < AH else {AH: AH - 2, AH + 1: AH}.get(k, k - 1)

        LAST = {7: 0, 15: 1, 19: 2, 23: 3}
        FIRST = {0: 0, 8: 1, 16: 2, 20: 3}

        def q_moves():
            for u in range(4):
                yield u, tb[:, u % 2, :].rearrange("p (h c) -> p h c", c=P), qT[:, 4 * u:4 * u + 4, :]

        def p_moves(h):
            if h < AH:
                u = 4 + h
                yield u, tb[:, u % 2, 0:3 * P], probT[:, h % 2, 0:3 * P]
                return
            banks = -(-nk // 4)
            for c in range(banks):
                u, n = 4 + AH + (h - AH) * banks + c, min(4, nk - 4 * c) * P
                yield u, tb[:, u % 2, 0:n], probT[:, h % 2, 512 * c:512 * c + n]

        def o_moves():
            for c in range(4):
                u = FILLS - 4 + c
                yield u, tb[:, u % 2, :], OT[:, 512 * c:512 * c + 512]

        def pairs(e, body, first=False, last=False):
            n = nt // 2
            if first:
                body(0, 0)
            lo, hi = int(first), n - last
            if hi > lo:
                with e.Fori(0, hi - lo) as j:
                    body(j, lo)
            if last and n > lo:
                body(0, n - 1)

        def rope_a(e, link, n, b, tmp):
            return rope_steps(e, link, qr[:, b, 0:D], q[:, b, 0:D], tmp, tab[:, b, 0:AD], tab[:, b, AD:2 * AD], AH, 1)

        def rope_b(e, link, n, b, normed, tmp):
            three = lambda ap: ap.rearrange("p (h c) -> p h c", c=BD)
            link(e.tensor_tensor(three(normed), three(q[:, b, D:]),
                                 rB[:, bass.ds(n(0), 1), 0:BH].rearrange("p a h -> p (a h)").unsqueeze(2).to_broadcast([P, BH, BD]),
                                 ALU.mult))
            link(e.tensor_tensor(three(normed), three(normed), qg[:].unsqueeze(1).to_broadcast([P, BH, BD]), ALU.mult))
            return rope_steps(e, link, qr[:, b, D:], normed, tmp, tab[:, b, 128:256], tab[:, b, 256:384], BH, 2)

        with nc.Block() as block:
            @block.sync
            def _(sp):
                def load(b, row):
                    sp.dma_start(q[:, b, 0:D], proj[bass.ds(row, P), QA:KA]).then_inc(q_ld[b], 16)
                    sp.dma_start(q[:, b, D:], proj[bass.ds(row, P), QB:KB]).then_inc(q_ld[b], 16)
                    sp.dma_start(tab[:, b, :], rope[bass.ds(row, P), :]).then_inc(q_ld[b], 16)
                    sp.dma_start(mask[:, b, :], masks[bass.ds(row, P), :]).then_inc(mask_ld[b], 16)

                load(0, 0)
                load(1, P)
                if bg:
                    bg.load(sp, 1)

                def pair(j, p):
                    last_pair = p == nt // 2 - 1
                    for b in range(2):
                        n = At(j, 2, 2 * p + b)
                        half = At(j, FILLS, (2 * p + b) * FILLS // 2)
                        for par in range(2):
                            sp.wait_ge(t_free[par], half(FILLS // 2 + 1))
                        sp.dma_start(mixed[bass.ds(n(0) * P, P), :], OT[:]).then_inc(ot_stored, 16)
                        if not last_pair:
                            load(b, n(2) * P)

                pairs(sp, pair, last=True)
                sp.wait_ge(ot_stored, 16 * (nt + 1))

            @block.gpsimd
            def _(pool):
                link = Chain(pool, pool_chain)
                pool.sem_inc(ot_stored, 16)
                if bg:
                    pool.wait_ge(bg.ld, 96)

                def pair(j, p):
                    link.enter(j, 10 if p else 6)
                    for b in range(2):
                        n = At(j, 2, 2 * p + b)
                        pool.wait_ge(q_ld[b], j * 48 + 48 * (p + 1))
                        if p == 0 and b == 0:
                            rope_a(nc.gpsimd, link, n, b, qtmp[:]).then_inc(q_ready, 1)
                            pool.wait_ge(q_ready, 1)
                            if bg:
                                bg.gather_window(pool, 1, b, At(j, 16, SLOTS), n)
                            continue
                        if p:
                            pool.wait_ge(s_full, (n(-2)) * NH + 1)
                        link(rope_b(nc.gpsimd, link, n, b, qn[:], qtmp[:]))
                        rope_a(nc.gpsimd, link, n, b, qtmp[:]).then_inc(q_ready, 1)
                        pool.wait_ge(q_ready, n(1))
                        if bg:
                            bg.gather_window(pool, 1, b, At(j, 16, SLOTS + 16 * p + 8 * b), n)
                    link.leave(nt // 2 - 1 if p else 1)

                pairs(pool, pair, first=True)

            @block.scalar
            def _(act):
                act.sem_inc(t_free[0], 1)

                def pair(j, p):
                    for b in range(2):
                        n = At(j, 2, 2 * p + b)
                        head = At(j, 2 * NH, (2 * p + b) * NH)
                        fill = At(j, 2 * FILLS, (2 * p + b) * FILLS)

                        def move(moves):
                            for u, src, dst in moves:
                                if u % 2 == 0:
                                    act.wait_ge(t_full, fill(u + 1))
                                    nc.scalar.copy(dst, src).then_inc(t_free[0], 1)

                        move(q_moves())
                        for stage, k in steps():
                            if stage == "scores":
                                act.wait_ge(nm_ready, head(k + 1))
                                if k < AH:
                                    nc.scalar.activation(prob[:, slot(k, SW)], Sm[:, k % 4, :], ACT.Exp, bias=nm[:, k:k + 1],
                                                         accum_out=rsum[:, k:k + 1]).then_inc(prob_ready, 1)
                                else:
                                    nc.scalar.activation(prob[:, slot(k, nk * P)], S[:, slot(k, nk * P)], ACT.Exp,
                                                         bias=nm[:, k:k + 1], scale=B_SCALE,
                                                         accum_out=rsum[:, k:k + 1]).then_inc(prob_ready, 1)
                            elif stage == "spread":
                                move(p_moves(k))
                                if bg and k in GELUS:
                                    bg.gelu4(act, At(j, 16, SLOTS + 16 * p + 8 * b), 4 * GELUS.index(k))
                        act.wait_ge(ot_stored, n(1) * 16)
                        move(o_moves())

                pairs(act, pair)

            @block.vector
            def _(dve):
                link = Chain(dve, chain)
                dve.sem_inc(o_free, 2)
                dve.sem_inc(t_free[1], 1)

                def pair(j, p):
                    link.enter(j, 2 * (NH + 4) + (2 * len(ADDS) if bg else 0))
                    for b in range(2):
                        n = At(j, 2, 2 * p + b)
                        head = At(j, 2 * NH, (2 * p + b) * NH)
                        bank = At(j, 8, (2 * p + b) * 4)
                        fill = At(j, 2 * FILLS, (2 * p + b) * FILLS)

                        def move(moves):
                            for u, src, dst in moves:
                                if u % 2 == 1:
                                    dve.wait_ge(t_full, fill(u + 1))
                                    nc.vector.tensor_copy(dst, src).then_inc(t_free[1], 1)

                        move(q_moves())
                        dve.wait_ge(mask_ld[b], j * 16 + 16 * (p + 1))
                        for stage, k in steps():
                            if stage == "scores" and k < AH:
                                dve.wait_ge(s_full, head(k + 1))
                                if k >= 4:
                                    dve.wait_ge(prob_ready, head(freed(k)))
                                nc.vector.tensor_copy(Sm[:, k % 4, SW - 1:SW], sinks[:, k:k + 1])
                                link(nc.vector.tensor_tensor_reduce(
                                    out=Sm[:, k % 4, 0:SW - 1], in0=S[:, slot(k, SW - 1)], in1=mask[:, b, :], scale=A_SCALE,
                                    scalar=NEG, op0=ALU.add, op1=ALU.max, accum_out=mx[:, k:k + 1]))
                                nc.vector.tensor_scalar(nm[:, k:k + 1], mx[:, k:k + 1], sinks[:, k:k + 1], -1.0,
                                                        ALU.max, ALU.mult).then_inc(nm_ready, 1)
                            elif stage == "scores":
                                dve.wait_ge(s_full, head(k + 1))
                                link(nc.vector.reduce_max(mx[:, k:k + 1], S[:, slot(k, nk * P)], AXX))
                                nc.vector.tensor_scalar(nm[:, k:k + 1], mx[:, k:k + 1], -B_SCALE, None,
                                                        ALU.mult).then_inc(nm_ready, 1)
                            elif stage == "spread":
                                move(p_moves(k))
                            if bg and stage == "spread":
                                at = At(j, 16, SLOTS + 16 * p + 8 * b)
                                for s in range(8):
                                    if DOTS[s] == k:
                                        bg.dot_of(dve, at, s // 2 * 2, s % 2)
                                for s in range(8):
                                    if ADDS[s] == k:
                                        bg.add_of(dve, link, 1, at, s // 2 * 2, s % 2)
                            if stage == "values" and k in LAST:
                                w = LAST[k]
                                hs = slice(8 * w, 8 * w + 8) if w < 2 else slice(4 * w + 8, 4 * w + 12)
                                nh = hs.stop - hs.start
                                dve.wait_ge(o_full, bank(w + 1))
                                link(nc.vector.reciprocal(rinv[:, hs], rsum[:, hs]))
                                nc.vector.tensor_tensor(
                                    O[:, 512 * w:512 * w + 512].rearrange("p (h c) -> p h c", h=nh),
                                    Op[:, w % 2, :].rearrange("p (h c) -> p h c", h=nh),
                                    rinv[:, hs].unsqueeze(2).to_broadcast([P, nh, 512 // nh]), ALU.mult).then_inc(o_free, 1)
                        dve.wait_ge(ot_stored, n(1) * 16)
                        move(o_moves())
                    link.leave(nt // 2)

                dve.wait_ge(q_ld[0], 48)
                rope_b(nc.vector, link, At(0, 1, 0), 0, prob[:, 0:D], prob[:, D:2 * D]).then_inc(first_b_ready, 1)
                if bg:
                    bg.start(dve, link, 1)
                pairs(dve, pair)

            @block.tensor
            def _(pe):
                def pair(j, p):
                    for b in range(2):
                        n = At(j, 2, 2 * p + b)
                        head = At(j, 2 * NH, (2 * p + b) * NH)
                        bank = At(j, 8, (2 * p + b) * 4)
                        half = At(j, FILLS, (2 * p + b) * FILLS // 2)

                        def free(u):
                            pe.wait_ge(t_free[u % 2], half(u // 2 + 1))

                        def moved(u):
                            pe.wait_ge(t_free[u % 2], half(u // 2 + 2))

                        pe.wait_ge(q_ready, n(1))
                        if p == 0 and b == 0:
                            pe.wait_ge(first_b_ready, 1)
                        for u, src, dst in q_moves():
                            free(u)
                            for c in range(4):
                                at = (4 * u + c) * P
                                last = nc.tensor.transpose(tb[:, u % 2, c * P:(c + 1) * P], qr[:, b, at:at + P], ident[:])
                            last.then_inc(t_full, 1)
                        for stage, k in steps():
                            if stage == "scores":
                                if k < AH and k % 8 == 0:
                                    moved(k // 8)
                                if k >= AH and k % 4 == 0:
                                    moved(2 + (k - AH) // 4)
                                if k >= 4:
                                    pe.wait_ge(prob_ready, head(freed(k)))
                                if k < AH:
                                    last = nc.tensor.matmul(S[:, slot(k, 3 * P)], qT[:, k // 2, :],
                                                            kTA[:, k // 4 * 2 + k % 2, bass.ds(n(0) * P, 3 * P)],
                                                            start=True, stop=True)
                                else:
                                    for c in range(0, nk * P, 512):
                                        w = min(512, nk * P - c)
                                        at = slot(k, w).start + c
                                        last = nc.tensor.matmul(S[:, at:at + w], qT[:, 8 + k - AH, :],
                                                                kTB[:, (k - AH) // 4, c:c + w],
                                                                start=True, stop=True)
                                last.then_inc(s_full, 1)
                            elif stage == "spread":
                                pe.wait_ge(prob_ready, head(k + 1))
                                for c, (u, src, dst) in enumerate(p_moves(k)):
                                    free(u)
                                    for t in range(src.shape[-1] // P):
                                        at = slot(k, P).start + c * 512 + t * P
                                        last = nc.tensor.transpose(tb[:, u % 2, t * P:(t + 1) * P], prob[:, at:at + P], ident[:])
                                    last.then_inc(t_full, 1)
                            else:
                                h = k
                                for u, src, dst in p_moves(h):
                                    moved(u)
                                if h in FIRST:
                                    pe.wait_ge(o_free, bank(FIRST[h] + 1))
                                w = h // 8 if h < AH else 2 + (h - AH) // 4
                                if h < AH:
                                    dst = Op[:, w % 2, (h % 8) * AD:(h % 8) * AD + AD]
                                    for t in range(3):
                                        kv = h // 4
                                        last = nc.tensor.matmul(dst, probT[:, h % 2, t * P:(t + 1) * P],
                                                                vA[:, bass.ds(n(t), 1), kv * AD:(kv + 1) * AD].rearrange("p a c -> p (a c)"),
                                                                start=(t == 0), stop=(t == 2))
                                else:
                                    dst = Op[:, w % 2, (h % 4) * BD:(h % 4) * BD + BD]
                                    for t in range(nk):
                                        kv = (h - AH) // 4
                                        last = nc.tensor.matmul(dst, probT[:, h % 2, t * P:(t + 1) * P],
                                                                vB[:, t, kv * BD:(kv + 1) * BD],
                                                                start=(t == 0), stop=(t == nk - 1))
                                if h in LAST:
                                    last.then_inc(o_full, 1)
                        for c, (u, src, dst) in enumerate(o_moves()):
                            pe.wait_ge(o_free, bank(c + 1 + 2))
                            free(u)
                            for t in range(4):
                                last = nc.tensor.transpose(tb[:, u % 2, t * P:(t + 1) * P],
                                                           O[:, 512 * c + t * P:512 * c + (t + 1) * P], ident[:])
                            last.then_inc(t_full, 1)

                pairs(pe, pair)


def phase_merge(nc, sems, tag, nt, x, mixed, proj, b_gate, w_oa, w_ob, w_out, ident_d, x2, bg=None, x2_sample=None, out=None):
    with ExitStack() as ctx:
        m = Mem(nc, ctx, sems, tag)
        ident = m.sb("ident", [P, P])
        wa, wb, wo = (m.sb(n, [P, KD, D]) for n in ("wa", "wb", "wo"))
        bias = m.sb("bias", [P, 2 * D])
        mixT = m.sb("mixT", [P, 2, 2 * D])
        gate = m.sb("gate", [P, 2, 2 * D])
        xt = m.sb("xt", [P, 2, D])
        part = m.sb("part", [P, 2, 512])
        merged = m.sb("merged", [P, D])
        mT = m.sb("mT", [P, D])
        res = m.sb("res", [P, D])
        Y = m.ps("Y", [P, 2, D])
        tb = m.ps("tb", [P, D])
        Z = m.ps("Z", [P, D])
        w_ld = [[m.sem(f"w_ld{h}{br}") for br in range(2)] for h in range(2)]
        wo_ld, bias_ld, ident_ld = m.sem("wo_ld"), m.sem("bias_ld"), m.sem("ident_ld")
        ld = [m.sem(f"ld{b}") for b in range(2)]
        x_ld = [m.sem(f"x_ld{b}") for b in range(2)]
        biased, gated = m.sem("biased"), m.sem("gated")
        y_full = m.sem("y_full")
        y_free = m.sem("y_free")
        merged_ready = m.sem("merged_ready")
        m_transposed = m.sem("m_transposed")
        mT_ready = m.sem("mT_ready")
        z_full = m.sem("z_full")
        res_ready = m.sem("res_ready")
        res_stored = m.sem("res_stored")
        chain = m.sem("chain")

        HALF = SLOTS + 8 * nt

        def before(n):
            return At(n.i, 16, HALF + 8 * n.base - (4 if n.per == 2 and n.base else 0))

        def after(n):
            return At(n.i, 16, HALF + 8 * n.base + (4 if n.base == nt - 1 else 8))

        def order(e, first, second, link=None):
            first(At(0, 2, 0), 0)
            if nt > 2:
                with e.Fori(0, nt // 2 - 1) as j:
                    if link:
                        link.enter(j, 4 + (2 * 2 * 4 if bg else 0))
                    for b in range(2):
                        first(At(j, 2, b + 1), (b + 1) % 2)
                        second(At(j, 2, b), b)
                    if link:
                        link.leave(nt // 2 - 1)
            first(At(0, 2, nt - 1), 1)
            second(At(0, 2, nt - 2), 0)
            second(At(0, 2, nt - 1), 1)

        with nc.Block() as block:
            @block.sync
            def _(sp):
                def load(b, row):
                    sp.dma_start(mixT[:, b, :], mixed[bass.ds(row, P), :]).then_inc(ld[b], 16)
                    sp.dma_start(gate[:, b, :], proj[bass.ds(row, P), GATE:]).then_inc(ld[b], 16)

                def load_x(b, row):
                    sp.dma_start(xt[:, b, :], x[bass.ds(row, P), :]).then_inc(x_ld[b], 16)

                load(0, 0)
                for h in range(2):
                    for br, (dst, src) in enumerate(((wa, w_oa), (wb, w_ob))):
                        cols = slice(h * 512, h * 512 + 512)
                        sp.dma_start(dst[:, :, cols], src.rearrange("(k p) c -> p k c", p=P)[:, :, cols]).then_inc(w_ld[h][br], 16)
                        if (h, br) == (0, 1):
                            sp.dma_start(bias[:], b_gate.broadcast_to([P, 2 * D])).then_inc(bias_ld, 16)
                sp.dma_start(ident[:], ident_d).then_inc(ident_ld, 16)
                load(1, P)
                sp.dma_start(wo[:], w_out.rearrange("(k p) c -> p k c", p=P)).then_inc(wo_ld, 16)
                load_x(0, 0)
                load_x(1, P)

                def tile(n, b, more):
                    if more:
                        sp.wait_ge(merged_ready, n(1))
                        load(b, n(2) * P)
                    sp.wait_ge(res_ready, n(1 + 1))
                    sp.dma_start(x2[bass.ds(n(0) * P, P), :], res[:]).then_inc(res_stored, 16)
                    if more:
                        load_x(b, n(2) * P)

                if nt > 2:
                    with sp.Fori(0, nt // 2 - 1) as j:
                        for b in range(2):
                            tile(At(j, 2, b), b, True)
                if bg:
                    sp.wait_ge(y_full, 4 * nt)
                    bg.load_last(sp, 1, x2_sample, wa[:, 0:4, :])
                for b in range(2):
                    tile(At(0, 2, nt - 2 + b), b, False)
                if bg:
                    bg.store(sp, 1, out)
                sp.wait_ge(res_stored, 16 * (nt + 1))

            @block.gpsimd
            def _(pool):
                pool.sem_inc(res_stored, 16)
                if bg:
                    bg.gather_window(pool, 1, 1, At(0, 16, HALF), At(0, 2, nt), 4)
                pool.wait_ge(bias_ld, 16)

                def add_bias(n, b):
                    pool.wait_ge(ld[b], n.i * 32 + 32 * (n.base // 2 + 1))
                    nc.gpsimd.tensor_tensor(gate[:, b, :], gate[:, b, :], bias[:], ALU.add).then_inc(biased, 1)

                def rows(n, b):
                    if bg:
                        bg.gather_window(pool, 1, b, At(n.i, 16, HALF + 8 * n.base + 4), At(n.i, 2, nt + 1 + n.base),
                                         4 if n.base == nt - 1 else 8)

                order(pool, add_bias, rows)

            @block.scalar
            def _(act):
                act.sem_inc(mT_ready, 1)

                def sigmoid(n, b):
                    act.wait_ge(biased, n(1))
                    nc.scalar.activation(gate[:, b, :], gate[:, b, :], ACT.Sigmoid).then_inc(gated, 1)
                    if bg:
                        bg.gelu(act, before(n), 0)
                        if n.base == 0:
                            bg.gelu(act, before(n), 2)

                def spread(n, b):
                    act.wait_ge(m_transposed, n(1 + 1))
                    nc.scalar.copy(mT[:], tb[:]).then_inc(mT_ready, 1)
                    if bg:
                        if n.base < nt - 1:
                            bg.gelu(act, before(At(n.i, 2, n.base + 1)), 2)
                        for k in (0, 2):
                            bg.gelu(act, after(n), k)

                order(act, sigmoid, spread)
                if bg:
                    bg.square_root(act, 1)

            @block.vector
            def _(dve):
                link = Chain(dve, chain)
                dve.sem_inc(y_free, 1)
                dve.sem_inc(res_ready, 1)

                def gates(n, b):
                    dve.wait_ge(gated, n(1))
                    for h in range(2):
                        cols = slice(h * 512, h * 512 + 512)
                        if bg:
                            bg.dots(dve, before(n), 2 * h)
                        for br in range(2):
                            dve.wait_ge(y_full, n.i * 8 + (n.base * 4 + 2 * h + br + 1))
                            last = nc.vector.tensor_tensor(part[:, br, :], Y[:, br, cols],
                                                           gate[:, b, br * D + h * 512:br * D + h * 512 + 512], ALU.mult)
                        if h == 1:
                            last.then_inc(y_free, 1)
                            dve.wait_ge(y_free, n(1 + 1))
                        else:
                            link(last)
                            dve.wait_ge(m_transposed, n(1))
                        last = nc.vector.tensor_tensor(merged[:, cols], part[:, 0, :], part[:, 1, :], ALU.add)
                        if h == 0:
                            link(last)
                        else:
                            last.then_inc(merged_ready, 1)
                        if bg:
                            bg.add(dve, link, 1, before(n), 2 * h)
                    dve.wait_ge(merged_ready, n(1))

                def residual(n, b):
                    if bg:
                        bg.dots(dve, after(n), 0)
                    dve.wait_ge(res_stored, n(1) * 16)
                    dve.wait_ge(x_ld[b], n.i * 16 + 16 * (n.base // 2 + 1))
                    dve.wait_ge(z_full, n(1))
                    nc.vector.tensor_tensor(res[:], Z[:], xt[:, b, :], ALU.add).then_inc(res_ready, 1)
                    if bg:
                        bg.dots(dve, after(n), 2)
                        for k in (0, 2):
                            bg.add(dve, link, 1, after(n), k)

                order(dve, gates, residual, link)
                if bg:
                    bg.finish(dve, link, 1)

            @block.tensor
            def _(pe):
                pe.sem_inc(m_transposed, 1)

                def branches(n, b):
                    pe.wait_ge(ld[b], n.i * 32 + 32 * (n.base // 2 + 1))
                    pe.wait_ge(y_free, n(1))
                    for h in range(2):
                        for br, w in enumerate((wa, wb)):
                            pe.wait_ge(w_ld[h][br], 16)
                            for k in range(KD):
                                last = nc.tensor.matmul(Y[:, br, h * 512:h * 512 + 512],
                                                        mixT[:, b, (br * KD + k) * P:(br * KD + k + 1) * P],
                                                        w[:, k, h * 512:h * 512 + 512], start=(k == 0), stop=(k == KD - 1))
                            last.then_inc(y_full, 1)

                def project(n, b):
                    pe.wait_ge(wo_ld, 16)
                    pe.wait_ge(ident_ld, 16)
                    pe.wait_ge(merged_ready, n(1))
                    pe.wait_ge(mT_ready, n(1))
                    for k in range(KD):
                        last = nc.tensor.transpose(tb[:, k * P:(k + 1) * P], merged[:, k * P:(k + 1) * P], ident[:])
                    last.then_inc(m_transposed, 1)
                    pe.wait_ge(mT_ready, n(2))
                    pe.wait_ge(res_ready, n(1))
                    for h in range(2):
                        for k in range(KD):
                            last = nc.tensor.matmul(Z[:, h * 512:h * 512 + 512], mT[:, k * P:(k + 1) * P],
                                                    wo[:, k, h * 512:h * 512 + 512], start=(k == 0), stop=(k == KD - 1))
                    last.then_inc(z_full, 1)

                order(pe, branches, project)


def phase_experts(nc, sems, tag, nt, x2, g_ffn, w_query, sub_keys, experts, g_final, ident_d, iota_d, out, kept=None):
    with ExitStack() as ctx:
        m = Mem(nc, ctx, sems, tag)
        RING = 8
        PAIR = 2
        STEPS = SLOTS // PAIR
        BACK = RING // PAIR
        ident = m.sb("ident", [P, P])
        iota = m.sb("iota", [P, TOPK])
        gffn, gfin = m.sb("gffn", [P, D]), m.sb("gfin", [P, D])
        wq = m.sb("wq", [P, KD, HEADS * 2 * P])
        keys = m.sb("keys", [P, 2 * HEADS, KEYS])
        eps = m.sb("eps", [P, 1])
        ring = m.sb("ring", [P, 1 if kept else RING, 2 * D])
        xn, xr = m.sb("xn", [P, D]), m.sb("xr", [P, D])
        h_next, h_now = m.sb("h_next", [P, nt if kept else 1, D]), m.sb("h_now", [P, D])
        hT = m.sb("hT", [P, D])
        junk = m.sb("junk", [P, 2, D], mybir.dt.bfloat16)
        sqj = m.sb("sqj", [P, D])
        stat = m.sb("stat", [P, 6])
        qT = m.sb("qT", [P, 2, 2 * P])
        top = m.sb("top", [P, HEADS, 2, TOPK])
        topi = m.sb("topi", [P, HEADS, 2, TOPK], U32)
        topf = m.sb("topf", [P, HEADS, 2, TOPK])
        rest = m.sb("rest", [P, 2, 2, KEYS])
        cand, crest = m.sb("cand", [P, 2, TOPK * TOPK]), m.sb("crest", [P, 2, TOPK * TOPK])
        best = m.sb("best", [P, HEADS, TOPK])
        pos = m.sb("pos", [P, 2, TOPK], U32)
        posd = m.sb("posd", [P, 2, 2, TOPK], U32)
        posf = m.sb("posf", [P, 2, 2, TOPK])
        hit = m.sb("hit", [P, 2, 2, TOPK, TOPK])
        sel = m.sb("sel", [P, 2, 2, TOPK])
        idx_all = m.sb("idx_all", [P, nt, SLOTS], I32)
        idx = m.sb("idx", [P, 2, SLOTS], I32)
        soft, ssum = m.sb("soft", [P, HEADS, TOPK]), m.sb("ssum", [P, HEADS])
        g_next, g_now = m.sb("g_next", [P, SLOTS]), m.sb("g_now", [P, SLOTS])
        dot, ge, wgt = (m.sb(n, [P, SLOTS]) for n in ("dot", "ge", "wgt"))
        diag = m.sb("diag", [P, 2, PAIR, P])
        y, yo = m.sb("y", [P, D]), m.sb("yo", [P, D])
        tb = m.ps("tb", [P, D])
        qp, sc = m.ps("qp", [P, 2, 512]), m.ps("sc", [P, 2, 512])
        acc = m.ps("acc", [P, D])
        const_ld, eps_set = m.sem("const_ld"), m.sem("eps_set")
        gffn_ld, ident_ld = m.sem("gffn_ld"), m.sem("ident_ld")
        w_ld = [m.sem(f"w_ld{i}") for i in range(4)]
        xn_ld, xr_ld = m.sem("xn_ld"), m.sem("xr_ld")
        root, h_ready, h_transposed, hT_ready = (m.sem(n) for n in ("root", "h_ready", "h_transposed", "hT_ready"))
        q_full, s_full = m.sem("q_full"), m.sem("s_full")
        q_ready = m.sem("q_ready")
        s_free = m.sem("s_free")
        best_ready, exp_ready, chosen = m.sem("best_ready"), m.sem("exp_ready"), m.sem("chosen")
        row_ld = [m.sem(f"row_ld{r}") for r in range(RING)]
        dotted, gelued, weighted, diag_ready = (m.sem(n) for n in ("dotted", "gelued", "weighted", "diag_ready"))
        used = m.sem("used")
        y_ready = m.sem("y_ready")
        root2, yo_ready = m.sem("root2"), m.sem("yo_ready")
        out_stored = m.sem("out_stored")
        idx_ready, heads_chosen = m.sem("idx_ready"), m.sem("heads_chosen")
        pool_passed, dve_passed = m.sem("pool_passed"), m.sem("dve_passed")
        act_chain, chain = m.sem("act_chain"), m.sem("chain")
        kept_ready, g_stored, kept_stored = m.sem("kept_ready"), m.sem("g_stored"), m.sem("kept_stored")
        HALF = HEADS // 2
        extra = 0 if kept else 1
        Q0, QS = 6, 6

        def head_at(step, lag):
            h, off = divmod(step - Q0 - lag, QS)
            return h if off == 0 and 0 <= h < HEADS else None

        def tiles(e, prologue, tile, link=None, per=0):
            for n in range(nt if kept else 1):
                prologue(At(0, 1, n))
            if kept:
                return
            tile(At(0, 1, 0), True, False)
            with e.Fori(0, nt - 2) as i:
                if link:
                    link.enter(i, per)
                tile(At(i, 1, 1), True, True)
                if link:
                    link.leave(nt - 2)
            tile(At(0, 1, nt - 1), False, True)

        def which(n):
            return n.base if kept else 0

        def source(n):
            return xr if kept and n.base else xn

        def mul(n, k, c):
            return n.i * (n.per * k) + (n.base * k + c)

        with nc.Block() as block:
            @block.sync
            def _(sp):
                sp.dma_start(xn[:], x2[0:P, :]).then_inc(xn_ld, 16)
                if kept:
                    sp.dma_start(xr[:], x2[P:2 * P, :]).then_inc(xr_ld, 16)
                sp.dma_start(gffn[:], g_ffn.broadcast_to([P, D])).then_inc(gffn_ld, 16)
                sp.dma_start(ident[:], ident_d).then_inc(ident_ld, 16)
                wv = w_query.rearrange("(k p) c -> p k c", p=P)
                for i in range(4):
                    sp.dma_start(wq[:, :, i * 512:(i + 1) * 512], wv[:, :, i * 512:(i + 1) * 512]).then_inc(w_ld[i], 16)
                    if i == 0:
                        for dst, src in ((keys[:], sub_keys), (iota[:], iota_d.broadcast_to([P, TOPK])),
                                         (gfin[:], g_final.broadcast_to([P, D]))):
                            sp.dma_start(dst, src).then_inc(const_ld, 16)

                def keep():
                    for n in range(nt):
                        sp.wait_ge(h_ready, n + 1)
                        sp.dma_start(kept[0][n * P:(n + 1) * P, :], h_next[:, n, :]).then_inc(kept_stored, 16)
                    for n in range(nt):
                        sp.wait_ge(kept_ready, n + 1)
                        sp.dma_start(kept[1][n * P:(n + 1) * P, :], idx_all[:, n, :]).then_inc(kept_stored, 16)
                        sp.dma_start(kept[2][n * P:(n + 1) * P, :], g_next[:]).then_inc(g_stored, 16)
                    sp.wait_ge(kept_stored, 32 * nt)
                    sp.wait_ge(g_stored, 16 * nt)

                def tile(n, more, before):
                    if more:
                        sp.wait_ge(h_ready, n(1))
                        sp.dma_start(xn[:], x2[bass.ds(n(1) * P, P), :]).then_inc(xn_ld, 16)
                    sp.wait_ge(y_ready, n(1))
                    sp.dma_start(xr[:], x2[bass.ds(n(0) * P, P), :]).then_inc(xr_ld, 16)
                    if before:
                        store(n(-1), n(0))

                def store(t, count):
                    sp.wait_ge(yo_ready, count)
                    sp.dma_start(out[bass.ds(t * P, P), :], yo[:]).then_inc(out_stored, 16)

                if kept:
                    keep()
                else:
                    tiles(sp, lambda n: None, tile)
                    store(nt - 1, nt)
                    sp.wait_ge(out_stored, 16 * (nt + 1))

            @block.gpsimd
            def _(pool):
                if kept:
                    return
                pool.sem_inc(out_stored, 16)

                def rows(n, column):
                    for s in range(SLOTS):
                        if n.base == 0 and s % TOPK == 0:
                            pool.wait_ge(heads_chosen, s // TOPK + 1)
                        if s % PAIR == 0:
                            pool.wait_ge(used, mul(n, STEPS, s // PAIR + 1))
                            pool.sem_inc(pool_passed, 1)
                        nc.gpsimd.indirect_dma_start(
                            out=ring[:, s % RING, :], out_offset=None, in_=experts,
                            in_offset=bass.IndirectOffsetOnAxis(ap=column(s), axis=0)).then_inc(row_ld[s % RING], 16)

                def tile(n, b):
                    pool.wait_ge(chosen, n(1))
                    nc.gpsimd.tensor_copy(idx[:, b, :], idx_all[:, bass.ds(n(0), 1), :].rearrange("p a s -> p (a s)")).then_inc(idx_ready, 1)
                    pool.wait_ge(idx_ready, n(0))
                    rows(n, lambda s: idx[:, b, s:s + 1])

                rows(At(0, 2, 0), lambda s: idx_all[:, 0, s:s + 1])
                with pool.Fori(0, nt // 2 - 1) as j:
                    for b in (1, 2):
                        tile(At(j, 2, b), b % 2)
                tile(At(0, 2, nt - 1), 1)

            @block.scalar
            def _(act):
                link = Chain(act, act_chain)

                def norm(n):
                    if kept and n.base:
                        act.wait_ge(xr_ld, 16)
                        act.wait_ge(h_ready, 1)
                    else:
                        act.wait_ge(xn_ld, mul(n, 16, 16))
                    link(nc.scalar.activation(sqj[:], source(n)[:], ACT.Square, accum_out=stat[:, 0:1]))
                    nc.scalar.activation(stat[:, 1:2], stat[:, 0:1], ACT.Sqrt, bias=eps[:], scale=1.0 / D).then_inc(root, 1)

                def spread_h(n):
                    act.wait_ge(h_transposed, n(1))
                    nc.scalar.copy(hT[:], tb[:]).then_inc(hT_ready, 1)

                def spread_q(n, h):
                    act.wait_ge(q_full, mul(n, HEADS, h + 1))
                    nc.scalar.copy(qT[:, h % 2, :], qp[:, h % 2, 0:2 * P]).then_inc(q_ready, 1)

                def expo_some(hs, count):
                    act.wait_ge(best_ready, count)
                    nc.scalar.activation(soft[:, hs, :], soft[:, hs, :], ACT.Exp).then_inc(exp_ready, 1)

                def expo(n):
                    expo_some(slice(0, HEADS), n(1 + extra))

                def first(n):
                    if n.base == 0:
                        act.sem_inc(q_ready, 2)
                        act.wait_ge(eps_set, 1)
                        for t in range(nt if kept else 1):
                            norm(At(0, 1, t))
                    EARLY = 2
                    if n.base == 0:
                        spread_h(n)
                    for h in range(EARLY if n.base else 0, HEADS):
                        if not kept and h == HEADS - EARLY:
                            expo_some(slice(0, HALF), 1)
                        spread_q(n, h)
                    if not kept:
                        return
                    if kept and n.base + 1 < nt:
                        spread_h(At(0, 1, n.base + 1))
                        for h in range(EARLY):
                            spread_q(At(0, 1, n.base + 1), h)
                    expo(n)

                def tile(n, more, before):
                    nxt = At(n.i, 1, n.base + 1)
                    for g in range(STEPS + 1):
                        if g == 4 and not before:
                            expo_some(slice(HALF, HEADS), 2)
                        if g < STEPS:
                            act.wait_ge(dotted, mul(n, SLOTS, PAIR * (g + 1)))
                            c = slice(PAIR * g, PAIR * (g + 1))
                            nc.scalar.activation(ge[:, c], dot[:, c], ACT.Gelu).then_inc(gelued, 1)
                        if g >= 1:
                            act.wait_ge(weighted, mul(n, STEPS, g))
                            act.wait_ge(used, mul(n, STEPS, g - 2 + BACK))
                            for c in range(PAIR):
                                s = PAIR * (g - 1) + c
                                last = nc.scalar.activation(diag[:, (g - 1) % 2, c, :], ident[:], ACT.Copy, scale=wgt[:, s:s + 1])
                            last.then_inc(diag_ready, 1)
                        if more:
                            if g == 0:
                                norm(nxt)
                            if g == 5:
                                spread_h(nxt)
                            if (h := head_at(g, 2)) is not None:
                                spread_q(nxt, h)
                            if g == 59:
                                expo(nxt)
                        if before and g == 2:
                            norm_y(n(1))

                def norm_y(count):
                    act.wait_ge(y_ready, count)
                    link(nc.scalar.activation(sqj[:], y[:], ACT.Square, accum_out=stat[:, 3:4]))
                    nc.scalar.activation(stat[:, 4:5], stat[:, 3:4], ACT.Sqrt, bias=eps[:], scale=1.0 / D).then_inc(root2, 1)

                tiles(act, first, tile, link, 2)
                if not kept:
                    norm_y(nt + 1)

            @block.vector
            def _(dve):
                link = Chain(dve, chain)

                def norm(n):
                    dve.wait_ge(root, n(1))
                    link(nc.vector.reciprocal(stat[:, 2:3], stat[:, 1:2]))
                    nc.vector.scalar_tensor_tensor(h_next[:, which(n), :], source(n)[:], stat[:, 2:3], gffn[:], ALU.mult, ALU.mult).then_inc(h_ready, 1)

                def top16(lists):
                    def top8(eight, scores):
                        for vals, index, *rows in lists:
                            last = nc.vector.max(vals[:, eight], rows[scores])
                        link(last)
                        dve.sem_inc(dve_passed, 1)
                        for vals, index, *rows in lists:
                            last = nc.vector.max_index(index[:, eight], vals[:, eight], rows[scores])
                        return last

                    top8(slice(0, 8), 0)
                    for vals, index, scores, left in lists:
                        last = nc.vector.match_replace(left, vals[:, 0:8], scores, -3e38)
                    link(last)
                    dve.sem_inc(dve_passed, 1)
                    link(top8(slice(8, 16), 1))

                def choose(n, heads, part):
                    if part == 0:
                        dve.wait_ge(s_full, mul(n, HEADS, heads[-1] + 1))
                        dve.sem_inc(dve_passed, 1)
                        top16([(top[:, h, p, :], topi[:, h, p, :], sc[:, h % 2, p * P:(p + 1) * P], rest[:, h % 2, p, :])
                               for h in heads for p in range(2)])
                    elif part == 1:
                        dve.sem_inc(s_free, len(heads))
                        for h in heads:
                            nc.vector.tensor_copy(topf[:, h, :, :], topi[:, h, :, :])
                            last = nc.vector.tensor_tensor(cand[:, h % 2, :].rearrange("p (a b) -> p a b", a=TOPK),
                                                           top[:, h, 0, :].unsqueeze(2).to_broadcast([P, TOPK, TOPK]),
                                                           top[:, h, 1, :].unsqueeze(1).to_broadcast([P, TOPK, TOPK]), ALU.add)
                        link(last)
                        dve.sem_inc(dve_passed, 1)
                        top16([(best[:, h, :], pos[:, h % 2, :], cand[:, h % 2, :], crest[:, h % 2, :]) for h in heads])
                    else:
                        for h in heads:
                            nc.vector.tensor_scalar(posd[:, h % 2, 0, :], pos[:, h % 2, :], 4, None, ALU.logical_shift_right)
                            last = nc.vector.tensor_scalar(posd[:, h % 2, 1, :], pos[:, h % 2, :], TOPK - 1, None, ALU.bitwise_and)
                        link(last)
                        for h in heads:
                            last = nc.vector.tensor_copy(posf[:, h % 2, :, :], posd[:, h % 2, :, :])
                        link(last)
                        for h in heads:
                            for p in range(2):
                                last = nc.vector.tensor_tensor(hit[:, h % 2, p, :, :],
                                                               posf[:, h % 2, p, :].unsqueeze(2).to_broadcast([P, TOPK, TOPK]),
                                                               iota[:].unsqueeze(1).to_broadcast([P, TOPK, TOPK]), ALU.is_equal)
                        link(last)
                        for h in heads:
                            for p in range(2):
                                last = nc.vector.tensor_tensor(hit[:, h % 2, p, :, :], hit[:, h % 2, p, :, :],
                                                               topf[:, h, p, :].unsqueeze(1).to_broadcast([P, TOPK, TOPK]), ALU.mult)
                        link(last)
                        for h in heads:
                            last = nc.vector.reduce_sum(sel[:, h % 2, :, :], hit[:, h % 2, :, :, :], AXX)
                        link(last)
                        for h in heads:
                            last = nc.vector.scalar_tensor_tensor(
                                idx_all[:, bass.ds(n(0), 1), h * TOPK:(h + 1) * TOPK].rearrange("p a s -> p (a s)"),
                                sel[:, h % 2, 0, :], float(KEYS), sel[:, h % 2, 1, :], ALU.mult, ALU.add)
                        link(last)

                def choose_all(n, heads):
                    for part in range(3):
                        choose(n, heads, part)
                    dve.sem_inc(heads_chosen, len(heads))

                def soften_some(hs):
                    nc.vector.tensor_tensor(soft[:, hs, :], best[:, hs, :],
                                            best[:, hs, 0:1].to_broadcast([P, hs.stop - hs.start, TOPK]),
                                            ALU.subtract).then_inc(best_ready, 1)

                def gates_some(hs, g, count):
                    dve.wait_ge(exp_ready, count)
                    link(nc.vector.reduce_sum(ssum[:, hs], soft[:, hs, :], AXX))
                    link(nc.vector.reciprocal(ssum[:, hs], ssum[:, hs]))
                    link(nc.vector.tensor_tensor(g[:].rearrange("p (h c) -> p h c", c=TOPK)[:, hs, :], soft[:, hs, :],
                                                 ssum[:, hs].unsqueeze(2).to_broadcast([P, hs.stop - hs.start, TOPK]), ALU.mult))

                def soften(n):
                    dve.sem_inc(chosen, 1)
                    soften_some(slice(0, HEADS))

                def gates(n):
                    gates_some(slice(0, HEADS), g_next, n(1 + extra))

                def first(n):
                    if n.base == 0:
                        dve.sem_inc(used, BACK)
                        dve.sem_inc(s_free, 2)
                        dve.sem_inc(y_ready, 1)
                        nc.vector.memset(eps[:], EPS).then_inc(eps_set, 1)
                        dve.wait_ge(gffn_ld, 16)
                        for t in range(nt if kept else 1):
                            norm(At(0, 1, t))
                        dve.wait_ge(const_ld, 3 * 16)
                    for heads in ((0,), (1,), (2, 3), (4, 5), (6, 7))[:None if kept else 3]:
                        choose_all(n, heads)
                    if not kept:
                        soften_some(slice(0, HALF))
                        gates_some(slice(0, HALF), g_now, 1)
                        return
                    soften(n)
                    if kept and n.base:
                        dve.wait_ge(g_stored, 16 * n.base)
                        dve.sem_inc(dve_passed, 1)
                    gates(n)
                    if kept:
                        dve.sem_inc(kept_ready, 1)

                def tile(n, more, before):
                    nxt = At(n.i, 1, n.base + 1)
                    last = nc.vector.tensor_copy(h_now[:], h_next[:, 0, :])
                    if before:
                        last = nc.vector.tensor_copy(g_now[:], g_next[:])
                    link(last)
                    for g in range(STEPS + 1):
                        if g < STEPS:
                            for s in range(PAIR * g, PAIR * (g + 1)):
                                dve.wait_ge(row_ld[s % RING], mul(n, 16 * SLOTS // RING, 16 * (s // RING + 1)))
                                if s >= 2:
                                    dve.wait_ge(dotted, mul(n, SLOTS, s - 1))
                                nc.vector.tensor_tensor_reduce(
                                    out=junk[:, s % 2, :], in0=ring[:, s % RING, 0:D], in1=h_now[:], scale=1.0, scalar=0.0,
                                    op0=ALU.mult, op1=ALU.add, accum_out=dot[:, s:s + 1]).then_inc(dotted, 1)
                        if g >= 1:
                            dve.wait_ge(gelued, mul(n, STEPS, g))
                            c = slice(PAIR * (g - 1), PAIR * g)
                            nc.vector.tensor_tensor(wgt[:, c], ge[:, c], g_now[:, c], ALU.mult).then_inc(weighted, 1)
                        if not before:
                            if g in (0, 2):
                                choose_all(n, (HALF + g, HALF + g + 1))
                            if g == 2:
                                dve.sem_inc(chosen, 1)
                                soften_some(slice(HALF, HEADS))
                            if g == 5:
                                gates_some(slice(HALF, HEADS), g_now, 2)
                        if more:
                            if g == 1:
                                norm(nxt)
                            for part, lag in enumerate((6, 8, 9)):
                                if (h := head_at(g, lag)) is not None:
                                    choose(nxt, (h,), part)
                            if g == 58:
                                soften(nxt)
                            if g == 61:
                                gates(nxt)
                        if before and g == 4:
                            norm_y(n(0), mul(n, 16, 0))
                    dve.wait_ge(xr_ld, mul(n, 16, 16))
                    dve.wait_ge(used, mul(n, STEPS, STEPS + BACK))
                    nc.vector.tensor_tensor(y[:], acc[:], xr[:], ALU.add).then_inc(y_ready, 1)

                def norm_y(count, stored):
                    dve.wait_ge(root2, count)
                    link(nc.vector.reciprocal(stat[:, 5:6], stat[:, 4:5]))
                    dve.wait_ge(out_stored, stored)
                    nc.vector.scalar_tensor_tensor(yo[:], y[:], stat[:, 5:6], gfin[:], ALU.mult, ALU.mult).then_inc(yo_ready, 1)
                    dve.wait_ge(yo_ready, count)

                tiles(dve, first, tile, link, 126)
                if not kept:
                    norm_y(nt, 16 * nt)

            @block.tensor
            def _(pe):
                def transpose_h(n):
                    pe.wait_ge(h_ready, n(1))
                    for k in range(KD):
                        last = nc.tensor.transpose(tb[:, k * P:(k + 1) * P], h_next[:, which(n), k * P:(k + 1) * P], ident[:])
                    last.then_inc(h_transposed, 1)

                def query(n, h, p):
                    if p == 0:
                        if h == 0:
                            pe.wait_ge(hT_ready, n(1))
                        pe.wait_ge(q_ready, mul(n, HEADS, h + 1))
                    for k in range(KD):
                        last = nc.tensor.matmul(qp[:, h % 2, p * P:(p + 1) * P], wq[:, k, (2 * h + p) * P:(2 * h + p + 1) * P],
                                                hT[:, k * P:(k + 1) * P], start=(k == 0), stop=(k == KD - 1))
                    if p == 1:
                        last.then_inc(q_full, 1)

                def scores(n, h):
                    pe.wait_ge(q_ready, mul(n, HEADS, h + 1 + 2))
                    pe.wait_ge(s_free, mul(n, HEADS, h + 1))
                    for p in range(2):
                        last = nc.tensor.matmul(sc[:, h % 2, p * P:(p + 1) * P], qT[:, h % 2, p * P:(p + 1) * P],
                                                keys[:, 2 * h + p, :], start=True, stop=True)
                    last.then_inc(s_full, 1)

                def first(n):
                    pe.wait_ge(ident_ld, 16)
                    transpose_h(n)
                    for h in range(HEADS):
                        if h % 2 == 0:
                            pe.wait_ge(w_ld[h // 2], 16)
                        query(n, h, 0)
                        query(n, h, 1)
                        if h == 0:
                            pe.wait_ge(const_ld, 3 * 16)
                        if h != 1:
                            scores(n, max(h - 1, 0))
                    scores(n, HEADS - 1)

                def tile(n, more, before):
                    nxt = At(n.i, 1, n.base + 1)
                    pe.wait_ge(y_ready, n(1))
                    for g in range(STEPS + 1):
                        if g >= 1:
                            pe.wait_ge(diag_ready, mul(n, STEPS, g))
                            for c in range(PAIR):
                                s = PAIR * (g - 1) + c
                                for half in range(2):
                                    last = nc.tensor.matmul(acc[:, half * 512:half * 512 + 512], diag[:, (g - 1) % 2, c, :],
                                                            ring[:, s % RING, D + half * 512:D + half * 512 + 512],
                                                            start=(s == 0), stop=(s == SLOTS - 1))
                            last.then_inc(used, 1)
                        if more:
                            if g == 4:
                                transpose_h(nxt)
                            for p in range(2):
                                if (h := head_at(g, p)) is not None:
                                    query(nxt, h, p)
                            if (h := head_at(g, 4)) is not None:
                                scores(nxt, h)

                tiles(pe, first, tile)


def build(nc, x, g_mix, w_all, b_gate, sink, q_norm_g, k_norm_g, w_oa, w_ob, w_out, g_ffn, w_query,
          sub_keys, experts, g_final, rope, masks, ident, iota, out):
    def scratch(name, shape):
        return nc.dram_tensor(name, shape, F32, kind="Internal").ap()

    proj, mixed, x2 = scratch("proj_dram", (TOK, COLS)), scratch("mixed_dram", (TOK, 2 * D)), scratch("x2_dram", (TOK, D))
    kept = (scratch("kept_h_dram", (SAMPLE, D)), nc.dram_tensor("kept_idx_dram", (SAMPLE, SLOTS), I32, kind="Internal").ap(),
            scratch("kept_g_dram", (SAMPLE, SLOTS)))

    def of(ap, prompt):
        return ap[SAMPLE:, :] if prompt else ap[0:SAMPLE, :]

    for prompt in (False, True):
        tag, nt = ("prompt", PT_) if prompt else ("sample", ST)
        x_, proj_, mixed_, x2_, out_, rope_, masks_ = [of(ap, prompt) for ap in (x, proj, mixed, x2, out, rope, masks)]
        sems = []
        with ExitStack() as back:
            bg = Background(nc, Mem(nc, back, sems, "bg"), kept, experts, g_final) if prompt else None
            phase_project(nc, sems, tag + "_proj", nt, x_, g_mix, w_all, ident, proj_, bg, of(x2, False), of(out, False))
            phase_attend(nc, sems, tag + "_att", nt, proj_, rope_, masks_, sink, q_norm_g, k_norm_g, ident, mixed_, bg)
            phase_merge(nc, sems, tag + "_mrg", nt, x_, mixed_, proj_, b_gate, w_oa, w_ob, w_out, ident, x2_, bg,
                        of(x2, False), of(out, False))
        phase_experts(nc, sems, tag + "_exp", nt, x2_, g_ffn, w_query, sub_keys, experts, g_final, ident, iota, out_,
                      None if prompt else kept)
        if not prompt:
            release(nc, sems)


def kernel(x_prompt, x_sample, g_mix, w_in, w_gate, b_gate, sink, q_norm_g, k_norm_g, w_oa, w_ob, w_out,
           g_ffn, w_query, sub_keys, expert_u, expert_v, g_final):
    import numpy as np
    import concourse.bacc as bacc
    from concourse.bass_utils import run_bass_kernel_spmd

    def rope_tables(pos, dim):
        inv = (np.float64(10000.0) ** (-np.arange(0, dim, 2) / dim)).astype(np.float32)
        ang = pos.astype(np.float32)[:, None] * inv[None, :]
        return np.concatenate([np.cos(ang)] * 2, -1), np.concatenate([-np.sin(ang), np.sin(ang)], -1)

    pos = np.concatenate([np.arange(SAMPLE), np.arange(PROMPT)])
    cos_a, sin_a = rope_tables(pos, AD)
    cos_r, sin_r = rope_tables(pos // 64, BD // 2)
    cos_c, sin_c = rope_tables(pos % 64, BD // 2)
    rope = np.concatenate([cos_a, sin_a, cos_r, cos_c, sin_r, sin_c], -1).astype(np.float32)
    masks = np.zeros((NT, P, 3 * P), np.float32)
    q, k = np.arange(P)[:, None], np.arange(3 * P)[None, :] - P
    for t in range(NT):
        first, last = t in (0, ST), t in (ST - 1, NT - 1)
        ok = (np.abs(q - k) <= P) & ((k >= 0) | (not first)) & ((k < P) | (not last))
        masks[t] = np.where(ok, 0.0, NEG / A_SCALE)
    masks = masks.reshape(TOK, 3 * P)
    arrays = {
        "x": np.concatenate([x_sample[0], x_prompt[0]], 0),
        "g_mix": g_mix, "w_all": np.concatenate([w_in[0], w_gate[0]], 1), "b_gate": b_gate, "sink": sink,
        "q_norm_g": q_norm_g, "k_norm_g": k_norm_g, "w_oa": w_oa[0], "w_ob": w_ob[0], "w_out": w_out[0],
        "g_ffn": g_ffn, "w_query": w_query[0],
        "sub_keys": np.asarray(sub_keys)[0].reshape(2 * HEADS, KEYS, P).transpose(2, 0, 1),
        "experts": np.concatenate([expert_u[0], expert_v[0]], 1),
        "g_final": np.asarray(g_final)[None], "rope": rope, "masks": masks, "ident": np.eye(P, dtype=np.float32),
        "iota": np.arange(TOPK, dtype=np.float32)[None],
    }
    nc = bacc.Bacc("TRN2", target_bir_lowering=False, num_devices=1)
    ins, args = {}, []
    for name, a in arrays.items():
        a = np.ascontiguousarray(a)
        ins[f"in_{name}_dram"] = a
        args.append(nc.dram_tensor(f"in_{name}_dram", a.shape, F32, kind="ExternalInput").ap())
    args.append(nc.dram_tensor("out_0_dram", (TOK, D), F32, kind="ExternalOutput").ap())
    build(nc, *args)
    got = run_bass_kernel_spmd(nc, [ins], core_ids=[0]).results[0]["out_0_dram"]
    return got[SAMPLE:].reshape(1, PROMPT, D), got[:SAMPLE].reshape(1, SAMPLE, D)
```
